# Optimizing a Trainium2 kernel written in Bass

```python
import jax, jax.numpy as jnp
from jax import lax
import numpy as np
import jax
import jax.numpy as jnp

D_MODEL = 1024
BATCH = 1
SEQ = 256
DEPTH = 2

GRID_W = 64
CTX_LEN = 256
HEAD_DIM = 64
ATTN_WIDTH = D_MODEL // 2
N_Q_HEADS = ATTN_WIDTH // HEAD_DIM
N_KV_HEADS = N_Q_HEADS // 4
GQA_GROUP = N_Q_HEADS // N_KV_HEADS
KV_WIDTH = N_KV_HEADS * HEAD_DIM
POOL_WINDOWS = (2, 4, 8, 16)
N_POOL_GROUPS = len(POOL_WINDOWS)
POOL_WIDTH = D_MODEL // 4
POOL_GROUP = POOL_WIDTH // N_POOL_GROUPS
N_FOURIER_GROUPS = 4
FOURIER_WIDTH = D_MODEL // 4
FOURIER_GROUP = FOURIER_WIDTH // N_FOURIER_GROUPS
MIX_WIDTH = ATTN_WIDTH + POOL_WIDTH + FOURIER_WIDTH
Q_END = ATTN_WIDTH
K_END = Q_END + KV_WIDTH
KV_END = K_END + KV_WIDTH
POOL_END = KV_END + POOL_WIDTH
IN_WIDTH = POOL_END + FOURIER_WIDTH
D_FF = -(-8 * D_MODEL // (3 * 256)) * 256
Q_BLOCK = 128
ROPE_THETA = 10000.0
EPS = 1e-6


def rms_norm(x, g):
    xf = x.astype(jnp.float32)
    y = xf * lax.rsqrt(jnp.mean(xf * xf, axis=-1, keepdims=True) + EPS)
    return (y * g.astype(jnp.float32)).astype(x.dtype)

def axial_rope_tables(length):
    rows = length // GRID_W
    row_ids = jnp.repeat(jnp.arange(rows), GRID_W).astype(jnp.float32)
    col_ids = jnp.tile(jnp.arange(GRID_W), rows).astype(jnp.float32)
    n_freq = HEAD_DIM // 4
    freqs = ROPE_THETA ** (-jnp.arange(n_freq, dtype=jnp.float32) / n_freq)
    ang = jnp.stack([row_ids[:, None] * freqs, col_ids[:, None] * freqs], axis=1)
    return jnp.cos(ang), jnp.sin(ang)

def apply_rope(x, cos, sin):
    n_freq = HEAD_DIM // 4
    xf = x.astype(jnp.float32).reshape(*x.shape[:-1], 2, 2, n_freq)
    x1, x2 = xf[..., 0, :], xf[..., 1, :]
    cb, sb = cos[None, :, None], sin[None, :, None]
    out = jnp.stack([x1 * cb - x2 * sb, x2 * cb + x1 * sb], axis=-2)
    return out.reshape(x.shape).astype(x.dtype)

def gqa_softmax(qg, k, v):
    s = jnp.einsum('bqgrd,bkgd->bgrqk', qg, k, preferred_element_type=jnp.float32) * (HEAD_DIM ** -0.5)
    p = jax.nn.softmax(s, axis=-1).astype(v.dtype)
    return jnp.einsum('bgrqk,bkgd->bqgrd', p, v)

def latent_attention(q, k, v, k_ctx, v_ctx):
    b, s = q.shape[:2]
    n_blk = s // Q_BLOCK
    k_all = jnp.concatenate([k_ctx, k], axis=1)
    v_all = jnp.concatenate([v_ctx, v], axis=1)
    qb = q.reshape(b, n_blk, Q_BLOCK, N_KV_HEADS, GQA_GROUP, HEAD_DIM).transpose(1, 0, 2, 3, 4, 5)
    o = lax.map(lambda qblk: gqa_softmax(qblk, k_all, v_all), qb)
    return o.transpose(1, 0, 2, 3, 4, 5).reshape(b, s, ATTN_WIDTH)

def context_attention(q, k, v):
    b, cl = q.shape[:2]
    qg = q.reshape(b, cl, N_KV_HEADS, GQA_GROUP, HEAD_DIM)
    return gqa_softmax(qg, k, v).reshape(b, cl, ATTN_WIDTH)

def pool_mix(u, w_pool, pool_scale):
    b, length, _ = u.shape
    ug = u.astype(jnp.float32).reshape(b, length, N_POOL_GROUPS, POOL_GROUP)
    cs = jnp.concatenate([jnp.zeros((b, 1, N_POOL_GROUPS, POOL_GROUP), jnp.float32),
                          jnp.cumsum(ug, axis=1)], axis=1)
    t = jnp.arange(length)
    means = []
    for gi, w in enumerate(POOL_WINDOWS):
        lo = jnp.clip(t - w // 2, 0, length)
        hi = jnp.clip(t + w - w // 2, 0, length)
        cs_g = cs[:, :, gi]
        cnt = (hi - lo).astype(jnp.float32)
        means.append((cs_g[:, hi] - cs_g[:, lo]) / cnt[None, :, None])
    d = jnp.stack(means, axis=2) - ug
    y = jnp.einsum('blgc,gcd->blgd', d, w_pool.astype(jnp.float32)).reshape(b, length, POOL_WIDTH)
    return (y * pool_scale.astype(jnp.float32)).astype(u.dtype)

def fourier_mix(u, w_four):
    b, length, _ = u.shape
    ug = u.astype(jnp.float32).reshape(b, length, N_FOURIER_GROUPS, FOURIER_GROUP)
    f = jnp.fft.fft2(ug, axes=(1, 3), norm='ortho').real
    y = jnp.einsum('blgc,gcd->blgd', f, w_four.astype(jnp.float32))
    return y.reshape(b, length, FOURIER_WIDTH).astype(u.dtype)

def head_rms(x, g):
    return rms_norm(x, g)

def swiglu(h, w_gate_up, w_down):
    gate, up = jnp.split(h @ w_gate_up, 2, axis=-1)
    return (jax.nn.silu(gate) * up) @ w_down

def first_inputs(seed: int = 0) -> dict:
    key = jax.random.key(seed)
    ks = jax.random.split(key, 18)
    f32 = jnp.float32

    def nrm(k, shape, s):
        return jax.random.normal(k, shape, f32) * s

    return {
        "x": nrm(ks[0], (BATCH, SEQ, D_MODEL), 1.0),
        "c": nrm(ks[1], (BATCH, D_MODEL), 1.0),
        "ctx": nrm(ks[2], (BATCH, CTX_LEN, D_MODEL), 1.0),
        "c_ctx": nrm(ks[3], (D_MODEL,), 1.0),
        "w_ada": nrm(ks[4], (DEPTH, D_MODEL, 6 * D_MODEL), D_MODEL ** -0.5),
        "b_ada": nrm(ks[5], (DEPTH, 6 * D_MODEL), 0.01),
        "g_mix": 1.0 + nrm(ks[6], (DEPTH, D_MODEL), 0.02),
        "g_ffn": 1.0 + nrm(ks[7], (DEPTH, D_MODEL), 0.02),
        "w_in": nrm(ks[8], (DEPTH, D_MODEL, IN_WIDTH), D_MODEL ** -0.5),
        "q_gain": 1.0 + nrm(ks[9], (DEPTH, HEAD_DIM), 0.02),
        "k_gain": 1.0 + nrm(ks[10], (DEPTH, HEAD_DIM), 0.02),
        "w_pool": nrm(ks[11], (DEPTH, N_POOL_GROUPS, POOL_GROUP, POOL_GROUP), POOL_GROUP ** -0.5),
        "pool_scale": 1.0 + nrm(ks[12], (DEPTH, POOL_WIDTH), 0.02),
        "w_four": nrm(ks[13], (DEPTH, N_FOURIER_GROUPS, FOURIER_GROUP, FOURIER_GROUP), FOURIER_GROUP ** -0.5),
        "w_out": nrm(ks[14], (DEPTH, MIX_WIDTH, D_MODEL), MIX_WIDTH ** -0.5),
        "w_gate_up": nrm(ks[15], (DEPTH, D_MODEL, 2 * D_FF), D_MODEL ** -0.5),
        "w_down": nrm(ks[16], (DEPTH, D_FF, D_MODEL), D_FF ** -0.5),
    }

def first_block(x, c, ctx, c_ctx, w_ada, b_ada, g_mix, g_ffn, w_in, q_gain, k_gain,
              w_pool, pool_scale, w_four, w_out, w_gate_up, w_down):
    b, s, _ = x.shape
    cl = ctx.shape[1]
    cos, sin = axial_rope_tables(s)
    sc, scc = jax.nn.silu(c), jax.nn.silu(c_ctx)
    for i in range(DEPTH):
        update_ctx = i < DEPTH - 1
        mod_x = (sc @ w_ada[i] + b_ada[i])[:, None, :]
        mod_c = scc @ w_ada[i] + b_ada[i]
        sh1, sc1, ga1, sh2, sc2, ga2 = jnp.split(mod_x, 6, axis=-1)
        csh1, csc1, cga1, csh2, csc2, cga2 = jnp.split(mod_c, 6, axis=-1)

        hx = rms_norm(x, g_mix[i]) * (1.0 + sc1) + sh1
        hc = rms_norm(ctx, g_mix[i]) * (1.0 + csc1) + csh1
        zx = hx @ w_in[i]
        if update_ctx:
            zc = hc @ w_in[i]
            zc_kv = zc[..., Q_END:KV_END]
        else:
            zc_kv = hc @ w_in[i][:, Q_END:KV_END]
        kc = head_rms(zc_kv[..., :KV_WIDTH].reshape(b, cl, N_KV_HEADS, HEAD_DIM), k_gain[i])
        vc = zc_kv[..., KV_WIDTH:].reshape(b, cl, N_KV_HEADS, HEAD_DIM)

        q = apply_rope(head_rms(zx[..., :Q_END].reshape(b, s, N_Q_HEADS, HEAD_DIM), q_gain[i]), cos, sin)
        k = apply_rope(head_rms(zx[..., Q_END:K_END].reshape(b, s, N_KV_HEADS, HEAD_DIM), k_gain[i]), cos, sin)
        v = zx[..., K_END:KV_END].reshape(b, s, N_KV_HEADS, HEAD_DIM)
        mx = jnp.concatenate([
            latent_attention(q, k, v, kc, vc),
            pool_mix(zx[..., KV_END:POOL_END], w_pool[i], pool_scale[i]),
            fourier_mix(zx[..., POOL_END:], w_four[i]),
        ], axis=-1)
        x = x + ga1 * (mx @ w_out[i])

        if update_ctx:
            qc = head_rms(zc[..., :Q_END].reshape(b, cl, N_Q_HEADS, HEAD_DIM), q_gain[i])
            mc = jnp.concatenate([
                context_attention(qc, kc, vc),
                pool_mix(zc[..., KV_END:POOL_END], w_pool[i], pool_scale[i]),
                fourier_mix(zc[..., POOL_END:], w_four[i]),
            ], axis=-1)
            ctx = ctx + cga1 * (mc @ w_out[i])

        fx = rms_norm(x, g_ffn[i]) * (1.0 + sc2) + sh2
        x = x + ga2 * swiglu(fx, w_gate_up[i], w_down[i])
        if update_ctx:
            fc = rms_norm(ctx, g_ffn[i]) * (1.0 + csc2) + csh2
            ctx = ctx + cga2 * swiglu(fc, w_gate_up[i], w_down[i])
    return x


DEPTH_2 = 1

D_MIX = D_MODEL
D_ATT = D_MIX // 2
ATT_HEAD_DIM = 64
ATT_HEADS = D_ATT // ATT_HEAD_DIM
D_MLSTM = D_MIX - D_ATT
MLSTM_HEADS = 4
MLSTM_HEAD_DIM = D_MLSTM // MLSTM_HEADS
IN_WIDTH_2 = 3 * D_ATT + 4 * D_MLSTM + 2 * MLSTM_HEADS

MOBA_BLOCK = 256
MOBA_TOPK = 3
MOBA_Q_CHUNK = 32

MLSTM_CHUNK = 128
CONV_WIDTH = 4

N_GROUPS = 4
EXPERTS_PER_GROUP = 8
N_EXPERTS = N_GROUPS * EXPERTS_PER_GROUP
TOP_K_EXPERTS = 2
D_EXPERT = 512
MOE_BLOCK_ROWS = 256

NORM_EPS = 1e-6
NEG_INF = -1e30


def rms_norm_2(x, g):
    xf = x.astype(jnp.float32)
    y = xf * lax.rsqrt(jnp.mean(xf * xf, axis=-1, keepdims=True) + NORM_EPS)
    return (y * g.astype(jnp.float32)).astype(x.dtype)

def head_rms_norm(h, g, n_heads):
    b, s, w = h.shape
    hf = h.astype(jnp.float32).reshape(b, s, n_heads, w // n_heads)
    hf = hf * lax.rsqrt(jnp.mean(hf * hf, axis=-1, keepdims=True) + NORM_EPS)
    return (hf.reshape(b, s, w) * g.astype(jnp.float32)).astype(h.dtype)

def modulate(x, g, shift, scale):
    return rms_norm_2(x, g) * (1.0 + scale[:, None, :]) + shift[:, None, :]

def split_heads(t, n_heads):
    b, s, w = t.shape
    return t.reshape(b, s, n_heads, w // n_heads).transpose(0, 2, 1, 3)

def merge_heads(t):
    b, h, s, d = t.shape
    return t.transpose(0, 2, 1, 3).reshape(b, s, h * d)

def rope(t, positions):
    half = t.shape[-1] // 2
    inv_freq = ROPE_THETA ** (-jnp.arange(half, dtype=jnp.float32) / half)
    ang = positions.astype(jnp.float32)[:, None, :, None] * inv_freq
    cos, sin = jnp.cos(ang), jnp.sin(ang)
    tf = t.astype(jnp.float32)
    t1, t2 = tf[..., :half], tf[..., half:]
    return jnp.concatenate([t1 * cos - t2 * sin, t2 * cos + t1 * sin], axis=-1).astype(t.dtype)

def moba_attention(q, k, v):
    b, h, s, dh = q.shape
    nb = -(-s // MOBA_BLOCK)
    s_pad = nb * MOBA_BLOCK
    pad = ((0, 0), (0, 0), (0, s_pad - s), (0, 0))
    kb = jnp.pad(k, pad).reshape(b, h, nb, MOBA_BLOCK, dh)
    vb = jnp.pad(v, pad).reshape(b, h, nb, MOBA_BLOCK, dh)
    scale = dh ** -0.5

    k_mean = jnp.mean(kb.astype(jnp.float32), axis=3)
    gate = jnp.einsum('bhsd,bhnd->bhsn', q.astype(jnp.float32), k_mean)
    q_blk = jnp.arange(s) // MOBA_BLOCK
    past = jnp.arange(nb)[None, :] < q_blk[:, None]
    gate = jnp.where(past, gate, NEG_INF)
    topk = min(MOBA_TOPK, nb)
    _, sel = lax.top_k(gate, topk)
    sel_valid = sel < q_blk[:, None]

    nqc = s // MOBA_Q_CHUNK

    def to_chunks(t):
        t = t.reshape((b, h, nqc, MOBA_Q_CHUNK) + t.shape[3:])
        return jnp.moveaxis(t, 2, 0)

    bi = jnp.arange(b)[:, None, None]
    hi = jnp.arange(h)[None, :, None]

    def chunk(args):
        q_c, sel_c, valid_c, ci = args
        start = ci * MOBA_Q_CHUNK
        j = start // MOBA_BLOCK
        k_own = lax.dynamic_index_in_dim(kb, j, axis=2, keepdims=False)
        v_own = lax.dynamic_index_in_dim(vb, j, axis=2, keepdims=False)
        q_pos = start + jnp.arange(MOBA_Q_CHUNK)
        k_pos = j * MOBA_BLOCK + jnp.arange(MOBA_BLOCK)
        causal = k_pos[None, :] <= q_pos[:, None]
        qf = q_c.astype(jnp.float32) * scale
        s_own = jnp.where(causal, jnp.einsum('bhqd,bhkd->bhqk', qf, k_own.astype(jnp.float32)), NEG_INF)
        scores = [s_own]
        for r in range(topk):
            k_r = kb[bi, hi, sel_c[..., r]]
            s_r = jnp.einsum('bhqd,bhqkd->bhqk', qf, k_r.astype(jnp.float32))
            scores.append(jnp.where(valid_c[..., r, None], s_r, NEG_INF))
        s_all = jnp.stack(scores, axis=3)
        p = jax.nn.softmax(s_all.reshape(b, h, MOBA_Q_CHUNK, -1), axis=-1).reshape(s_all.shape)
        out = jnp.einsum('bhqk,bhkd->bhqd', p[..., 0, :], v_own.astype(jnp.float32))
        for r in range(topk):
            v_r = vb[bi, hi, sel_c[..., r]]
            out = out + jnp.einsum('bhqk,bhqkd->bhqd', p[..., r + 1, :], v_r.astype(jnp.float32))
        return out.astype(v.dtype)

    out = lax.map(chunk, (to_chunks(q), to_chunks(sel), to_chunks(sel_valid),
                          jnp.arange(nqc, dtype=jnp.int32)))
    return jnp.moveaxis(out, 0, 2).reshape(b, h, s, dh)

def mlstm_chunkwise(q, k, v, i_pre, f_pre):
    b, nh, s, dh = q.shape
    L = MLSTM_CHUNK
    nc = s // L
    q = q.reshape(b, nh, nc, L, dh)
    k = k.reshape(b, nh, nc, L, dh)
    v = v.reshape(b, nh, nc, L, dh)
    logf = jax.nn.log_sigmoid(f_pre).reshape(b, nh, nc, L)
    ig = i_pre.reshape(b, nh, nc, L)
    cum = jnp.cumsum(logf, axis=-1)
    a = cum[..., -1]

    g = a[..., None] - cum + ig
    m_loc = jnp.max(g, axis=-1)
    w = jnp.exp(g - m_loc[..., None])
    c_loc = jnp.einsum('bhcs,bhcse,bhcsd->bhced', w, v, k)
    n_loc = jnp.einsum('bhcs,bhcsd->bhcd', w, k)

    def step(carry, inp):
        c_st, n_st, m_st = carry
        a_c, m_loc_c, c_loc_c, n_loc_c = inp
        m_new = jnp.maximum(a_c + m_st, m_loc_c)
        s_prev = jnp.exp(a_c + m_st - m_new)
        s_loc = jnp.exp(m_loc_c - m_new)
        c_new = s_prev[..., None, None] * c_st + s_loc[..., None, None] * c_loc_c
        n_new = s_prev[..., None] * n_st + s_loc[..., None] * n_loc_c
        return (c_new, n_new, m_new), (c_st, n_st, m_st)

    init = (jnp.zeros((b, nh, dh, dh), jnp.float32),
            jnp.zeros((b, nh, dh), jnp.float32),
            jnp.zeros((b, nh), jnp.float32))
    xs = (jnp.moveaxis(a, 2, 0), jnp.moveaxis(m_loc, 2, 0),
          jnp.moveaxis(c_loc, 2, 0), jnp.moveaxis(n_loc, 2, 0))
    _, (c_prev, n_prev, m_prev) = lax.scan(step, init, xs)
    c_prev = jnp.moveaxis(c_prev, 0, 2)
    n_prev = jnp.moveaxis(n_prev, 0, 2)
    m_prev = jnp.moveaxis(m_prev, 0, 2)

    causal = jnp.tril(jnp.ones((L, L), dtype=bool))
    dmat = jnp.where(causal, cum[..., :, None] - cum[..., None, :] + ig[..., None, :], NEG_INF)
    inter = cum + m_prev[..., None]
    m_t = jnp.maximum(inter, jnp.max(dmat, axis=-1))
    s_qk = jnp.einsum('bhctd,bhcsd->bhcts', q, k) * jnp.exp(dmat - m_t[..., None])
    w_inter = jnp.exp(inter - m_t)
    num = (jnp.einsum('bhcts,bhcse->bhcte', s_qk, v)
           + w_inter[..., None] * jnp.einsum('bhced,bhctd->bhcte', c_prev, q))
    den = jnp.sum(s_qk, axis=-1) + w_inter * jnp.einsum('bhcd,bhctd->bhct', n_prev, q)
    h = num / jnp.maximum(jnp.abs(den), jnp.exp(-m_t))[..., None]
    return h.reshape(b, nh, s, dh)

def causal_conv(u, w, bias):
    ch = u.shape[-1]
    out = lax.conv_general_dilated(u, w[:, None, :], window_strides=(1,),
                                   padding=[(CONV_WIDTH - 1, 0)],
                                   dimension_numbers=('NWC', 'WIO', 'NWC'),
                                   feature_group_count=ch)
    return out + bias

def hier_moe(h, w_rg, b_rg, w_re, b_re, w1, w3, w2):
    t, d = h.shape
    gp = jax.nn.softmax((h @ w_rg + b_rg).astype(jnp.float32), axis=-1)
    g_w, g_idx = lax.top_k(gp, 1)
    el = (h @ w_re + b_re).astype(jnp.float32).reshape(t, N_GROUPS, EXPERTS_PER_GROUP)
    el_sel = jnp.take_along_axis(el, g_idx[:, :, None], axis=1)[:, 0]
    ep = jax.nn.softmax(el_sel, axis=-1)
    e_w, e_loc = lax.top_k(ep, TOP_K_EXPERTS)
    weights = g_w * e_w / jnp.sum(e_w, axis=-1, keepdims=True)
    expert_id = g_idx * EXPERTS_PER_GROUP + e_loc

    n_assign = t * TOP_K_EXPERTS
    flat_e = expert_id.reshape(-1)
    flat_w = weights.reshape(-1)
    flat_tok = jnp.repeat(jnp.arange(t, dtype=jnp.int32), TOP_K_EXPERTS)
    order = jnp.argsort(flat_e)
    sorted_e = flat_e[order]
    counts = jnp.bincount(flat_e, length=N_EXPERTS)
    padded = ((counts + MOE_BLOCK_ROWS - 1) // MOE_BLOCK_ROWS) * MOE_BLOCK_ROWS
    pad_end = jnp.cumsum(padded)
    pad_start = pad_end - padded
    cnt_start = jnp.cumsum(counts) - counts
    dest = pad_start[sorted_e] + (jnp.arange(n_assign) - cnt_start[sorted_e])
    n_rows = n_assign + N_EXPERTS * MOE_BLOCK_ROWS
    n_blocks = n_rows // MOE_BLOCK_ROWS
    row_tok = jnp.zeros((n_rows,), jnp.int32).at[dest].set(flat_tok[order])
    row_w = jnp.zeros((n_rows,), jnp.float32).at[dest].set(flat_w[order])
    block_e = jnp.minimum(jnp.searchsorted(pad_end, jnp.arange(n_blocks) * MOE_BLOCK_ROWS, side='right'),
                          N_EXPERTS - 1)
    xs = h[row_tok].reshape(n_blocks, MOE_BLOCK_ROWS, d)

    def expert_block(args):
        xb, e = args
        return (jax.nn.silu(xb @ w1[e]) * (xb @ w3[e])) @ w2[e]

    ys = lax.map(expert_block, (xs, block_e)).reshape(n_rows, d)
    ys = ys * row_w[:, None].astype(h.dtype)
    return jnp.zeros((t, d), h.dtype).at[row_tok].add(ys)

def second_inputs(seed: int = 0) -> dict:
    key = jax.random.key(seed)
    ks = jax.random.split(key, 24)

    def nrm(k, shape, scale):
        return jax.random.normal(k, shape, jnp.float32) * scale

    x = nrm(ks[0], (BATCH, SEQ, D_MODEL), 1.0)
    c = nrm(ks[1], (BATCH, D_MODEL), 1.0)
    positions = (jnp.arange(SEQ, dtype=jnp.int32)[None, :]
                 + jax.random.randint(ks[2], (BATCH, 1), 0, 1024, dtype=jnp.int32))
    w_ada = nrm(ks[3], (DEPTH_2, D_MODEL, 6 * D_MODEL), 0.5 * D_MODEL ** -0.5)
    b_ada = nrm(ks[4], (DEPTH_2, 6 * D_MODEL), 0.02)
    norm1_g = 1.0 + nrm(ks[5], (DEPTH_2, D_MODEL), 0.02)
    w_in = nrm(ks[6], (DEPTH_2, D_MODEL, IN_WIDTH_2), D_MODEL ** -0.5)
    b_gate = jnp.concatenate([
        nrm(ks[7], (DEPTH_2, MLSTM_HEADS), 0.1),
        jnp.linspace(3.0, 6.0, MLSTM_HEADS, dtype=jnp.float32)[None, :]
        + nrm(ks[8], (DEPTH_2, MLSTM_HEADS), 0.1)], axis=-1)
    conv_w = nrm(ks[9], (DEPTH_2, CONV_WIDTH, 2 * D_MLSTM), CONV_WIDTH ** -0.5)
    conv_b = nrm(ks[10], (DEPTH_2, 2 * D_MLSTM), 0.02)
    attn_out_g = 1.0 + nrm(ks[11], (DEPTH_2, D_ATT), 0.02)
    mlstm_out_g = 1.0 + nrm(ks[12], (DEPTH_2, D_MLSTM), 0.02)
    w_out = nrm(ks[13], (DEPTH_2, D_MIX, D_MODEL), D_MIX ** -0.5)
    norm2_g = 1.0 + nrm(ks[14], (DEPTH_2, D_MODEL), 0.02)
    w_rg = nrm(ks[15], (DEPTH_2, D_MODEL, N_GROUPS), D_MODEL ** -0.5)
    b_rg = nrm(ks[16], (DEPTH_2, N_GROUPS), 0.01)
    w_re = nrm(ks[17], (DEPTH_2, D_MODEL, N_EXPERTS), D_MODEL ** -0.5)
    b_re = nrm(ks[18], (DEPTH_2, N_EXPERTS), 0.01)
    w1 = nrm(ks[19], (DEPTH_2, N_EXPERTS, D_MODEL, D_EXPERT), D_MODEL ** -0.5)
    w3 = nrm(ks[20], (DEPTH_2, N_EXPERTS, D_MODEL, D_EXPERT), D_MODEL ** -0.5)
    w2 = nrm(ks[21], (DEPTH_2, N_EXPERTS, D_EXPERT, D_MODEL), D_EXPERT ** -0.5)
    norm_f_g = 1.0 + nrm(ks[22], (D_MODEL,), 0.02)
    return {"x": x, "c": c, "positions": positions, "w_ada": w_ada, "b_ada": b_ada,
            "norm1_g": norm1_g, "w_in": w_in, "b_gate": b_gate, "conv_w": conv_w,
            "conv_b": conv_b, "attn_out_g": attn_out_g, "mlstm_out_g": mlstm_out_g,
            "w_out": w_out, "norm2_g": norm2_g, "w_rg": w_rg, "b_rg": b_rg,
            "w_re": w_re, "b_re": b_re, "w1": w1, "w3": w3, "w2": w2, "norm_f_g": norm_f_g}

def second_block(x, c, positions, w_ada, b_ada, norm1_g, w_in, b_gate, conv_w, conv_b,
              attn_out_g, mlstm_out_g, w_out, norm2_g, w_rg, b_rg, w_re, b_re,
              w1, w3, w2, norm_f_g):
    b, s, d = x.shape
    offs = [D_ATT, 2 * D_ATT, 3 * D_ATT, 3 * D_ATT + 2 * D_MLSTM,
            3 * D_ATT + 3 * D_MLSTM, 3 * D_ATT + 4 * D_MLSTM]
    for l in range(DEPTH_2):
        mod = jax.nn.silu(c) @ w_ada[l] + b_ada[l]
        sh1, sc1, g1, sh2, sc2, g2 = jnp.split(mod, 6, axis=-1)

        h = modulate(x, norm1_g[l], sh1, sc1)
        proj = h @ w_in[l]
        q_a, k_a, v_a, qk_m, v_m, o_m, gates = jnp.split(proj, offs, axis=-1)

        qa = rope(split_heads(q_a, ATT_HEADS), positions)
        ka = rope(split_heads(k_a, ATT_HEADS), positions)
        attn = merge_heads(moba_attention(qa, ka, split_heads(v_a, ATT_HEADS)))
        attn = head_rms_norm(attn, attn_out_g[l], ATT_HEADS)

        qk_m = jax.nn.silu(causal_conv(qk_m, conv_w[l], conv_b[l]))
        q_m, k_m = jnp.split(qk_m, 2, axis=-1)
        gates = gates.astype(jnp.float32) + b_gate[l].astype(jnp.float32)
        i_pre = jnp.transpose(gates[..., :MLSTM_HEADS], (0, 2, 1))
        f_pre = jnp.transpose(gates[..., MLSTM_HEADS:], (0, 2, 1))
        hm = mlstm_chunkwise(split_heads(q_m, MLSTM_HEADS).astype(jnp.float32),
                             split_heads(k_m, MLSTM_HEADS).astype(jnp.float32) * MLSTM_HEAD_DIM ** -0.5,
                             split_heads(v_m, MLSTM_HEADS).astype(jnp.float32),
                             i_pre, f_pre)
        hm = head_rms_norm(merge_heads(hm), mlstm_out_g[l], MLSTM_HEADS)
        hm = (hm * jax.nn.sigmoid(o_m.astype(jnp.float32))).astype(x.dtype)

        y = jnp.concatenate([attn.astype(x.dtype), hm], axis=-1) @ w_out[l]
        x = x + g1[:, None, :] * y

        h2 = modulate(x, norm2_g[l], sh2, sc2)
        moe = hier_moe(h2.reshape(b * s, d), w_rg[l], b_rg[l], w_re[l], b_re[l],
                       w1[l], w3[l], w2[l]).reshape(b, s, d)
        x = x + g2[:, None, :] * moe
    return rms_norm_2(x, norm_f_g)


def setup_inputs(seed=0):
    out = dict(first_inputs(seed))
    for name, value in second_inputs(seed + 1).items():
        if name != "x":
            out[name + "_2"] = value
    return out


def reference(
    x, c, ctx, c_ctx, w_ada, b_ada, g_mix, g_ffn, w_in, q_gain, k_gain, w_pool, pool_scale,
    w_four, w_out, w_gate_up, w_down, c_2, positions_2, w_ada_2, b_ada_2, norm1_g_2, w_in_2,
    b_gate_2, conv_w_2, conv_b_2, attn_out_g_2, mlstm_out_g_2, w_out_2, norm2_g_2, w_rg_2,
    b_rg_2, w_re_2, b_re_2, w1_2, w3_2, w2_2, norm_f_g_2,
):
    x = first_block(
        x, c, ctx, c_ctx, w_ada, b_ada, g_mix, g_ffn, w_in, q_gain, k_gain, w_pool, pool_scale,
        w_four, w_out, w_gate_up, w_down,
    )
    return second_block(
        x, c_2, positions_2, w_ada_2, b_ada_2, norm1_g_2, w_in_2, b_gate_2, conv_w_2, conv_b_2,
        attn_out_g_2, mlstm_out_g_2, w_out_2, norm2_g_2, w_rg_2, b_rg_2, w_re_2, b_re_2, w1_2,
        w3_2, w2_2, norm_f_g_2,
    )


_drawn_inputs = setup_inputs


def setup_inputs(seed=0):
    import zlib

    import numpy as np

    out = dict(_drawn_inputs(seed))
    spreads = {}
    factors = {'b_ada': 2.732,
     'g_mix': 4.772,
     'g_ffn': 2.847,
     'q_gain': 8.0,
     'k_gain': 8.0,
     'pool_scale': 6.508,
     'b_ada_2': 3.596,
     'norm1_g_2': 8.0,
     'conv_b_2': 64.0,
     'attn_out_g_2': 8.0,
     'mlstm_out_g_2': 8.0,
     'norm2_g_2': 8.0,
     'b_rg_2': 8.0,
     'b_re_2': 34.337,
     'norm_f_g_2': 8.755}
    for name, (base, spread) in spreads.items():
        noise = np.random.default_rng([zlib.crc32(name.encode()), seed]).standard_normal(out[name].shape)
        drawn = base * np.exp(spread * noise) if base else spread * noise
        out[name] = jnp.asarray(drawn.astype(out[name].dtype))
    for name, factor in factors.items():
        out[name] = (out[name] * factor).astype(out[name].dtype)
    return out
```

```python
import numpy as np
import concourse.bass as bass
from concourse import mybir

F32 = mybir.dt.float32
F32R = mybir.dt.float32r
BF16 = mybir.dt.bfloat16
I32 = mybir.dt.int32
U32 = mybir.dt.uint32
ALU = mybir.AluOpType
ACT = mybir.ActivationFunctionType
AX = mybir.AxisListType

D = 1024
KT = 8
NEG = -1.0e30
EPS = 1e-6
HALF = 11
N_EXP = 32
CAP = 128
N_EXTRA = 3
N_BLOCKS = N_EXP + N_EXTRA
N_SLOTS = 16
EXTRA_AFTER = {7 + 8 * j: j for j in range(N_EXTRA)}

V_C, V_CCTX, V_C2, V_GMIX, V_GFFN = 0, 8, 16, 24, 40
V_N1, V_N2, V_NF, V_CW, V_CB, V_AG, V_MG = 56, 64, 72, 80, 112, 120, 124
V_BADA, V_PS, V_QG, V_KG, V_BADA2 = 128, 224, 228, 230, 256

K_POOL, K_DFT, K_R1, K_D, K_RD, K_CD, K_SD = 0, 0, 1024, 1152, 1408, 1664, 1792
K_END = 1920
S_ID, S_BD, S_COS, S_SIN = 0, 128, 256, 512
S_END = 768
B_R2, B_TRI, B_TRIT, B_SLT, B_IOTA, B_FREQ = 0, 128, 384, 512, 640, 768
B_END = 769


def constants():
    eye = np.eye(128)
    blocks = np.kron(np.eye(2), np.ones((64, 64)))
    r1 = np.zeros((128, 128))
    r2 = np.zeros((128, 128))
    for m in range(128):
        if (m // 16) % 2 == 0:
            r1[m, m + 16] = -1
        else:
            r1[m, m - 16] = 1
        if (m // 32) % 2 == 0:
            r2[m, m + 32] = -1
        else:
            r2[m, m - 32] = 1
    dup = [np.zeros((128, 128)) for _ in range(2)]
    for g in range(2):
        for m in range(128):
            dup[g][m, 64 * g + m % 64] = 1
    t = np.arange(256)
    freqs = np.float32(10000.0) ** (-np.arange(16, dtype=np.float32) / np.float32(16))
    ang = np.zeros((128, 256), np.float32)
    for m in range(128):
        a, f = (m % 64) // 32, m % 16
        ids = (t // 64 if a == 0 else t % 64).astype(np.float32)
        ang[m] = ids * freqs[f]
    lt = 2 * np.pi * ((t[:, None] * t[None, :]) % 256) / 256
    c = np.arange(64)
    ld = 2 * np.pi * ((c[:, None] * c[None, :]) % 64) / 64
    dft = np.concatenate([np.cos(lt), np.sin(lt)], axis=1) / 16.0
    pool = np.zeros((256, 4, 256))
    for w, win in enumerate((2, 4, 8, 16)):
        for i in range(256):
            lo, hi = max(i - win // 2, 0), min(i + win - win // 2, 256)
            pool[lo:hi, w, i] += 1.0 / (hi - lo)
            pool[i, w, i] -= 1.0
    mix = np.zeros((128, K_END))
    kpool = pool.reshape(2, 128, 1024).transpose(1, 0, 2).reshape(128, 2048)
    mix[:, K_DFT:K_R1] = dft.reshape(2, 128, 512).transpose(1, 0, 2).reshape(128, 1024)
    mix[:, K_R1:K_D] = r1.T
    for g in range(2):
        mix[:, K_D + 128 * g:K_D + 128 * g + 128] = dup[g].T
        mix[:, K_RD + 128 * g:K_RD + 128 * g + 128] = (r1 @ dup[g]).T
    mix[:, K_CD:K_SD] = np.kron(np.eye(2), np.cos(ld) / 8.0)
    mix[:, K_SD:K_END] = np.kron(np.eye(2), -np.sin(ld) / 8.0)
    res = np.zeros((128, S_END))
    res[:, S_ID:S_BD] = eye
    res[:, S_BD:S_COS] = blocks
    res[:, S_COS:S_SIN] = np.cos(ang)
    res[:, S_SIN:S_END] = np.sin(ang)
    two = np.zeros((128, B_END))
    i = np.arange(128)
    two[:, B_R2:B_TRI] = r2.T
    two[:, B_TRI + 128:B_TRIT] = np.where(i[None, :] <= i[:, None], 0, NEG)
    two[:, B_TRIT:B_SLT] = np.where(i[:, None] <= i[None, :], 0, NEG)
    two[:, B_SLT:B_IOTA] = i[:, None] < i[None, :]
    two[:, B_IOTA:B_FREQ] = np.arange(128)
    half = np.arange(32, dtype=np.float32)
    inv = np.float32(10000.0) ** (-half / np.float32(32))
    two[:, B_FREQ] = inv[i % 32]
    return {"k_pool": np.ascontiguousarray(kpool, np.float32), "k_mix": mix.astype(np.float32), "k_res": res.astype(np.float32), "k_two": two.astype(np.float32)}


class Engine:

    def __init__(self, sem):
        self.sem, self.n, self.entries = sem, 0, []

    def __call__(self, fn, *waits):
        self.n += 1
        self.entries.append((fn, waits, True))
        return (self.sem, self.n)

    def raw(self, fn, *waits):
        self.entries.append((fn, waits, False))

    def last(self):
        return (self.sem, self.n)

    def emit(self, eng):
        reached = {}

        def wait(tokens):
            for t in tokens:
                if isinstance(t, list):
                    wait(t)
                elif t is not None and t[1] > reached.get(t[0].name, 0):
                    eng.wait_ge(t[0], t[1])
                    reached[t[0].name] = t[1]

        for fn, waits, counted in self.entries:
            wait(list(waits))
            ins = fn(eng)
            if counted:
                ins.then_inc(self.sem, 1)


class Buffers:

    def __init__(self, places, free=()):
        self.places, self.i = places, 0
        self.free = [list(free) for _ in places]

    def take(self):
        k = self.i % len(self.places)
        self.i += 1
        before, self.free[k] = self.free[k], []
        return self.places[k], before, self.free[k]


class Loaded:
    def __init__(self, place, ready):
        self.place, self.ready, self.done = place, ready, []


class Chunk:

    def __init__(self, load, view):
        self.load, self.view, self.item = load, view, None

    def get(self):
        if self.item is None:
            self.item = self.load()
        return self.item


class Ring:

    def __init__(self, sp, slots, sems, counts, before):
        self.sp, self.slots, self.sems, self.counts = sp, slots, sems, counts
        self.before, self.i = before, 0

    def load(self, fill, dmas=1):
        k = self.i % len(self.slots)
        self.i += 1
        place, sem = self.slots[k], self.sems[k]
        self.counts[k] += 16 * dmas
        item = Loaded(place, (sem, self.counts[k]))
        self.sp.raw(lambda e: fill(e, place, sem), self.before[k])
        self.before[k] = item.done
        return item


def block_program(nc, A):
    pe, act, dve, pool, sp = (Engine(nc.alloc_semaphore(n)) for n in
                              ("s_pe", "s_act", "s_dve", "s_pool", "s_sp"))
    KB = 1024
    BASE = 16512

    def at(name, shape, dt, off):
        return nc.alloc_sbuf_tensor_at(name, shape, dt, offset=BASE + off)

    oX, oH, oG, oR, oZ, oS, oW = 0, 16 * KB, 48 * KB, 92 * KB, 156 * KB, 176 * KB, 176 * KB + 9888
    XT = at("XT", [128, KT, 512], F32, oX)
    HH = at("HH", [128, KT, 512], F32R, oH)
    HL = at("HL", [128, KT, 512], F32R, oH + 16 * KB)
    GH = at("GH", [128, HALF, 512], F32R, oG)
    GL = at("GL", [128, HALF, 512], F32R, oG + 22 * KB)
    ring_slots = [at(f"R{i}", [128, 2048], F32, oR + 8 * KB * i) for i in range(8)]
    ws = [(at(f"WH{i}", [128, HALF, 128], F32R, oW + i * 11264),
           at(f"WL{i}", [128, HALF, 128], F32R, oW + i * 11264 + 5632)) for i in range(2)]
    QT = at("QT", [128, 4, 512], F32, oZ)
    KTr = at("KTr", [128, 512], F32, oZ + 8 * KB)
    Z = at("Z", [128, 4, 640], F32, oZ + 10 * KB)
    tmp = [at(f"TMP{i}", [128, 512], F32, oZ + 2 * KB * i) for i in range(8)]
    RES = at("RES", [128, S_END], F32, oS)
    ONES = at("ONES", [128, 128], F32, oS + 3072)
    VEC = at("VEC", [128, 304], F32, oS + 3584)
    MOD = at("MOD", [128, 3, 48, 3], F32, oS + 4800)
    SG = at("SG", [128, 8, 2], F32, oS + 6528)
    WPF = at("WPF", [128, 4, 128], F32, oS + 6592)
    ST = at("ST", [128, 48], F32, oS + 8640)
    EB = at("EB", [128, 1], F32, oS + 8832)
    SC = at("SC", [128, KT, 32], F32, oS + 8864)
    AB = Buffers([at(f"AT{i}", [128, 512], F32, oZ + 16 * KB + 2048 * i) for i in range(2)])
    QR = at("QR", [128, 4, 512], F32, oH)
    KD = at("KD", [128, 2, 512], F32, oH + 8 * KB)
    mt = [at(f"MT{i}", [128, 512], F32, oH + 12 * KB + 2 * KB * i) for i in range(3)]
    pbuf = [at(f"P{i}", [128, 512], F32, oH + 18 * KB + 2 * KB * i) for i in range(3)]
    ptbuf = [at(f"PT{i}", [128, 4, 256], F32, oH + 24 * KB + 4 * KB * i) for i in range(2)]
    zt = [at(f"ZT{i}", [128, 512], F32, oG + 2 * KB * i) for i in range(3)]
    VR = at("VR", [128, 3, 128], F32, oG)

    banks = [nc.alloc_psum_tensor(f"ps{i}", [128, 512], F32) for i in range(8)]
    PS = Buffers(banks)
    WS = Buffers(ws)
    ident = RES[:, S_ID:S_BD]
    bd = RES[:, S_BD:S_COS]
    cos1, sin1 = RES[:, S_COS:S_SIN], RES[:, S_SIN:S_END]

    def fence():
        return [pe.last(), act.last(), dve.last(), pool.last()]

    s_res, s_vec, s_wp = (nc.alloc_semaphore(n) for n in ("s_res", "s_vec", "s_wp"))
    sems = [nc.alloc_semaphore(f"s_r{i}") for i in range(N_SLOTS)]
    counts = [0] * N_SLOTS
    ring = Ring(sp, ring_slots, sems, counts, [[] for _ in range(8)])

    pool.raw(lambda e: e.dma_start(RES[:, :], A["k_res"]).then_inc(s_res, 16))
    t_ones = dve(lambda e: e.memset(ONES[:, :], 1.0))
    t_wpf = dve(lambda e: e.memset(WPF[:, :, :], 0.0))
    t_eb = dve(lambda e: e.memset(EB[:, :], EPS))
    t_vr = dve(lambda e: e.memset(VR[:, :, :], 0.0))
    n_vec = [0]

    def vec_rows(col, ap):
        t, r = divmod(col, 128)
        n = ap.shape[0]
        n_vec[0] += 16
        act.raw(lambda e: e.dma_start(VR[r:r + n, t, 0:ap.shape[1]], ap).then_inc(s_vec, 16), t_vr)

    def rows(ap, pattern, **kw):
        return ap.rearrange(pattern, **kw)

    one = "(a p) -> a p"
    vec_rows(V_C, rows(A["c"], "o (a p) -> (o a) p", p=128))
    vec_rows(V_CCTX, rows(A["c_ctx"], one, p=128))
    vec_rows(V_BADA, rows(A["b_ada"], "l (a p) -> (l a) p", p=128))
    vec_rows(V_GMIX, rows(A["g_mix"], "l (a p) -> (l a) p", p=128))
    vec_rows(V_GFFN, rows(A["g_ffn"], "l (a p) -> (l a) p", p=128))
    vec_rows(V_C2, rows(A["c_2"], "o (a p) -> (o a) p", p=128))
    vec_rows(V_N1, rows(A["norm1_g_2"], "o (a p) -> (o a) p", p=128))
    vec_rows(V_N2, rows(A["norm2_g_2"], "o (a p) -> (o a) p", p=128))
    vec_rows(V_NF, rows(A["norm_f_g_2"], one, p=128))
    vec_rows(V_CW, rows(A["conv_w_2"], "o i (a p) -> (o i a) p", p=128))
    vec_rows(V_CB, rows(A["conv_b_2"], "o (a p) -> (o a) p", p=128))
    vec_rows(V_AG, rows(A["attn_out_g_2"], "o (a p) -> (o a) p", p=128))
    vec_rows(V_MG, rows(A["mlstm_out_g_2"], "o (a p) -> (o a) p", p=128))
    vec_rows(V_PS, rows(A["pool_scale"], "l (a p) -> (l a) p", p=128))
    vec_rows(V_BADA2, rows(A["b_ada_2"], "o (a p) -> (o a) p", p=128))
    for base, name in ((V_QG, "q_gain"), (V_KG, "k_gain")):
        for c in range(2):
            n_vec[0] += 16
            act.raw(lambda e, base=base, name=name, c=c: e.dma_start(
                VR[base - 128:base - 126, 1, 64 * c:64 * c + 64], A[name]).then_inc(s_vec, 16), t_vr)

    def load_mixer_weights(layer, free):
        for k, name in enumerate(("w_pool", "w_four")):
            for g in range(4):
                h = 64 * (g % 2)
                pool.raw(lambda e, k=k, g=g, h=h, name=name: e.dma_start(
                    WPF[h:h + 64, 2 * k + g // 2, h:h + 64], A[name][layer, g]).then_inc(s_wp, 16),
                    t_wpf, free)
        return (s_wp, 128 * (layer + 1))

    rdy_wp = load_mixer_weights(0, [])

    def transpose(out, in_, n=128):
        return lambda e: e.transpose(out, in_, ident[0:n, 0:n])

    def fill_tokens(name):
        def fill(e, place, sem):
            e.dma_start(place[:, :].rearrange("p (a d) -> p a d", a=2),
                        A[name][0].rearrange("(a p) d -> p a d", p=128)).then_inc(sem, 16)
        return fill

    tok = [ring.load(fill_tokens("x")), ring.load(fill_tokens("ctx"))]

    ada_src = [A["w_ada"][0], A["w_ada"][1], A["w_ada_2"][0]]

    def wchunk(src, c0, n):
        v = src.rearrange("(k p) n -> p k n", p=128)

        def fill(e, place, sem):
            e.dma_start(place[:, 0:8 * n].rearrange("p (k n) -> p k n", k=8), v[:, :, c0:c0 + n])\
                .then_inc(sem, 16)
        return fill

    t_vec = []
    bank, before, free = PS.take()
    for t in range(3):
        tt = pe(lambda e, t=t, bank=bank: e.transpose(bank[:, 128 * t:128 * t + 128], VR[:, t, :], ident),
                (s_res, 16), (s_vec, n_vec[0]), before)
    t_vec = dve(lambda e, bank=bank: e.tensor_copy(VEC[:, :], bank[:, 0:304]), tt)
    free.append(t_vec)
    t_qg = dve(lambda e: e.tensor_scalar(VEC[:, V_QG:V_QG + 2], VEC[:, V_QG:V_QG + 2], 0.125, None, ALU.mult), t_vec)
    t_sc = dve(lambda e: e.memset(SC[:, :, :], 0.0))
    t_sc = act(lambda e: e.activation(SC[:, :, 0:3], VEC[:, 0:24].rearrange("p (j k) -> p k j", j=3), ACT.Silu),
               t_vec, t_sc)

    t_x = []
    for k in range(KT):
        bank, before, free = PS.take()
        for a in range(4):
            tt = pe(lambda e, k=k, a=a, bank=bank: e.transpose(
                bank[:, 128 * a:128 * a + 128],
                tok[a // 2].place[:, 1024 * (a % 2) + 128 * k:1024 * (a % 2) + 128 * k + 128], ident),
                tok[a // 2].ready, before, (s_res, 16))
        tc = dve(lambda e, k=k, bank=bank: e.tensor_copy(XT[:, k, :], bank[:, :]), tt)
        free.append(tc)
        t_x.append(tc)
    for item in tok:
        item.done.append(tt)

    t_mod = [[], [], []]

    def ada_load(which, c):
        return which, c, ring.load(wchunk(ada_src[which], 256 * c, 256))

    def ada_use(which, c, item):
        w = item.place[:, :].rearrange("p (k n) -> p k n", k=8)
        bank, before, free = PS.take()

        def mm(e):
            for k in range(KT):
                g = k % 4
                last = e.matmul(bank[32 * g:32 * g + 32, 0:256], SC[:, k, :], w[:, k, :], start=(k < 4), stop=(k >= 4))
            return last
        tp = pe(mm, item.ready, before, t_sc)
        item.done.append(tp)
        AT, bf, fr = AB.take()
        ta = act(lambda e: e.activation(AT[:, 0:256], bank[:, 0:256], ACT.Copy), tp, bf)
        free.append(ta)
        bank2, before, free = PS.take()

        def tr(e):
            for m in range(2):
                last = e.transpose(bank2[:, 128 * m:128 * m + 128], AT[:, 128 * m:128 * m + 128], ident)
            return last
        tp = pe(tr, ta, before)
        fr.append(tp)
        t1 = dve(lambda e: e.tensor_reduce(
            MOD[:, which, 2 * c:2 * c + 2, :],
            bank2[:, 0:256].rearrange("p (m g j) -> p m j g", m=2, g=4)[:, :, 0:3, :], AX.X, ALU.add), tp)
        free.append(t1)
        bcol = (V_BADA + 48 * which if which < 2 else V_BADA2) + 2 * c
        td = dve(lambda e: e.tensor_tensor(
            MOD[:, which, 2 * c:2 * c + 2, :], MOD[:, which, 2 * c:2 * c + 2, :],
            VEC[:, bcol:bcol + 2].unsqueeze(2).to_broadcast([128, 2, 3]), ALU.add), t1, t_vec)
        t_mod[which].append(td)

    def split_weights(parts, n):
        (wh, wl), before, free = WS.take()
        k0 = 0
        th, tl = [], []
        for chunk, col, K in parts:
            item = chunk.get()
            w = chunk.view(item.place)[:, :, col:col + n]
            h, l = wh[:, k0:k0 + K, 0:n], wl[:, k0:k0 + K, 0:n]
            t = act(lambda e, h=h, w=w: e.activation(h, w, ACT.Copy), item.ready, before)
            th.append(t)
            t = dve(lambda e, h=h, l=l, w=w: e.tensor_tensor(l, w, h.bitcast(F32), ALU.subtract),
                    item.ready, before, t)
            tl.append(t)
            item.done.append(t)
            k0 += K
        return wh, wl, k0, th, tl, free

    def linear(tiles, xh, xl, t_in, N, evac, hooks=None):
        hooks = list(hooks or [])
        n_hooks = len(hooks)
        nxt = split_weights(*tiles[0])
        for i, (_, n) in enumerate(tiles):
            h, l, K, th, tl, free_w = nxt
            if i + 1 < len(tiles):
                nxt = split_weights(*tiles[i + 1])
            bank, before, free = PS.take()

            def mms(e, ks, parts, h=h, l=l, K=K, n=n, bank=bank):
                for k in ks:
                    for wi, xi in parts:
                        w_, x_ = (h, l)[wi][:, k, 0:n], (xh, xl)[xi](k)
                        first = k == 0 and (wi, xi) == (0, 0)
                        final = k == K - 1 and wi == 1
                        last = e.matmul(bank[0:n, 0:N], w_, x_, start=first, stop=final)
                return last

            if i == 0:
                for k in range(K):
                    pe(lambda e, k=k, f=mms: f(e, [k], ((0, 0), (0, 1))), before, th, t_in[k])
            else:
                pe(lambda e, f=mms, K=K: f(e, range(K), ((0, 0), (0, 1))), before, th, t_in)
            tp = pe(lambda e, f=mms, K=K: f(e, range(K), ((1, 0),)), tl)
            free_w.append(tp)
            free.extend(evac(i, bank, tp))
            while n_hooks - len(hooks) < n_hooks * (i + 1) // len(tiles):
                hooks.pop(0)()

    def split_out(src, hi, lo, tok_, *waits):
        th = act(lambda e: e.activation(hi, src, ACT.Copy), tok_, *waits)
        tl = dve(lambda e: e.tensor_tensor(lo, src, hi.bitcast(F32), ALU.subtract), th, tok_, *waits)
        return th, tl

    def rstd(sums, mean, out, *waits):
        t = act(lambda e: e.activation(out, sums, ACT.Ln, bias=EB[:, 0:1], scale=mean), t_eb, *waits)
        return act(lambda e: e.activation(out, out, ACT.Exp, scale=-0.5), t)

    def adaln(N, t_src, scales, TB, hi, lo, t_free, keep=None):
        bank, before, free = PS.take()
        for k in range(KT):
            sq, bf, fr = TB.take()
            if k % 2:
                ts = act(lambda e, k=k, sq=sq: e.activation(sq[:, 0:N], XT[:, k, 0:N], ACT.Square), t_src[k], bf)
            else:
                ts = dve(lambda e, k=k, sq=sq: e.tensor_tensor(sq[:, 0:N], XT[:, k, 0:N], XT[:, k, 0:N], ALU.mult),
                         t_src[k], bf)
            tp = pe(lambda e, k=k, sq=sq, bank=bank: e.matmul(bank[:, 0:N], ONES[:, :], sq[:, 0:N],
                                                               start=(k == 0), stop=(k == KT - 1)), ts, before, t_ones)
            fr.append(tp)
        rb = tmp[7]
        tr = rstd(bank[:, 0:N], 1.0 / D, rb[:, 0:N], tp, t_free)
        free.append(tr)
        out = []
        for k in range(KT):
            t, bf, fr = TB.take()
            t1 = dve(lambda e, k=k, t=t: e.tensor_tensor(t[:, 0:N], XT[:, k, 0:N], rb[:, 0:N], ALU.mult), tr, bf)
            dst = t if keep is None else keep(k)
            for cols, s, b, tw in scales:
                t2 = act(lambda e, k=k, t=t, dst=dst, cols=cols, s=s, b=b: e.activation(
                    dst[:, cols[0]:cols[1]], t[:, cols[0]:cols[1]], ACT.Identity, bias=b(k), scale=s(k)),
                    t1, tw, t_free)
            if hi is None:
                fr.append(t2)
                out.append([t2])
                continue
            th, tl = split_out(dst[:, 0:N], hi(k), lo(k), t2, t_free)
            fr.append(tl)
            out.append([th, tl])
        return out

    n_st = [0]
    st_free = [[] for _ in range(16)]

    def stat():
        k = n_st[0] % 16
        n_st[0] += 1
        before, st_free[k] = st_free[k], []
        return ST[:, 3 * k:3 * k + 3], before, st_free[k]

    def attention(jobs, PB, PTB, pair_done):
        steps = [(h, a) for h in range(len(jobs)) for a in range(len(jobs[h]["nk"]))]
        state, head_pt, pair = {}, {}, {}

        def scores(h, a):
            J = jobs[h]
            n = 128 * J["nk"][a]
            bank, before, free = PS.take()
            tp = pe(lambda e: e.matmul(bank[:, 0:n], J["q"](a), J["k"](n), start=True, stop=True),
                    before, J["waits"])
            P, bf, fr = PB.take()
            st, sbf, sfr = stat()
            src = bank
            if J["mask"] is not None:
                tp = dve(lambda e: e.tensor_tensor(P[:, 0:n], bank[:, 0:n], J["mask"](a), ALU.add), tp, bf)
                free.append(tp)
                src = P
            tm = dve(lambda e: e.tensor_reduce(st[:, 0:1], src[:, 0:n], AX.X, ALU.max, negate=True), tp, sbf)
            te = act(lambda e: e.activation(P[:, 0:n], src[:, 0:n], ACT.Exp, bias=st[:, 0:1],
                                            accum_out=st[:, 1:2]), tm, bf, tp)
            if src is bank:
                free.append(te)
            tr = dve(lambda e: e.reciprocal(st[:, 2:3], st[:, 1:2]), te)
            tn = dve(lambda e: e.tensor_scalar(P[:, 0:n], P[:, 0:n], st[:, 2:3], None, ALU.mult), tr)
            sfr.append(tn)
            state[h, a] = (P, fr, tn)

        def turn(h, a):
            J = jobs[h]
            nk = J["nk"][a]
            P, fr, tn = state.pop((h, a))
            if a == 0:
                head_pt[h] = (*PTB.take(), [])
            PT, bf, ptfr, toks = head_pt[h]
            bank, before, free = PS.take()

            def tr(e):
                for j in range(nk):
                    last = e.transpose(bank[:, 128 * j:128 * j + 128], P[:, 128 * j:128 * j + 128], ident)
                return last
            tp = pe(tr, tn, before)
            fr.append(tp)
            tc = act(lambda e: e.activation(PT[:, 0:nk, 128 * a:128 * a + 128],
                                            bank[:, 0:128 * nk].rearrange("p (j n) -> p j n", n=128), ACT.Copy),
                     tp, bf)
            free.append(tc)
            toks.append(tc)

        def values(h):
            J = jobs[h]
            PT, bf, ptfr, toks = head_pt.pop(h)
            if h % 2 == 0:
                pair[0] = PS.take()
            bank, before, free = pair[0]
            nk = J["nk"]
            r = 64 * (h % 2)

            def pv(e):
                groups = [(0, 128 * len(nk), nk[0])] if len(set(nk)) == 1 else \
                    [(128 * a, 128 * a + 128, nk[a]) for a in range(len(nk))]
                for lo, hi, m in groups:
                    for j in range(m):
                        last = e.matmul(bank[r:r + 64, lo:hi], J["v"](j), PT[:, j, lo:hi],
                                        start=(j == 0), stop=(j == m - 1))
                return last
            tp = pe(pv, toks, before, J["waits"])
            ptfr.append(tp)
            if h % 2:
                free.extend(pair_done(h // 2, bank, tp))

        LAG = 2
        for i in range(len(steps) + LAG):
            if i < len(steps):
                scores(*steps[i])
            if i >= LAG:
                h, a = steps[i - LAG]
                turn(h, a)
                if a == len(jobs[h]["nk"]) - 1:
                    values(h)

    MH = lambda m, lo, hi: GH[:, m, lo:hi]
    ML = lambda m, lo, hi: GL[:, m, lo:hi]

    def head_norm(src, rows_n, gain, MT, dst, waits, mean=1.0 / 64, red=None, t_free=None):
        n = rows_n
        sq, bf, fr = MT.take()
        ts = act(lambda e: e.activation(sq[:, 0:n], src, ACT.Square), waits, bf)
        bank, before, free = PS.take()
        tp = pe(lambda e: e.matmul(bank[:, 0:n], bd if red is None else red, sq[:, 0:n], start=True, stop=True),
                ts, before)
        t2 = rstd(bank[:, 0:n], mean, sq[:, 0:n], tp)
        free.append(t2)
        t3 = dve(lambda e: e.scalar_tensor_tensor(dst, src, gain, sq[:, 0:n], ALU.mult, ALU.mult), t2, waits, t_free)
        fr.append(t3)
        return t3

    def rope_into(dst, straight, turned, cos, sin, MT, waits, t_free=None):
        a, bf, fr = MT.take()
        t1 = dve(lambda e: e.tensor_tensor(a[:, 0:256], turned, sin, ALU.mult), waits, bf)
        t2 = dve(lambda e: e.tensor_tensor(dst, straight, cos, ALU.mult), waits, t_free)
        t3 = dve(lambda e: e.tensor_tensor(dst, dst, a[:, 0:256], ALU.add), t1, t2)
        fr.append(t3)
        return t1, t3

    def fm(ap, k=8):
        return ap.rearrange("p (k n) -> p k n", k=k)

    def wide(src, c0, n):
        return Chunk(lambda: ring.load(wchunk(src, c0, n)), lambda place: fm(place[:, 0:8 * n]))

    for c in range(24):
        ada_use(*ada_load(0, c))

    ada_queue = [(w, c) for w in (1, 2) for c in range(24)]

    def layer(i, t_x, rdy_wp):
        both = i == 0
        N = 512 if both else 256
        streams = (0, 1) if both else (0,)
        tmp_free = fence()
        TB = Buffers(tmp[:7], tmp_free)
        t_sg = dve(lambda e: e.scalar_tensor_tensor(
            SG[:, :, :], MOD[:, i, 8:16, 0:2], 1.0,
            VEC[:, V_GMIX + 8 * i:V_GMIX + 8 * i + 8].unsqueeze(2).to_broadcast([128, 8, 2]),
            ALU.add, ALU.mult), t_mod[i], t_vec, tmp_free)
        scales = [((256 * s, 256 * s + 256), lambda k, s=s: SG[:, k, s:s + 1], lambda k, s=s: MOD[:, i, k, s:s + 1], t_sg)
                  for s in (0, 1)]
        t_h = adaln(512, t_x, scales, TB, lambda k: HH[:, k, :], lambda k: HL[:, k, :], tmp_free)
        zfree = fence()
        chunks = [wide(A["w_in"][i], 256 * c, 256) for c in range(5)]

        def tile_of(m):
            return [(chunks[m // 2], 128 * (m % 2), 8)], 128

        t_q, t_k, t_z = [None] * 4, [None], []

        def evac(j, bank, tp):
            if j < 4:
                t_q[j] = act(lambda e: e.activation(QT[:, j, 0:N], bank[:, 0:N], ACT.Copy), tp, zfree)
                return [t_q[j]]
            t_k[0] = act(lambda e: e.activation(KTr[:, :], bank[:, :], ACT.Copy), tp, zfree)
            return [t_k[0]]

        xh, xl = lambda k: HH[:, k, 0:N], lambda k: HL[:, k, 0:N]
        linear([tile_of(m) for m in range(4)], xh, xl, t_h, N, evac)
        xh, xl = lambda k: HH[:, k, :], lambda k: HL[:, k, :]

        ZT = Buffers(zt, zfree)

        def evac_z(j, bank, tp, nt):
            t, bf, fr = ZT.take()
            tc = act(lambda e: e.activation(t[:, 0:128 * nt], bank[:, 0:128 * nt], ACT.Copy), tp, bf)
            bank2, before, free2 = PS.take()

            def tr(e):
                for a in range(nt):
                    last = e.transpose(bank2[:, 128 * a:128 * a + 128], t[:, 128 * a:128 * a + 128], ident)
                return last
            tt = pe(tr, tc, before)
            fr.append(tt)
            td = dve(lambda e: e.tensor_copy(Z[:, 0:nt, 128 * j:128 * j + 128],
                                             bank2[:, 0:128 * nt].rearrange("p (a n) -> p a n", n=128)), tt, zfree)
            free2.append(td)
            t_z.append(td)
            return [tc]
        nt = 4 if both else 2
        linear([tile_of(m) for m in (4, 5)], xh, xl, t_h, 512,
               lambda j, b, tp: evac_z(0, b, tp, 4) if j else evac(4, b, tp))
        xh, xl = lambda k: HH[:, k, 0:N], lambda k: HL[:, k, 0:N]
        linear([tile_of(m) for m in range(6, 10)], xh, xl, t_h, N,
               lambda j, b, tp: evac_z(j + 1, b, tp, nt))
        hfree = fence()
        MT, PB, PTB = Buffers(mt, hfree), Buffers(pbuf, hfree), Buffers(ptbuf, hfree)
        const = [ring.load(lambda e, place, sem, nm=nm, n=n: e.dma_start(place[:, 0:n], A[nm]).then_inc(sem, 16))
                 for nm, n in (("k_pool", 2048), ("k_mix", K_END))]
        kp, kc = const[0].place, const[1].place
        qg = VEC[:, V_QG + i:V_QG + i + 1]
        kg = VEC[:, V_KG + i:V_KG + i + 1]
        mfree = hfree
        t_kn = head_norm(KTr[:, :], 512, kg, MT, KTr[:, :], t_k[0])
        t_kd = []
        for g in range(2):
            bank, before, free = PS.take()
            tp = pe(lambda e, g=g, bank=bank: e.matmul(bank[:, :], kc[:, K_D + 128 * g:K_D + 128 * g + 128],
                                                       KTr[:, :], start=True, stop=True), t_kn, before, const[0].ready, const[1].ready)
            bank2, before, free2 = PS.take()
            tp2 = pe(lambda e, g=g, bank2=bank2: e.matmul(bank2[:, 0:256], kc[:, K_RD + 128 * g:K_RD + 128 * g + 128],
                                                          KTr[:, 0:256], start=True, stop=True), before)
            t0 = act(lambda e, g=g, bank=bank: e.activation(KD[:, g, 256:512], bank[:, 256:512], ACT.Copy), tp, hfree)
            t1, t3 = rope_into(KD[:, g, 0:256], bank[:, 0:256], bank2[:, 0:256], cos1, sin1, MT, [tp2, t0], hfree)
            free.extend([t0, t3])
            free2.append(t1)
            t_kd += [t0, t3]
        t_qr = [[], []]
        for m in range(4):
            tn = head_norm(QT[:, m, 0:N], N, qg, MT, QT[:, m, 0:N], [t_q[m], t_qg])
            bank, before, free = PS.take()
            tp = pe(lambda e, m=m, bank=bank: e.matmul(bank[:, 0:256], kc[:, K_R1:K_R1 + 128], QT[:, m, 0:256],
                                                       start=True, stop=True), tn, before)
            t1, t3 = rope_into(QR[:, m, 0:256], QT[:, m, 0:256], bank[:, 0:256], cos1, sin1, MT, [tp, tn], hfree)
            free.append(t1)
            t_qr[0].append(t3)
            t_qr[1].append(tn)
        t_m = [[] for _ in range(8)]

        def out_split(bank, m, lo, tp, scale=None):
            t, bf, fr = MT.take()
            if scale is None:
                tc = dve(lambda e: e.tensor_copy(t[:, 0:256], bank[:, 0:256]), tp, bf)
            else:
                tc = dve(lambda e: e.tensor_scalar(t[:, 0:256], bank[:, 0:256], scale, None, ALU.mult), tp, bf)
            th, tl = split_out(t[:, 0:256], MH(m, lo, lo + 256), ML(m, lo, lo + 256), tc, mfree)
            fr.append(tl)
            t_m[m] += [th, tl]
            return [tc]

        for s in streams:
            src = QR if s == 0 else QT
            jobs = []
            for h in range(8):
                r, m, g = 64 * (h % 2), h // 2, h // 4
                k0 = 0 if s == 0 else 256
                jobs.append({
                    "q": lambda a, r=r, m=m, s=s, src=src: src[r:r + 64, m, 256 * s + 128 * a:256 * s + 128 * a + 128],
                    "k": lambda n, r=r, g=g, k0=k0: KD[r:r + 64, g, k0:k0 + n],
                    "v": lambda j, g=g, s=s: Z[:, 2 * s + j, 64 * g:64 * g + 64],
                    "nk": [4, 4] if s == 0 else [2, 2], "mask": None,
                    "waits": [t_kd, t_qr[s][m], t_z[0]],
                })
            attention(jobs, PB, PTB, lambda p, bank, tp, s=s: out_split(bank, p, 256 * s, tp))
        for s in streams:
            for j in range(2):
                bank, before, free = PS.take()

                def mm(e, s=s, j=j, bank=bank):
                    for a in range(2):
                        for t in range(2):
                            c = 128 + 128 * j + 64 * a
                            p = K_POOL + 1024 * t + 256 * (2 * j + a)
                            last = e.matmul(bank[64 * a:64 * a + 64, 0:256], Z[:, 2 * s + t, c:c + 64],
                                            kp[:, p:p + 256], start=(t == 0), stop=(t == 1))
                    return last
                tp = pe(mm, t_z, before, const[0].ready, const[1].ready)
                d, bf, fr = MT.take()
                tc = act(lambda e, d=d, bank=bank: e.activation(d[:, 0:256], bank[:, 0:256], ACT.Copy), tp, bf)
                free.append(tc)
                bank, before, free = PS.take()
                tp = pe(lambda e, j=j, d=d, bank=bank: e.matmul(bank[:, 0:256], WPF[:, j, :], d[:, 0:256],
                                                                start=True, stop=True), tc, before, rdy_wp)
                fr.append(tp)
                free.extend(out_split(bank, 4 + j, 256 * s, tp, VEC[:, V_PS + 2 * i + j:V_PS + 2 * i + j + 1]))
            for j in range(2):
                bank, before, free = PS.take()

                def mm(e, s=s, j=j, bank=bank):
                    for t in range(2):
                        last = e.matmul(bank[:, :], Z[:, 2 * s + t, 384 + 128 * j:512 + 128 * j],
                                        kc[:, K_DFT + 512 * t:K_DFT + 512 * t + 512], start=(t == 0), stop=(t == 1))
                    return last
                tp = pe(mm, t_z, before, const[0].ready, const[1].ready)
                d, bf, fr = MT.take()
                tc = act(lambda e, d=d, bank=bank: e.activation(d[:, :], bank[:, :], ACT.Copy), tp, bf)
                free.append(tc)
                bank, before, free = PS.take()

                def mm(e, d=d, bank=bank):
                    e.matmul(bank[:, 0:256], kc[:, K_CD:K_SD], d[:, 0:256], start=True, stop=False)
                    return e.matmul(bank[:, 0:256], kc[:, K_SD:K_END], d[:, 256:512], start=False, stop=True)
                tp = pe(mm, tc, before)
                fr.append(tp)
                d, bf, fr = MT.take()
                tc = act(lambda e, d=d, bank=bank: e.activation(d[:, 0:256], bank[:, 0:256], ACT.Copy), tp, bf)
                free.append(tc)
                bank, before, free = PS.take()
                tp = pe(lambda e, j=j, d=d, bank=bank: e.matmul(bank[:, 0:256], WPF[:, 2 + j, :], d[:, 0:256],
                                                                start=True, stop=True), tc, before, rdy_wp)
                fr.append(tp)
                free.extend(out_split(bank, 6 + j, 256 * s, tp))
        for item in const:
            item.done.append(pe.last())
        t_mixers = fence()
        rdy_wp = load_mixer_weights(1, [pe.last()]) if both else None
        chunks_o = [wide(A["w_out"][i], 256 * c, 256) for c in range(4)]

        def residual(gate):
            def f(j, bank, tp):
                out = []
                for s in streams:
                    sl = slice(256 * s, 256 * s + 256)
                    out.append(dve(lambda e, sl=sl, s=s: e.scalar_tensor_tensor(
                        XT[:, j, sl], bank[:, sl], MOD[:, i, gate + j, s:s + 1], XT[:, j, sl], ALU.mult, ALU.add),
                        tp, t_xw[j]))
                t_xw[j] = out
                return out
            return f

        t_xw = [[t, fence()] for t in t_x]
        tiles = [([(chunks_o[m // 2], 128 * (m % 2), 8)], 128) for m in range(8)]
        linear(tiles, lambda k: GH[:, k, 0:N], lambda k: GL[:, k, 0:N], t_m, N, residual(16))
        TB = Buffers(tmp[:7], t_mixers)
        t_sg2 = dve(lambda e: e.scalar_tensor_tensor(
            SG[:, :, :], MOD[:, i, 32:40, 0:2], 1.0,
            VEC[:, V_GFFN + 8 * i:V_GFFN + 8 * i + 8].unsqueeze(2).to_broadcast([128, 8, 2]),
            ALU.add, ALU.mult), t_mod[i], t_mixers)
        scales = [((256 * s, 256 * s + 256), lambda k, s=s: SG[:, k, s:s + 1],
                   lambda k, s=s: MOD[:, i, 24 + k, s:s + 1], t_sg2) for s in streams]
        t_h = adaln(N, t_xw, scales, TB, lambda k: HH[:, k, 0:N], lambda k: HL[:, k, 0:N], t_mixers)
        xh, xl = lambda k: HH[:, k, 0:N], lambda k: HL[:, k, 0:N]
        g_free = fence()
        for half in range(2):
            items = []
            for c in range(0, 1408, 256):
                n = min(256, 1408 - c)
                gate = wide(A["w_gate_up"][i], 1408 * half + c, n)
                up = wide(A["w_gate_up"][i], 2816 + 1408 * half + c, n)
                for j in range(n // 128):
                    items += [([(gate, 128 * j, 8)], 128), ([(up, 128 * j, 8)], 128)]
            t_g = [[] for _ in range(HALF)]
            held = {}

            def evac(j, bank, tp):
                m = j // 2
                if j % 2 == 0:
                    t, bf, fr = TB.take()
                    ts = act(lambda e: e.activation(t[:, 0:N], bank[:, 0:N], ACT.Silu), tp, bf)
                    held[m] = (t, fr, ts)
                    return [ts]
                t, fr, ts = held.pop(m)
                t2 = dve(lambda e: e.tensor_tensor(t[:, 0:N], bank[:, 0:N], t[:, 0:N], ALU.mult), tp, ts)
                th, tl = split_out(t[:, 0:N], GH[:, m, 0:N], GL[:, m, 0:N], t2, g_free)
                fr.append(tl)
                t_g[m] += [th, tl]
                return [t2]
            hooks = []
            if both and half == 0:
                for fr in AB.free:
                    fr.append(t_mixers)
            if both:
                for _ in range(24):
                    w, c = ada_queue.pop(0)
                    hooks.append(lambda w=w, c=c: ada_use(*ada_load(w, c)))
            linear(items, xh, xl, t_h, N, evac, hooks)
            downs = []
            vd = A["w_down"][i].rearrange("(k p) n -> p k n", p=128)
            for c in range(4):
                pair = []
                for k0, kn in ((0, 6), (6, 5)):
                    def fill(e, place, sem, c=c, k0=k0, kn=kn, half=half):
                        e.dma_start(place[:, 0:kn * 256].rearrange("p (k n) -> p k n", k=kn),
                                    vd[:, HALF * half + k0:HALF * half + k0 + kn, 256 * c:256 * c + 256])\
                            .then_inc(sem, 16)
                    pair.append((Chunk(lambda fill=fill: ring.load(fill),
                                       lambda place, kn=kn: fm(place[:, 0:kn * 256], kn)), kn))
                downs += [([(ck, 128 * j, kn) for ck, kn in pair], 128) for j in range(2)]
            linear(downs, lambda k: GH[:, k, 0:N], lambda k: GL[:, k, 0:N], t_g, N, residual(40))
            g_free = fence()
        return t_xw, rdy_wp

    def second(t_x):
        N = 256
        V2 = 2
        M2H = at("M2H", [128, 8, 256], F32R, oG)
        M2L = at("M2L", [128, 8, 256], F32R, oG + 8 * KB)
        o = oG + 16 * KB
        QKM = at("QKM", [128, 8, 259], F32, o)
        QK2 = at("QK2", [128, 8, 256], F32, o + 8320)
        TWO = at("TWO", [128, B_END], F32, o + 16512)
        CS2 = at("CS2", [128, 2, 256], F32, o + 19616)
        GI = at("GI", [4, 256], F32, o + 21664)
        GF = at("GF", [4, 256], F32, o + 22688)
        BG = at("BG", [4, 2], F32, o + 23712)
        SEL = at("SEL", [4, 4, 128], F32, o + 23744)
        QA = at("QA", [128, 4, 256], F32, oZ)
        KA = at("KA", [128, 4, 256], F32, oZ + 4 * KB)
        VA = at("VA", [128, 2, 512], F32, oZ + 8 * KB)
        VM = at("VM", [128, 2, 512], F32, oZ + 12 * KB)
        OM = at("OM", [128, 4, 256], F32, oZ + 16 * KB)
        start = fence()
        s_two = nc.alloc_semaphore("s_two")
        pool.raw(lambda e: e.dma_start(TWO[:, :], A["k_two"]).then_inc(s_two, 16), start)
        for j in range(2):
            pool.raw(lambda e, j=j: e.dma_start(
                BG[:, j:j + 1], A["b_gate_2"][0][4 * j:4 * j + 4].rearrange("(h o) -> h o", o=1)).then_inc(s_two, 16),
                start)
        POSI = at("POSI", [128, 256], I32, o + 8320 + 7168)
        pool.raw(lambda e: e.dma_start(POSI[:, :], A["positions_2"][0].partition_broadcast(128)).then_inc(s_two, 16),
                 start)
        r_two = (s_two, 64)
        ang, nn, rr, rc, mk = (QK2[:, j, :] for j in range(5))
        t = dve(lambda e: e.tensor_copy(ang, POSI[:, :]), r_two, start)
        t = dve(lambda e: e.tensor_scalar(ang, ang, TWO[:, B_FREQ:B_FREQ + 1], None, ALU.mult), t)
        t = dve(lambda e: e.tensor_scalar(nn, ang, float(1 / (2 * np.pi)), 12582912.0, ALU.mult, ALU.add), t)
        t = dve(lambda e: e.tensor_scalar(nn, nn, 12582912.0, None, ALU.subtract), t)
        c1 = 6.28125
        c2 = float(np.float32(np.round((2 * np.pi - c1) * 2 ** 20) / 2 ** 20))
        c3 = float(2 * np.pi - c1 - c2)
        src = ang
        for c in (c1, c2, c3):
            t = dve(lambda e, c=c, src=src: e.scalar_tensor_tensor(rr, nn, -c, src, ALU.mult, ALU.add), t)
            src = rr
        LIM = 3.1415925
        t = dve(lambda e: e.tensor_scalar(rr, rr, LIM, -LIM, ALU.min, ALU.max), t)
        t_sin = act(lambda e: e.activation(CS2[:, 1, :], rr, ACT.Sin), t, start)
        t = dve(lambda e: e.tensor_scalar(rc, rr, float(np.pi / 2), None, ALU.add), t)
        t = dve(lambda e: e.tensor_scalar(mk, rc, float(np.pi), float(-2 * np.pi), ALU.is_gt, ALU.mult), t)
        t = dve(lambda e: e.tensor_tensor(rc, rc, mk, ALU.add), t)
        t = dve(lambda e: e.tensor_scalar(rc, rc, LIM, -LIM, ALU.min, ALU.max), t)
        t_cs = act(lambda e: e.activation(CS2[:, 0, :], rc, ACT.Sin), t)
        t_pad = dve(lambda e: e.memset(QKM[:, :, 0:3], 0.0), start)
        t_sel = [dve(lambda e, h=h: e.tensor_scalar(SEL[:, h, :], ONES[0:4, :], ident[0:4, h:h + 1], None, ALU.mult),
                     start, t_ones, (s_res, 16)) for h in range(4)]
        TB = Buffers(tmp[:7], start)
        t_sg = dve(lambda e: e.scalar_tensor_tensor(
            SG[:, :, 0], MOD[:, 2, 8:16, V2], 1.0, VEC[:, V_N1:V_N1 + 8], ALU.add, ALU.mult), t_mod[2], t_vec, start)
        scales = [((0, 256), lambda k: SG[:, k, 0:1], lambda k: MOD[:, 2, k, V2:V2 + 1], t_sg)]
        xh, xl = lambda k: HH[:, k, 0:N], lambda k: HL[:, k, 0:N]
        t_h = adaln(N, t_x, scales, TB, xh, xl, start)
        zfree = fence()
        chunks = [wide(A["w_in_2"][0], 256 * c, min(256, 3592 - 256 * c)) for c in range(15)]
        tiles = [([(chunks[m // 2], 128 * (m % 2), 8)], 128) for m in range(28)]
        tiles += [([(chunks[14], 4 * j, 8)], 4) for j in range(2)]
        t_qa, t_ka, t_va, t_qk, t_vm, t_om, t_g = ([] for _ in range(7))
        zt2 = [at(f"ZU{j}", [128, 256], F32, oG + KB * j) for j in range(3)]
        ZT = Buffers(zt2, start)

        def rows_of(bank, tp, dst, m, toks):
            tb, bf, fr = ZT.take()
            tc = act(lambda e: e.activation(tb[:, :], bank[:, 0:256], ACT.Copy), tp, bf)
            bank2, before, free2 = PS.take()

            def tr(e):
                for a in range(2):
                    last = e.transpose(bank2[:, 128 * a:128 * a + 128], tb[:, 128 * a:128 * a + 128], ident)
                return last
            tt = pe(tr, tc, before)
            fr.append(tt)
            td = dve(lambda e: e.tensor_copy(dst[:, :, 128 * m:128 * m + 128],
                                             bank2[:, 0:256].rearrange("p (a n) -> p a n", n=128)), tt, zfree)
            free2.append(td)
            toks.append(td)
            return [tc]

        def conv(j, tq):
            out = QK2[:, j, :]
            w = [VEC[:, V_CW + 8 * t + j:V_CW + 8 * t + j + 1] for t in range(4)]
            t1 = dve(lambda e: e.tensor_scalar(out, QKM[:, j, 0:256], w[0], VEC[:, V_CB + j:V_CB + j + 1],
                                               ALU.mult, ALU.add), tq, t_pad, t_cs, t_sin)
            for i in range(1, 4):
                t1 = dve(lambda e, i=i: e.scalar_tensor_tensor(out, QKM[:, j, i:i + 256], w[i], out,
                                                               ALU.mult, ALU.add), t1)
            t1 = act(lambda e: e.activation(out, out, ACT.Silu), t1)
            if j >= 4:
                t1 = dve(lambda e: e.tensor_scalar(out, out, float(128 ** -0.5), None, ALU.mult), t1)
            t_qk.append(t1)

        def evac(i, bank, tp):
            if i < 4:
                t1 = act(lambda e: e.activation(QA[:, i, :], bank[:, 0:256], ACT.Copy, scale=0.125), tp, zfree)
                t_qa.append(t1)
            elif i < 8:
                t1 = act(lambda e: e.activation(KA[:, i - 4, :], bank[:, 0:256], ACT.Copy), tp, zfree)
                t_ka.append(t1)
            elif i < 12:
                return rows_of(bank, tp, VA, i - 8, t_va)
            elif i < 20:
                t1 = dve(lambda e: e.tensor_copy(QKM[:, i - 12, 3:259], bank[:, 0:256]), tp, start)
                conv(i - 12, t1)
            elif i < 24:
                return rows_of(bank, tp, VM, i - 20, t_vm)
            elif i < 28:
                t1 = act(lambda e: e.activation(OM[:, i - 24, :], bank[:, 0:256], ACT.Sigmoid), tp, zfree)
                t_om.append(t1)
            else:
                dst = (GI, GF)[i - 28]
                t1 = dve(lambda e: e.tensor_scalar(dst[:, :], bank[0:4, 0:256], BG[:, i - 28:i - 27], None, ALU.add),
                         tp, r_two)
                t_g.append(t1)
            return [t1]
        linear(tiles, xh, xl, t_h, N, evac)
        hfree = fence()
        MT, PB, PTB = Buffers(mt, hfree), Buffers(pbuf, hfree), Buffers(ptbuf, hfree)
        QRB = at("QRB", [128, 4, 256], F32, oH)
        KRB = at("KRB", [128, 4, 256], F32, oH + 4 * KB)
        t_r = []
        for m in range(4):
            pair = []
            for src, dst, tq in ((QA, QRB, t_qa[m]), (KA, KRB, t_ka[m])):
                bank, before, free = PS.take()
                tp = pe(lambda e, src=src, m=m, bank=bank: e.matmul(
                    bank[:, 0:256], TWO[:, B_R2:B_R2 + 128], src[:, m, :], start=True, stop=True), tq, before, r_two)
                t1, t3 = rope_into(dst[:, m, :], src[:, m, :], bank[:, 0:256], CS2[:, 0, :], CS2[:, 1, :], MT,
                                   [tp, t_cs, t_sin], hfree)
                free.append(t1)
                pair.append(t3)
            t_r.append(pair)
        t_m = [[] for _ in range(8)]

        def gated_out(t, m, t3, fr, gate=None):
            if gate is not None:
                t3 = dve(lambda e: e.tensor_tensor(t[:, 0:256], t[:, 0:256], gate, ALU.mult), t3, t_om)
            th, tl = split_out(t[:, 0:256], M2H[:, m, :], M2L[:, m, :], t3, hfree)
            fr.append(tl)
            t_m[m] += [th, tl]

        def pair_done(p, bank, tp):
            t, bf, fr = MT.take()
            tc = act(lambda e: e.activation(t[:, 0:256], bank[:, 0:256], ACT.Copy), tp, bf)
            t3 = head_norm(t[:, 0:256], 256, VEC[:, V_AG + p:V_AG + p + 1], MT, t[:, 0:256], tc)
            gated_out(t, p, t3, fr)
            return [tc]

        jobs = [{
            "q": lambda a, r=64 * (h % 2), m=h // 2: QRB[r:r + 64, m, 128 * a:128 * a + 128],
            "k": lambda n, r=64 * (h % 2), m=h // 2: KRB[r:r + 64, m, 0:n],
            "v": lambda j, h=h: VA[:, j, 64 * h:64 * h + 64],
            "nk": [1, 2],
            "mask": lambda a: TWO[:, B_TRI + 128 * (1 - a):B_TRI + 256],
            "waits": [t_r[h // 2], t_va],
        } for h in range(8)]
        attention(jobs, PB, PTB, pair_done)
        lfree = fence()
        G4 = at("G4", [4, 8, 256], F32, oH)
        ab, lf, cum, bb, mm_, em, wi, nm = (G4[:, j, :] for j in range(8))
        BC = at("BC", [128, 2, 4], F32, oH + 8 * KB)
        S1 = at("S1", [4, 1], F32, oH + 8 * KB + 64)
        names = ("WT", "QW", "KW", "SWt", "DN")
        WT, QW, KW, SWt, DN = (at(nm_, [128, 4, 256], F32, oH + 9 * KB + 4 * KB * j) for j, nm_ in enumerate(names))
        CNa = at("CNa", [128, 256], F32, oH + 29 * KB)
        CNb = at("CNb", [128, 256], F32, oH + 30 * KB)
        CN = Buffers([CNa, CNb], lfree)
        ones4 = ONES[0:4, 0:128]
        t1 = act(lambda e: e.activation(ab, GF[:, :], ACT.Abs), t_g, lfree)
        t1 = act(lambda e: e.activation(ab, ab, ACT.Exp, scale=-1.0), t1)
        t1 = act(lambda e: e.activation(ab, ab, ACT.Ln, bias=ONES[0:4, 0:1]), t1)
        t1 = dve(lambda e: e.scalar_tensor_tensor(lf, GF[:, :], 0.0, ab, ALU.min, ALU.subtract), t1, t_g)
        ts = [dve(lambda e, c=c: e.tensor_tensor_scan(cum[:, 128 * c:128 * c + 128], ones4,
                                                      lf[:, 128 * c:128 * c + 128], 0.0, ALU.mult, ALU.add), t1)
              for c in range(2)]
        tb_ = dve(lambda e: e.tensor_tensor(bb, GI[:, :], cum, ALU.subtract), ts, t_g)
        t2 = dve(lambda e: e.tensor_tensor_scan(mm_[:, 0:128], bb[:, 0:128], bb[:, 0:128], 0.0, ALU.max, ALU.max), tb_)
        tm0 = dve(lambda e: e.tensor_tensor(S1[:, :], cum[:, 127:128], mm_[:, 127:128], ALU.add), t2)
        t3 = dve(lambda e: e.tensor_tensor_scan(mm_[:, 128:256], bb[:, 128:256], bb[:, 128:256], S1[:, 0:1],
                                                ALU.max, ALU.max), tm0)
        tn_ = dve(lambda e: e.tensor_scalar(nm, mm_, -1.0, None, ALU.mult), t3)
        te = dve(lambda e: e.tensor_tensor(em, cum, mm_, ALU.add), t3)
        te = act(lambda e: e.activation(em, em, ACT.Exp, scale=-1.0), te)
        tw = act(lambda e: e.activation(wi[:, 0:128], mm_[:, 128:256], ACT.Exp, bias=S1[:, 0:1], scale=-1.0), t3)
        bank, before, free = PS.take()

        def tr(e, bank=bank):
            for c in range(2):
                last = e.transpose(bank[:, 4 * c:4 * c + 4], bb[:, 128 * c:128 * c + 128], ident[0:4, 0:4])
            return last
        tp = pe(tr, tb_, before)
        t_bc = dve(lambda e, bank=bank: e.tensor_copy(BC[:, :, :], bank[:, 0:8].rearrange("p (c h) -> p c h", c=2)),
                   tp, lfree)
        free.append(t_bc)
        t_wt, t_qw, t_kw = [], [], []
        for h in range(4):
            bank, before, free = PS.take()
            tp = pe(lambda e, h=h, bank=bank: e.matmul(bank[:, 0:256], SEL[:, h, :], nm, start=True, stop=True),
                    tn_, t_sel, before)
            t1 = dve(lambda e, h=h, bank=bank: e.tensor_tensor(
                WT[:, h, :].rearrange("p (c n) -> p c n", c=2), bank[:, 0:256].rearrange("p (c n) -> p c n", c=2),
                TWO[:, B_TRIT:B_TRIT + 128].unsqueeze(1).to_broadcast([128, 2, 128]), ALU.add), tp, lfree)
            free.append(t1)
            w2_ = [act(lambda e, h=h, c=c: e.activation(WT[:, h, 128 * c:128 * c + 128], WT[:, h, 128 * c:128 * c + 128],
                                                        ACT.Exp, bias=BC[:, c, h:h + 1]), t1, t_bc) for c in range(2)]
            t_wt.append(w2_)
            bank, before, free = PS.take()
            tp = pe(lambda e, h=h, bank=bank: e.matmul(bank[:, 0:128], SEL[:, h, :], wi[:, 0:128],
                                                       start=True, stop=True), tw, before)
            t1 = dve(lambda e, h=h, bank=bank: e.tensor_tensor(QW[:, h, 0:128], QK2[:, h, 128:256], bank[:, 0:128],
                                                               ALU.mult), tp, t_qk, lfree)
            free.append(t1)
            t_qw.append(t1)
            bank, before, free = PS.take()
            tp = pe(lambda e, h=h, bank=bank: e.transpose(bank[:, 0:128], QK2[:, 4 + h, 0:128], ident), t_qk, before)
            t1 = dve(lambda e, h=h, bank=bank: e.tensor_scalar(KW[:, h, 0:128], bank[:, 0:128], WT[:, h, 127:128], None,
                                                               ALU.mult), tp, w2_, lfree)
            free.append(t1)
            t_kw.append(t1)
        for h in range(4):
            bank, before, free = PS.take()

            def st_mm(e, h=h, bank=bank):
                e.matmul(bank[:, 0:128], KW[:, h, 0:128], VM[:, 0, 128 * h:128 * h + 128], start=True, stop=True)
                return e.matmul(bank[:, 128:256], KW[:, h, 0:128], ONES[:, :], start=True, stop=True)
            tp = pe(st_mm, t_kw[h], t_vm, before)
            cn, bf, fr_cn = CN.take()
            t_cn = act(lambda e, cn=cn, bank=bank: e.activation(cn[:, :], bank[:, 0:256], ACT.Copy), tp, bf)
            free.append(t_cn)
            bank, before, free = PS.take()

            def s_mm(e, h=h, bank=bank):
                for c in range(2):
                    sl = slice(128 * c, 128 * c + 128)
                    last = e.matmul(bank[:, sl], QK2[:, 4 + h, sl], QK2[:, h, sl], start=True, stop=True)
                return last
            tp = pe(s_mm, t_qk, before)
            t_s = dve(lambda e, h=h, bank=bank: e.tensor_tensor(SWt[:, h, :], bank[:, 0:256], WT[:, h, :], ALU.mult),
                      tp, t_wt[h], lfree)
            free.append(t_s)
            bn, before, free_n = PS.take()
            bd_, before2, free_d = PS.take()

            def n_mm(e, h=h, bn=bn, bd_=bd_, cn=cn):
                for bk, lhs, st_ in ((bn, lambda c: VM[:, c, 128 * h:128 * h + 128], cn[:, 0:128]),
                                     (bd_, lambda c: ONES[:, :], cn[:, 128:256])):
                    e.matmul(bk[:, 0:128], lhs(0), SWt[:, h, 0:128], start=True, stop=True)
                    e.matmul(bk[:, 128:256], lhs(1), SWt[:, h, 128:256], start=True, stop=False)
                    last = e.matmul(bk[:, 128:256], st_, QW[:, h, 0:128], start=False, stop=True)
                return last
            tp = pe(n_mm, t_s, t_cn, t_qw[h], t_vm, before, before2)
            fr_cn.append(tp)
            be, before, free_e = PS.take()
            tpe = pe(lambda e, h=h, be=be: e.matmul(be[:, 0:256], SEL[:, h, :], em, start=True, stop=True), te, before)
            d = DN[:, h, :]
            t1 = act(lambda e, d=d, bd_=bd_: e.activation(d, bd_[:, 0:256], ACT.Abs), tp, lfree)
            free_d.append(t1)
            t1 = dve(lambda e, d=d, be=be: e.tensor_tensor(d, be[:, 0:256], d, ALU.max), t1, tpe)
            free_e.append(t1)
            t1 = dve(lambda e, d=d: e.reciprocal(d, d), t1)
            t1 = dve(lambda e, d=d, bn=bn: e.tensor_tensor(d, bn[:, 0:256], d, ALU.mult), t1, tp)
            free_n.append(t1)
            sq = Buffers([SWt[:, h, :]], [tp])
            t3 = head_norm(d, 256, VEC[:, V_MG + h:V_MG + h + 1], sq, d, t1, mean=1.0 / 128, red=ONES[:, :])
            gated_out(DN[:, h, :], 4 + h, t3, [], gate=OM[:, h, :])
        t_xw = [[t, fence()] for t in t_x]

        def residual2(i, bank, tp):
            t1 = dve(lambda e: e.scalar_tensor_tensor(XT[:, i, 0:256], bank[:, 0:256], MOD[:, 2, 16 + i, V2:V2 + 1],
                                                      XT[:, i, 0:256], ALU.mult, ALU.add), tp, t_xw[i])
            t_xw[i] = [t1]
            return [t1]
        chunks_o = [wide(A["w_out_2"][0], 256 * c, 256) for c in range(4)]
        linear([([(chunks_o[m // 2], 128 * (m % 2), 8)], 128) for m in range(8)],
               lambda k: M2H[:, k, :], lambda k: M2L[:, k, :], t_m, N, residual2)
        t_dense = fence()
        H2 = at("H2", [128, 8, 256], F32, o)
        WR = at("WR", [128, 8, 36], F32, oZ + 16 * KB)
        RB = at("RB", [128, 36], F32, oZ + 16 * KB + 1152)
        s_wr = nc.alloc_semaphore("s_wr")
        for c0, n, wn, bn_ in ((0, 4, "w_rg_2", "b_rg_2"), (4, 32, "w_re_2", "b_re_2")):
            pool.raw(lambda e, c0=c0, n=n, wn=wn: e.dma_start(
                WR[:, :, c0:c0 + n], A[wn][0].rearrange("(k p) n -> p k n", p=128)).then_inc(s_wr, 16), lfree, t_m[7])
            pool.raw(lambda e, c0=c0, n=n, bn_=bn_: e.dma_start(
                RB[:, c0:c0 + n], A[bn_][0].partition_broadcast(128)).then_inc(s_wr, 16))
        TB = Buffers(tmp[:7], t_dense)
        t_sg = dve(lambda e: e.scalar_tensor_tensor(
            SG[:, :, 0], MOD[:, 2, 32:40, V2], 1.0, VEC[:, V_N2:V_N2 + 8], ALU.add, ALU.mult), t_dense)
        scales = [((0, 256), lambda k: SG[:, k, 0:1], lambda k: MOD[:, 2, 24 + k, V2:V2 + 1], t_sg)]
        t_h2 = adaln(N, t_xw, scales, TB, None, None, t_dense, keep=lambda k: H2[:, k, :])
        rfree = fence()
        rt = at("RT", [128, 1800], F32, oZ)
        off = [0]

        def small(*shape):
            n = int(np.prod(shape))
            ap = rt[:, off[0]:off[0] + n]
            off[0] += n
            if len(shape) == 2:
                ap = ap.rearrange("p (a b) -> p a b", a=shape[0])
            elif len(shape) == 3:
                ap = ap.rearrange("p (a b c) -> p a b c", a=shape[0], b=shape[1])
            return ap
        LG, G8, MX, MXE = small(2, 36), small(2, 8), small(2, 8), small(2, 8)
        IX, IXE = small(2, 8), small(2, 8)
        EG, GW, GIF, OG, EP, E8 = small(2, 4), small(2), small(2), small(2, 4), small(2, 32), small(2, 8)
        R1, RD, WGT, IDF = small(2), small(2), small(2, 2), small(2, 2)
        AA, A01, PR, PC = small(4, 32), small(2, 32), small(4, 32), small(96)
        PP, S0, S1b, BIG, GS = small(4), small(4), small(4), small(4), small(4)
        IND, XI, BS, TJ, EIA = small(32), small(32), small(2, 32), small(32), small(8)
        GB, iota2 = small(4, N_BLOCKS), small(128)
        INTS = at("INTS", [128, 16], I32, oZ + 7424)
        bank, before, free = PS.take()

        def lg(e, bank=bank):
            for a in range(2):
                for k in range(KT):
                    last = e.matmul(bank[:, 36 * a:36 * a + 36], H2[:, k, 128 * a:128 * a + 128], WR[:, k, :],
                                    start=(k == 0), stop=(k == KT - 1))
            return last
        tp = pe(lg, t_h2, (s_wr, 64), before)
        dq = [None]

        def d(fn, *w):
            dq[0] = dve(fn, dq[0], *w)
            return dq[0]
        bank_lg = bank
        t = d(lambda e: e.tensor_tensor(LG, bank_lg[:, 0:72].rearrange("p (a n) -> p a n", a=2),
                                        RB[:, :].unsqueeze(1).to_broadcast([128, 2, 36]), ALU.add), tp, rfree)
        free.append(t)
        d(lambda e: e.memset(G8, -3.0e38))
        d(lambda e: e.tensor_copy(G8[:, :, 0:4], LG[:, :, 0:4]))

        def top(src, mx, ix):
            for a in range(2):
                d(lambda e, a=a: e.max(mx[:, a, :], src[:, a, :]))
                d(lambda e, a=a: e.max_index(ix[:, a, :].bitcast(U32), mx[:, a, :], src[:, a, :]))
        top(G8, MX, IX)
        d(lambda e: e.tensor_copy(GIF, IX[:, :, 0].bitcast(U32)))
        t = d(lambda e: e.tensor_tensor(EG, LG[:, :, 0:4], MX[:, :, 0:1].to_broadcast([128, 2, 4]), ALU.subtract))
        t = act(lambda e: e.activation(EG, EG, ACT.Exp), t)
        iota = TWO[:, B_IOTA:B_IOTA + 128]
        d(lambda e: e.tensor_tensor(OG, iota[:, 0:4].unsqueeze(1).to_broadcast([128, 2, 4]),
                                    GIF.unsqueeze(2).to_broadcast([128, 2, 4]), ALU.is_equal))
        for a in range(2):
            d(lambda e, a=a: e.tensor_tensor(
                EP[:, a, :].rearrange("p (j g) -> p j g", g=4),
                LG[:, a, 4:36].rearrange("p (g j) -> p j g", g=4),
                OG[:, a, :].unsqueeze(1).to_broadcast([128, 8, 4]), ALU.mult))
        d(lambda e: e.tensor_reduce(E8, EP.rearrange("p a (j g) -> p a j g", g=4), AX.X, ALU.add))
        top(E8, MXE, IXE)
        d(lambda e: e.tensor_reduce(GW, EG, AX.X, ALU.add), t)
        d(lambda e: e.reciprocal(GW, GW))
        t = d(lambda e: e.tensor_tensor(R1, MXE[:, :, 1], MXE[:, :, 0], ALU.subtract))
        t = act(lambda e: e.activation(R1, R1, ACT.Exp), t)
        d(lambda e: e.tensor_copy(IDF, IXE[:, :, 0:2].bitcast(U32)))
        d(lambda e: e.scalar_tensor_tensor(IDF, GIF.unsqueeze(2).to_broadcast([128, 2, 2]), 8.0, IDF,
                                           ALU.mult, ALU.add))
        d(lambda e: e.tensor_tensor(AA, iota[:, 0:32].unsqueeze(1).to_broadcast([128, 4, 32]),
                                    IDF.rearrange("p a k -> p (a k)").unsqueeze(2).to_broadcast([128, 4, 32]),
                                    ALU.is_equal))
        A4 = AA.rearrange("p (a k) n -> p a k n", a=2)
        t_a = d(lambda e: e.tensor_tensor(A01, A4[:, :, 0, :], A4[:, :, 1, :], ALU.add))
        bank2, before, free2 = PS.take()

        def cnt(e):
            slt = TWO[:, B_SLT:B_SLT + 128]
            e.matmul(bank2[:, 0:32], slt, A01[:, 0, :], start=True, stop=True)
            e.matmul(bank2[:, 32:64], slt, A01[:, 1, :], start=True, stop=False)
            e.matmul(bank2[:, 32:64], ONES[:, :], A01[:, 0, :], start=False, stop=True)
            e.matmul(bank2[:, 64:96], ONES[:, :], A01[:, 0, :], start=True, stop=False)
            return e.matmul(bank2[:, 64:96], ONES[:, :], A01[:, 1, :], start=False, stop=True)
        tp = pe(cnt, t_a, before)
        d(lambda e: e.tensor_scalar(RD, R1, 1.0, None, ALU.add), t)
        d(lambda e: e.reciprocal(RD, RD))
        d(lambda e: e.tensor_tensor(WGT[:, :, 0], GW, RD, ALU.mult))
        t_wgt = d(lambda e: e.tensor_tensor(WGT[:, :, 1], WGT[:, :, 0], R1, ALU.mult))
        free2.append(d(lambda e: e.tensor_copy(PC, bank2[:, 0:96]), tp))
        d(lambda e: e.tensor_scalar(IND, PC[:, 64:96], float(CAP), None, ALU.is_gt))
        d(lambda e: e.tensor_tensor_scan(XI, ONES[:, 0:32], IND, 0.0, ALU.mult, ALU.add))
        d(lambda e: e.tensor_copy(EIA[:, 6:7], XI[:, 31:32]))
        d(lambda e: e.tensor_tensor(XI, XI, IND, ALU.subtract))
        d(lambda e: e.tensor_scalar(BS[:, 0, :], iota[:, 0:32], float(CAP), None, ALU.mult))
        d(lambda e: e.tensor_scalar(BS[:, 1, :], XI, float(CAP), float(CAP * (N_EXP - 1)), ALU.mult, ALU.add))
        for j in range(N_EXTRA):
            d(lambda e, j=j: e.scalar_tensor_tensor(TJ, XI, float(j), IND, ALU.is_equal, ALU.mult))
            d(lambda e, j=j: e.tensor_tensor(TJ, TJ, iota[:, 0:32], ALU.mult))
            d(lambda e, j=j: e.tensor_reduce(EIA[:, j:j + 1], TJ, AX.X, ALU.add))
            d(lambda e, j=j: e.tensor_scalar(EIA[:, 3 + j:4 + j], EIA[:, 6:7], float(j), None, ALU.is_gt))
        t_ints = d(lambda e: e.tensor_copy(INTS[:, 0:6], EIA[:, 0:6]))
        for src, dst in ((PC[:, 0:64].rearrange("p (a n) -> p a n", a=2).unsqueeze(2).to_broadcast([128, 2, 2, 32]), PP),
                         (BS[:, 0, :].unsqueeze(1).to_broadcast([128, 4, 32]), S0),
                         (BS[:, 1, :].unsqueeze(1).to_broadcast([128, 4, 32]), S1b)):
            a_ = AA if src.ndim == 3 else A4
            p_ = PR if src.ndim == 3 else PR.rearrange("p (a k) n -> p a k n", a=2)
            d(lambda e, src=src, a_=a_, p_=p_: e.tensor_tensor(p_, a_, src, ALU.mult))
            d(lambda e, dst=dst: e.tensor_reduce(dst, PR, AX.X, ALU.add))
        d(lambda e: e.tensor_scalar(BIG, PP, float(CAP), None, ALU.is_ge))
        d(lambda e: e.tensor_tensor(S1b, S1b, S0, ALU.subtract))
        d(lambda e: e.tensor_tensor(S1b, S1b, BIG, ALU.mult))
        d(lambda e: e.tensor_tensor(GS, PP, S0, ALU.add))
        d(lambda e: e.tensor_tensor(GS, GS, S1b, ALU.add))
        t_idx = d(lambda e: e.tensor_copy(INTS[:, 8:12].bitcast(U32), GS))
        for q in range(4):
            t_gb = d(lambda e, q=q: e.tensor_scalar(GB[:, q, :], iota[:, 0:N_BLOCKS], float(-CAP), GS[:, q:q + 1],
                                                    ALU.mult, ALU.add))
        t_gb = d(lambda e: e.tensor_copy(iota2, iota))
        H2P = at("H2P", [128, 3, 2, 1024], BF16, oG + 24 * KB)
        HR = Buffers([at(f"HR{i}", [128, 512], F32, oZ + 8 * KB + 2 * KB * i) for i in range(2)], rfree)
        t_h2p = []
        for a in range(2):
            for hf in range(2):
                bank, before, free = PS.take()

                def tr(e, a=a, hf=hf, bank=bank):
                    for k in range(4):
                        last = e.transpose(bank[:, 128 * k:128 * k + 128], H2[:, 4 * hf + k, 128 * a:128 * a + 128], ident)
                    return last
                tp = pe(tr, t_h2, before)
                sl = slice(512 * hf, 512 * hf + 512)
                r, bf, fr = HR.take()
                t1 = act(lambda e, a=a, sl=sl, bank=bank: e.activation(H2P[:, 0, a, sl], bank[:, :], ACT.Copy), tp, rfree, t_gb)
                t2 = dve(lambda e, a=a, sl=sl, bank=bank, r=r: e.tensor_tensor(r[:, :], bank[:, :], H2P[:, 0, a, sl],
                                                                               ALU.subtract), t1, tp, bf)
                free.append(t2)
                t3 = act(lambda e, a=a, sl=sl, r=r: e.activation(H2P[:, 1, a, sl], r[:, :], ACT.Copy), t2, t_gb)
                t4 = dve(lambda e, a=a, sl=sl, r=r: e.tensor_tensor(H2P[:, 2, a, sl], r[:, :], H2P[:, 1, a, sl],
                                                                    ALU.subtract), t3)
                fr.append(t4)
                t_h2p += [t1, t3, t4]
        XGB = Buffers([(at(f"XH{i}", [128, 8, 128], F32R, oG + 8 * KB * i),
                        at(f"XL{i}", [128, 8, 128], F32R, oG + 8 * KB * i + 4 * KB)) for i in range(2)], t_dense)
        GGB = Buffers([(at(f"GGH{i}", [128, 4, 128], F32R, oG + 36 * KB + 4 * KB * i),
                        at(f"GGL{i}", [128, 4, 128], F32R, oG + 38 * KB + 4 * KB * i)) for i in range(2)], t_dense)
        UB = Buffers([at(f"U{i}", [128, 512], F32, oZ + 16 * KB + 2 * KB * i) for i in range(2)], rfree)
        UBfix = [pe.last()]
        for f in UB.free:
            f.extend(UBfix)
        WM = Buffers([(at(f"MH{i}", [128, 1024], F32R, oH + 8 * KB * i),
                       at(f"ML{i}", [128, 1024], F32R, oH + 8 * KB * i + 4 * KB)) for i in range(3)], t_dense)
        YB = Buffers([at(f"Y{i}", [128, 1024], F32, oH + 24 * KB + 4 * KB * i) for i in range(2)], t_dense)
        SB_ = Buffers([at(f"SB{i}", [128, 3, 128], BF16, oZ + 12 * KB + 1024 * i) for i in range(2)], rfree)
        YD = nc.dram_tensor("YD", (N_BLOCKS * CAP, D), F32, kind="Internal").ap()
        mslots = ring_slots + [at(f"RW{i}", [128, 2048], F32, oW + 8 * KB * i) for i in range(2)]
        mring = Ring(sp, mslots, sems, counts, ring.before + [t_dense, t_dense])
        mring.i = ring.i % 8
        s_y = [nc.alloc_semaphore(f"s_y{i}") for i in range(2)]
        w_src = (A["w1_2"][0], A["w3_2"][0], A["w2_2"][0])

        def expert_loads(which, extra):
            regs = {}

            def fill(j):
                src, k = w_src[j // 2], j % 2
                n = 512 if j < 4 else 1024
                kn = 2048 // n

                def f(e, place, sem):
                    dst = place[:, :].rearrange("p (k n) -> p k n", k=kn)
                    if not extra:
                        e.dma_start(dst, src[which].rearrange("(k p) n -> p k n", p=128)[:, kn * k:kn * k + kn, :])\
                            .then_inc(sem, 16)
                        return
                    if j == 0:
                        regs["e"] = e.value_load(INTS[0:1, which:which + 1], min_val=0, max_val=N_EXP - 1)
                        regs["on"] = e.value_load(INTS[0:1, 3 + which:4 + which], min_val=0, max_val=1)
                    v = src[bass.ds(regs["e"], 1)].rearrange("a (k p) n -> p (a k) n", p=128)
                    e.dma_start(dst, v[:, kn * k:kn * k + kn, :], cond=regs["on"]).then_inc(sem, 16)
                return f
            out = []
            for j in range(6):
                if extra and j == 0:
                    sp.raw(lambda e: None, t_ints)
                out.append(mring.load(fill(j)))
            return out

        def gather(b):
            S, bf, fr_s = SB_.take()
            t_s = []
            for a in range(2):
                t1 = dve(lambda e, a=a: e.tensor_scalar(S[:, 2, :], iota2, GB[:, 2 * a, b:b + 1], None, ALU.is_equal),
                         bf, t_gb, list(t_s))
                t2 = dve(lambda e, a=a: e.scalar_tensor_tensor(S[:, a, :], iota2, GB[:, 2 * a + 1, b:b + 1], S[:, 2, :],
                                                               ALU.is_equal, ALU.add), t1)
                t_s.append(t2)
            (xh_, xl_), bf, fr = XGB.take()
            toks = []
            for hf in range(2):
                bank, before, free = PS.take()

                def mm(e, hf=hf, bank=bank):
                    for k in range(4):
                        for a in range(2):
                            for q in range(3):
                                last = e.matmul(bank[:, 128 * k:128 * k + 128],
                                                H2P[:, q, a, 512 * hf + 128 * k:512 * hf + 128 * k + 128],
                                                S[:, a, :], start=(a == 0 and q == 0), stop=(a == 1 and q == 2))
                    return last
                tp = pe(mm, t_s, t_h2p, before)
                v = bank[:, :].rearrange("p (k n) -> p k n", k=4)
                ks = slice(4 * hf, 4 * hf + 4)
                t1 = act(lambda e, v=v, ks=ks: e.activation(xh_[:, ks, :], v, ACT.Copy), tp, bf)
                t2 = dve(lambda e, v=v, ks=ks: e.tensor_tensor(xl_[:, ks, :], v, xh_[:, ks, :].bitcast(F32),
                                                               ALU.subtract), t1, tp, bf)
                free.append(t2)
                toks += [t1, t2]
            fr_s.append(tp)
            return xh_, xl_, toks, fr

        def part_of(item, u):
            (wh, wl), bf, fr = WM.take()
            src = item.place[:, 1024 * u:1024 * u + 1024]
            th = act(lambda e: e.activation(wh[:, :], src, ACT.Copy), item.ready, bf)
            tl = dve(lambda e: e.tensor_tensor(wl[:, :], src, wh[:, :].bitcast(F32), ALU.subtract),
                     item.ready, bf, th)
            item.done.append(tl)
            return wh, wl, th, tl, fr

        def up_half(items, xh_, xl_, toks):
            bank, before, free = PS.take()
            for q in range(4):
                wh, wl, th, tl, fr = part_of(items[q // 2], q % 2)

                def mm(e, q=q, wh=wh):
                    for j in range(2):
                        k = 2 * q + j
                        e.matmul(bank[:, :], xh_[:, k, :], wh[:, 512 * j:512 * j + 512], start=(k == 0), stop=False)
                        last = e.matmul(bank[:, :], xl_[:, k, :], wh[:, 512 * j:512 * j + 512], start=False, stop=False)
                    return last
                pe(mm, toks, th, before)

                def mm2(e, q=q, wl=wl):
                    for j in range(2):
                        k = 2 * q + j
                        last = e.matmul(bank[:, :], xh_[:, k, :], wl[:, 512 * j:512 * j + 512], start=False, stop=(k == 7))
                    return last
                tp = pe(mm2, tl)
                fr.append(tp)
            return bank, tp, free

        def hidden(b1, t1, f1, b3, t3, f3):
            u, bf, fr = UB.take()
            ts = act(lambda e: e.activation(u[:, :], b1[:, :], ACT.Silu), t1, bf)
            f1.append(ts)
            tm = dve(lambda e: e.tensor_tensor(u[:, :], b3[:, :], u[:, :], ALU.mult), ts, t3)
            f3.append(tm)
            return u, tm, fr

        def hidden_parts(u, tm, fr_u):
            bank, before, free = PS.take()

            def tr(e):
                for k in range(4):
                    last = e.transpose(bank[:, 128 * k:128 * k + 128], u[:, 128 * k:128 * k + 128], ident)
                return last
            tp = pe(tr, tm, before)
            fr_u.append(tp)
            (gh, gl), bf, fr = GGB.take()
            v = bank[:, :].rearrange("p (k n) -> p k n", k=4)
            th = act(lambda e: e.activation(gh[:, :, :], v, ACT.Copy), tp, bf)
            tl = dve(lambda e: e.tensor_tensor(gl[:, :, :], v, gh[:, :, :].bitcast(F32), ALU.subtract), tp, bf, th)
            free.append(tl)
            return gh, gl, [th, tl], fr

        n_y = [0]

        def down_half(b, items, gh, gl, toks, fr_g):
            ba, before_a, free_a = PS.take()
            bb_, before_b, free_b = PS.take()
            for k in range(4):
                wh, wl, th, tl, fr = part_of(items[k // 2], k % 2)

                def mm(e, k=k, wh=wh):
                    for bk, c in ((ba, 0), (bb_, 512)):
                        e.matmul(bk[:, :], gh[:, k, :], wh[:, c:c + 512], start=(k == 0), stop=False)
                        last = e.matmul(bk[:, :], gl[:, k, :], wh[:, c:c + 512], start=False, stop=False)
                    return last
                pe(mm, toks, th, before_a, before_b)

                def mm2(e, k=k, wl=wl):
                    for bk, c in ((ba, 0), (bb_, 512)):
                        last = e.matmul(bk[:, :], gh[:, k, :], wl[:, c:c + 512], start=False, stop=(k == 3))
                    return last
                tp = pe(mm2, tl)
                fr.append(tp)
            fr_g.append(tp)
            y, bf, fr = YB.take()
            t1 = act(lambda e: e.activation(y[:, 0:512], ba[:, :], ACT.Copy), tp, bf)
            t2 = dve(lambda e: e.tensor_copy(y[:, 512:1024], bb_[:, :]), tp, bf)
            free_a.append(t1)
            free_b.append(t2)
            i = n_y[0]
            n_y[0] += 1
            sem = s_y[i % 2]
            pool.raw(lambda e: e.dma_start(YD[CAP * b:CAP * b + CAP, :], y[:, :]).then_inc(sem, 16), t1, t2)
            fr.append((sem, 16 * (i // 2 + 1)))

        order = []
        for e_ in range(N_EXP):
            order.append((e_, e_, False))
            if e_ in EXTRA_AFTER:
                j = EXTRA_AFTER[e_]
                order.append((N_EXP + j, j, True))
        nxt = gather(order[0][0])
        loads = None
        for i, (b, which, extra) in enumerate(order):
            xh_, xl_, toks, fr_x = nxt
            items = expert_loads(which, extra)
            b1, t1, f1 = up_half(items[0:2], xh_, xl_, toks)
            b3, t3, f3 = up_half(items[2:4], xh_, xl_, toks)
            fr_x.append(t3)
            h_ = hidden(b1, t1, f1, b3, t3, f3)
            if i + 1 < len(order):
                nxt = gather(order[i + 1][0])
            g_ = hidden_parts(*h_)
            down_half(b, items[4:6], *g_)
        done = fence()
        YG = at("YG", [128, 4, 1024], F32, oR)
        MO = at("MO", [128, 2, 1024], F32, oR + 16 * KB)
        s_g = nc.alloc_semaphore("s_g")
        ny = [(s_y[j], 16 * ((n_y[0] + 1 - j) // 2)) for j in range(2)]
        t_mo = []
        for q in range(4):
            pool.raw(lambda e, q=q: e.indirect_dma_start(
                YG[:, q, :], None, YD, bass.IndirectOffsetOnAxis(ap=INTS[:, 8 + q:9 + q].bitcast(U32), axis=0))
                .then_inc(s_g, 16), done, ny, t_idx)
        for a in range(2):
            t1 = dve(lambda e, a=a: e.tensor_scalar(MO[:, a, :], YG[:, 2 * a, :], WGT[:, a, 0:1], None, ALU.mult),
                     (s_g, 64), done, t_wgt)
            t1 = dve(lambda e, a=a: e.scalar_tensor_tensor(MO[:, a, :], YG[:, 2 * a + 1, :], WGT[:, a, 1:2],
                                                           MO[:, a, :], ALU.mult, ALU.add), t1)
            t_mo.append(t1)
        t_xf = []
        for k in range(KT):
            bank, before, free = PS.take()

            def tr(e, k=k, bank=bank):
                for a in range(2):
                    last = e.transpose(bank[:, 128 * a:128 * a + 128], MO[:, a, 128 * k:128 * k + 128], ident)
                return last
            tp = pe(tr, t_mo, before)
            t1 = dve(lambda e, k=k, bank=bank: e.scalar_tensor_tensor(
                XT[:, k, 0:256], bank[:, 0:256], MOD[:, 2, 40 + k, V2:V2 + 1], XT[:, k, 0:256], ALU.mult, ALU.add),
                tp, done)
            free.append(t1)
            t_xf.append(t1)
        TB = Buffers(tmp[:7], done)
        OUT = at("OUT", [128, 2, 1024], F32, oR + 24 * KB)
        bank_s, before, free_s = PS.take()
        for k in range(KT):
            sq, bf, fr = TB.take()
            ts = act(lambda e, k=k, sq=sq: e.activation(sq[:, 0:N], XT[:, k, 0:N], ACT.Square), t_xf[k], bf)
            tp = pe(lambda e, k=k, sq=sq: e.matmul(bank_s[:, 0:N], ONES[:, :], sq[:, 0:N],
                                                   start=(k == 0), stop=(k == KT - 1)), ts, before)
            fr.append(tp)
        rb = tmp[7]
        tr_ = rstd(bank_s[:, 0:N], 1.0 / D, rb[:, 0:N], tp, done)
        free_s.append(tr_)
        banks_o = [PS.take() for _ in range(4)]
        t_o = []
        for k in range(KT):
            t_, bf, fr = TB.take()
            t1 = dve(lambda e, k=k, t_=t_: e.scalar_tensor_tensor(t_[:, 0:N], XT[:, k, 0:N], VEC[:, V_NF + k:V_NF + k + 1],
                                                                  rb[:, 0:N], ALU.mult, ALU.mult), tr_, bf)

            def tr(e, k=k, t_=t_):
                for a in range(2):
                    last = e.transpose(banks_o[2 * a + k // 4][0][:, 128 * (k % 4):128 * (k % 4) + 128],
                                       t_[:, 128 * a:128 * a + 128], ident)
                return last
            tp = pe(tr, t1, [banks_o[j][1] for j in range(4)])
            fr.append(tp)
            if k % 4 == 3:
                hf = k // 4
                for a in range(2):
                    bk = banks_o[2 * a + hf][0]
                    t_o.append((dve if a else act)(
                        (lambda e, a=a, bk=bk, hf=hf: e.tensor_copy(OUT[:, a, 512 * hf:512 * hf + 512], bk[:, :])) if a else
                        (lambda e, a=a, bk=bk, hf=hf: e.activation(OUT[:, a, 512 * hf:512 * hf + 512], bk[:, :], ACT.Copy)),
                        tp, done))
        s_out = nc.alloc_semaphore("s_out")
        sp.raw(lambda e: e.dma_start(A["out"][0].rearrange("(a p) d -> p a d", p=128), OUT[:, :, :]).then_inc(s_out, 16),
               t_o)
        sp.raw(lambda e: None, (s_out, 16), (s_g, 64), ny)

    r = layer(0, t_x, rdy_wp)
    r = layer(1, [[t] for t in r[0]], r[1])
    second([[t] for t in r[0]])
    sp.raw(lambda e: None, [(sems[k], counts[k]) for k in range(N_SLOTS) if counts[k]], (s_wp, 256), (s_vec, n_vec[0]))
    finish(nc, pe, act, dve, pool, sp)


def finish(nc, pe, act, dve, pool, sp):
    with nc.Block() as block:
        @block.tensor
        def _(e):
            pe.emit(e)

        @block.scalar
        def _(e):
            act.emit(e)

        @block.vector
        def _(e):
            dve.emit(e)

        @block.gpsimd
        def _(e):
            pool.emit(e)

        @block.sync
        def _(e):
            sp.emit(e)


_INS = ("x", "c", "ctx", "c_ctx", "w_ada", "b_ada", "g_mix", "g_ffn", "w_in", "q_gain", "k_gain", "w_pool",
        "pool_scale", "w_four", "w_out", "w_gate_up", "w_down", "c_2", "positions_2", "w_ada_2", "b_ada_2",
        "norm1_g_2", "w_in_2", "b_gate_2", "conv_w_2", "conv_b_2", "attn_out_g_2", "mlstm_out_g_2", "w_out_2",
        "norm2_g_2", "w_rg_2", "b_rg_2", "w_re_2", "b_re_2", "w1_2", "w3_2", "w2_2", "norm_f_g_2")
_OUTS = [((1, 256, 1024), "float32")]


def kernel(**inputs):
    import numpy as _np
    import concourse.bacc as _bacc
    from concourse import mybir as _mybir
    from concourse.bass_utils import run_bass_kernel_spmd as _run

    nc = _bacc.Bacc("TRN2", target_bir_lowering=False, num_devices=1)
    arrays, args = {}, {}
    for name, a in [(n, inputs[n]) for n in _INS] + sorted(constants().items()):
        a = _np.ascontiguousarray(a)
        arrays[f"in_{name}_dram"] = a
        args[name] = nc.dram_tensor(f"in_{name}_dram", a.shape, _mybir.dt.from_np(a.dtype), kind="ExternalInput").ap()
    shape, dtype = _OUTS[0]
    args["out"] = nc.dram_tensor("out_0_dram", shape, _mybir.dt.from_np(_np.dtype(dtype)), kind="ExternalOutput").ap()
    block_program(nc, args)
    r = _run(nc, [arrays], core_ids=[0])
    return r.results[0]["out_0_dram"]
```

```python
import numpy as np
import concourse.bass as bass
from concourse import mybir

F32 = mybir.dt.float32
F32R = mybir.dt.float32r
BF16 = mybir.dt.bfloat16
I32 = mybir.dt.int32
U32 = mybir.dt.uint32
ALU = mybir.AluOpType
ACT = mybir.ActivationFunctionType
AX = mybir.AxisListType

D = 1024
KT = 8
NEG = -1.0e30
EPS = 1e-6
HALF = 11
N_EXP = 32
CAP = 64
N_EXTRA = 7
N_BLOCKS = N_EXP + N_EXTRA
N_SLOTS = 16

V_C, V_CCTX, V_C2, V_GMIX, V_GFFN = 0, 8, 16, 24, 40
V_N1, V_N2, V_NF, V_CW, V_CB, V_AG, V_MG = 56, 64, 72, 80, 112, 120, 124
V_BADA, V_PS, V_QG, V_KG, V_BADA2 = 128, 224, 228, 230, 256

K_POOL, K_DFT, K_R1, K_D, K_RD, K_CD, K_SD = 0, 0, 1024, 1152, 1408, 1664, 1792
K_END = 1920
S_ID, S_BD, S_COS, S_SIN = 0, 128, 256, 512
S_END = 768
B_R2, B_TRI, B_TRIT, B_SLT, B_IOTA, B_FREQ, B_MOD = 0, 128, 384, 512, 640, 768, 769
B_END = 897


def constants():
    eye = np.eye(128)
    blocks = np.kron(np.eye(2), np.ones((64, 64)))
    r1 = np.zeros((128, 128))
    r2 = np.zeros((128, 128))
    for m in range(128):
        if (m // 16) % 2 == 0:
            r1[m, m + 16] = -1
        else:
            r1[m, m - 16] = 1
        if (m // 32) % 2 == 0:
            r2[m, m + 32] = -1
        else:
            r2[m, m - 32] = 1
    dup = [np.zeros((128, 128)) for _ in range(2)]
    for g in range(2):
        for m in range(128):
            dup[g][m, 64 * g + m % 64] = 1
    t = np.arange(256)
    freqs = np.float32(10000.0) ** (-np.arange(16, dtype=np.float32) / np.float32(16))
    ang = np.zeros((128, 256), np.float32)
    for m in range(128):
        a, f = (m % 64) // 32, m % 16
        ids = (t // 64 if a == 0 else t % 64).astype(np.float32)
        ang[m] = ids * freqs[f]
    lt = 2 * np.pi * ((t[:, None] * t[None, :]) % 256) / 256
    c = np.arange(64)
    ld = 2 * np.pi * ((c[:, None] * c[None, :]) % 64) / 64
    dft = np.concatenate([np.cos(lt), np.sin(lt)], axis=1) / 16.0
    pool = np.zeros((256, 4, 256))
    for w, win in enumerate((2, 4, 8, 16)):
        for i in range(256):
            lo, hi = max(i - win // 2, 0), min(i + win - win // 2, 256)
            pool[lo:hi, w, i] += 1.0 / (hi - lo)
            pool[i, w, i] -= 1.0
    mix = np.zeros((128, K_END))
    kpool = pool.reshape(2, 128, 1024).transpose(1, 0, 2).reshape(128, 2048)
    mix[:, K_DFT:K_R1] = dft.reshape(2, 128, 512).transpose(1, 0, 2).reshape(128, 1024)
    mix[:, K_R1:K_D] = r1.T
    for g in range(2):
        mix[:, K_D + 128 * g:K_D + 128 * g + 128] = dup[g].T
        mix[:, K_RD + 128 * g:K_RD + 128 * g + 128] = (r1 @ dup[g]).T
    mix[:, K_CD:K_SD] = np.kron(np.eye(2), np.cos(ld) / 8.0)
    mix[:, K_SD:K_END] = np.kron(np.eye(2), -np.sin(ld) / 8.0)
    res = np.zeros((128, S_END))
    res[:, S_ID:S_BD] = eye
    res[:, S_BD:S_COS] = blocks
    res[:, S_COS:S_SIN] = np.cos(ang)
    res[:, S_SIN:S_END] = np.sin(ang)
    two = np.zeros((128, B_END))
    i = np.arange(128)
    two[:, B_R2:B_TRI] = r2.T
    two[:, B_TRI + 128:B_TRIT] = np.where(i[None, :] <= i[:, None], 0, NEG)
    two[:, B_TRIT:B_SLT] = np.where(i[:, None] <= i[None, :], 0, NEG)
    two[:, B_SLT:B_IOTA] = i[:, None] < i[None, :]
    two[:, B_IOTA:B_FREQ] = np.arange(128)
    half = np.arange(32, dtype=np.float32)
    inv = np.float32(10000.0) ** (-half / np.float32(32))
    two[:, B_FREQ] = inv[i % 32]
    two[:, B_MOD:B_END] = i % CAP
    return {"k_pool": np.ascontiguousarray(kpool, np.float32), "k_mix": mix.astype(np.float32), "k_res": res.astype(np.float32), "k_two": two.astype(np.float32)}


class Engine:

    def __init__(self, sem):
        self.sem, self.n, self.entries = sem, 0, []

    def __call__(self, fn, *waits):
        self.n += 1
        self.entries.append((fn, waits, True))
        return (self.sem, self.n)

    def raw(self, fn, *waits):
        self.entries.append((fn, waits, False))

    def last(self):
        return (self.sem, self.n)

    def emit(self, eng):
        reached = {}

        def wait(tokens):
            for t in tokens:
                if isinstance(t, list):
                    wait(t)
                elif t is not None and t[1] > reached.get(t[0].name, 0):
                    eng.wait_ge(t[0], t[1])
                    reached[t[0].name] = t[1]

        for fn, waits, counted in self.entries:
            wait(list(waits))
            ins = fn(eng)
            if counted:
                ins.then_inc(self.sem, 1)


class Buffers:

    def __init__(self, places, free=()):
        self.places, self.i = places, 0
        self.free = [list(free) for _ in places]

    def take(self):
        k = self.i % len(self.places)
        self.i += 1
        before, self.free[k] = self.free[k], []
        return self.places[k], before, self.free[k]


class Loaded:
    def __init__(self, place, ready):
        self.place, self.ready, self.done = place, ready, []


class Chunk:

    def __init__(self, load, view):
        self.load, self.view, self.item = load, view, None

    def get(self):
        if self.item is None:
            self.item = self.load()
        return self.item


class Ring:

    def __init__(self, sp, slots, sems, counts, before):
        self.sp, self.slots, self.sems, self.counts = sp, slots, sems, counts
        self.before, self.i = before, 0

    def load(self, fill, dmas=1):
        k = self.i % len(self.slots)
        self.i += 1
        place, sem = self.slots[k], self.sems[k]
        self.counts[k] += 16 * dmas
        item = Loaded(place, (sem, self.counts[k]))
        self.sp.raw(lambda e: fill(e, place, sem), self.before[k])
        self.before[k] = item.done
        return item


def block_program(nc, A):
    pe, act, dve, pool, sp = (Engine(nc.alloc_semaphore(n)) for n in
                              ("s_pe", "s_act", "s_dve", "s_pool", "s_sp"))
    KB = 1024
    BASE = 16512

    def at(name, shape, dt, off):
        return nc.alloc_sbuf_tensor_at(name, shape, dt, offset=BASE + off)

    oX, oH, oG, oR, oZ, oS, oW = 0, 16 * KB, 48 * KB, 92 * KB, 156 * KB, 176 * KB, 176 * KB + 9888
    XT = at("XT", [128, KT, 512], F32, oX)
    HH = at("HH", [128, KT, 512], F32R, oH)
    HL = at("HL", [128, KT, 512], F32R, oH + 16 * KB)
    GH = at("GH", [128, HALF, 512], F32R, oG)
    GL = at("GL", [128, HALF, 512], F32R, oG + 22 * KB)
    ring_slots = [at(f"R{i}", [128, 2048], F32, oR + 8 * KB * i) for i in range(8)]
    ws = [(at(f"WH{i}", [128, HALF, 128], F32R, oW + i * 11264),
           at(f"WL{i}", [128, HALF, 128], F32R, oW + i * 11264 + 5632)) for i in range(2)]
    QT = at("QT", [128, 4, 512], F32, oZ)
    KTr = at("KTr", [128, 512], F32, oZ + 8 * KB)
    Z = at("Z", [128, 4, 640], F32, oZ + 10 * KB)
    tmp = [at(f"TMP{i}", [128, 512], F32, oZ + 2 * KB * i) for i in range(8)]
    RES = at("RES", [128, S_END], F32, oS)
    ONES = at("ONES", [128, 128], F32, oS + 3072)
    VEC = at("VEC", [128, 304], F32, oS + 3584)
    MOD = at("MOD", [128, 3, 48, 3], F32, oS + 4800)
    SG = at("SG", [128, 8, 2], F32, oS + 6528)
    WPF = at("WPF", [128, 4, 128], F32, oS + 6592)
    ST = at("ST", [128, 48], F32, oS + 8640)
    EB = at("EB", [128, 1], F32, oS + 8832)
    SC = at("SC", [128, KT, 32], F32, oS + 8864)
    AB = Buffers([at(f"AT{i}", [128, 512], F32, oZ + 16 * KB + 2048 * i) for i in range(2)])
    QR = at("QR", [128, 4, 512], F32, oH)
    KD = at("KD", [128, 2, 512], F32, oH + 8 * KB)
    mt = [at(f"MT{i}", [128, 512], F32, oH + 12 * KB + 2 * KB * i) for i in range(3)]
    pbuf = [at(f"P{i}", [128, 512], F32, oH + 18 * KB + 2 * KB * i) for i in range(3)]
    ptbuf = [at(f"PT{i}", [128, 4, 256], F32, oH + 24 * KB + 4 * KB * i) for i in range(2)]
    zt = [at(f"ZT{i}", [128, 512], F32, oG + 2 * KB * i) for i in range(3)]
    VR = at("VR", [128, 3, 128], F32, oG)

    banks = [nc.alloc_psum_tensor(f"ps{i}", [128, 512], F32) for i in range(8)]
    PS = Buffers(banks)
    WS = Buffers(ws)
    ident = RES[:, S_ID:S_BD]
    bd = RES[:, S_BD:S_COS]
    cos1, sin1 = RES[:, S_COS:S_SIN], RES[:, S_SIN:S_END]

    def fence():
        return [pe.last(), act.last(), dve.last(), pool.last()]

    s_res, s_vec, s_wp = (nc.alloc_semaphore(n) for n in ("s_res", "s_vec", "s_wp"))
    sems = [nc.alloc_semaphore(f"s_r{i}") for i in range(N_SLOTS)]
    counts = [0] * N_SLOTS
    ring = Ring(sp, ring_slots, sems, counts, [[] for _ in range(8)])

    pool.raw(lambda e: e.dma_start(RES[:, :], A["k_res"]).then_inc(s_res, 16))
    t_ones = dve(lambda e: e.memset(ONES[:, :], 1.0))
    t_wpf = dve(lambda e: e.memset(WPF[:, :, :], 0.0))
    t_eb = dve(lambda e: e.memset(EB[:, :], EPS))
    t_vr = dve(lambda e: e.memset(VR[:, :, :], 0.0))
    n_vec = [0]

    def vec_rows(col, ap):
        t, r = divmod(col, 128)
        n = ap.shape[0]
        n_vec[0] += 16
        act.raw(lambda e: e.dma_start(VR[r:r + n, t, 0:ap.shape[1]], ap).then_inc(s_vec, 16), t_vr)

    def rows(ap, pattern, **kw):
        return ap.rearrange(pattern, **kw)

    one = "(a p) -> a p"
    vec_rows(V_C, rows(A["c"], "o (a p) -> (o a) p", p=128))
    vec_rows(V_CCTX, rows(A["c_ctx"], one, p=128))
    vec_rows(V_BADA, rows(A["b_ada"], "l (a p) -> (l a) p", p=128))
    vec_rows(V_GMIX, rows(A["g_mix"], "l (a p) -> (l a) p", p=128))
    vec_rows(V_GFFN, rows(A["g_ffn"], "l (a p) -> (l a) p", p=128))
    vec_rows(V_C2, rows(A["c_2"], "o (a p) -> (o a) p", p=128))
    vec_rows(V_N1, rows(A["norm1_g_2"], "o (a p) -> (o a) p", p=128))
    vec_rows(V_N2, rows(A["norm2_g_2"], "o (a p) -> (o a) p", p=128))
    vec_rows(V_NF, rows(A["norm_f_g_2"], one, p=128))
    vec_rows(V_CW, rows(A["conv_w_2"], "o i (a p) -> (o i a) p", p=128))
    vec_rows(V_CB, rows(A["conv_b_2"], "o (a p) -> (o a) p", p=128))
    vec_rows(V_AG, rows(A["attn_out_g_2"], "o (a p) -> (o a) p", p=128))
    vec_rows(V_MG, rows(A["mlstm_out_g_2"], "o (a p) -> (o a) p", p=128))
    vec_rows(V_PS, rows(A["pool_scale"], "l (a p) -> (l a) p", p=128))
    vec_rows(V_BADA2, rows(A["b_ada_2"], "o (a p) -> (o a) p", p=128))
    for base, name in ((V_QG, "q_gain"), (V_KG, "k_gain")):
        for c in range(2):
            n_vec[0] += 16
            act.raw(lambda e, base=base, name=name, c=c: e.dma_start(
                VR[base - 128:base - 126, 1, 64 * c:64 * c + 64], A[name]).then_inc(s_vec, 16), t_vr)

    def load_mixer_weights(layer, free):
        for k, name in enumerate(("w_pool", "w_four")):
            for g in range(4):
                h = 64 * (g % 2)
                pool.raw(lambda e, k=k, g=g, h=h, name=name: e.dma_start(
                    WPF[h:h + 64, 2 * k + g // 2, h:h + 64], A[name][layer, g]).then_inc(s_wp, 16),
                    t_wpf, free)
        return (s_wp, 128 * (layer + 1))

    rdy_wp = load_mixer_weights(0, [])

    def transpose(out, in_, n=128):
        return lambda e: e.transpose(out, in_, ident[0:n, 0:n])

    def fill_tokens(name):
        def fill(e, place, sem):
            e.dma_start(place[:, :].rearrange("p (a d) -> p a d", a=2),
                        A[name][0].rearrange("(a p) d -> p a d", p=128)).then_inc(sem, 16)
        return fill

    tok = [ring.load(fill_tokens("x")), ring.load(fill_tokens("ctx"))]

    ada_src = [A["w_ada"][0], A["w_ada"][1], A["w_ada_2"][0]]

    def wchunk(src, c0, n):
        v = src.rearrange("(k p) n -> p k n", p=128)

        def fill(e, place, sem):
            e.dma_start(place[:, 0:8 * n].rearrange("p (k n) -> p k n", k=8), v[:, :, c0:c0 + n])\
                .then_inc(sem, 16)
        return fill

    t_vec = []
    bank, before, free = PS.take()
    for t in range(3):
        tt = pe(lambda e, t=t, bank=bank: e.transpose(bank[:, 128 * t:128 * t + 128], VR[:, t, :], ident),
                (s_res, 16), (s_vec, n_vec[0]), before)
    t_vec = dve(lambda e, bank=bank: e.tensor_copy(VEC[:, :], bank[:, 0:304]), tt)
    free.append(t_vec)
    t_qg = dve(lambda e: e.tensor_scalar(VEC[:, V_QG:V_QG + 2], VEC[:, V_QG:V_QG + 2], 0.125, None, ALU.mult), t_vec)
    t_sc = dve(lambda e: e.memset(SC[:, :, :], 0.0))
    t_sc = act(lambda e: e.activation(SC[:, :, 0:3], VEC[:, 0:24].rearrange("p (j k) -> p k j", j=3), ACT.Silu),
               t_vec, t_sc)

    t_x = []
    for k in range(KT):
        bank, before, free = PS.take()
        for a in range(4):
            tt = pe(lambda e, k=k, a=a, bank=bank: e.transpose(
                bank[:, 128 * a:128 * a + 128],
                tok[a // 2].place[:, 1024 * (a % 2) + 128 * k:1024 * (a % 2) + 128 * k + 128], ident),
                tok[a // 2].ready, before, (s_res, 16))
        tc = dve(lambda e, k=k, bank=bank: e.tensor_copy(XT[:, k, :], bank[:, :]), tt)
        free.append(tc)
        t_x.append(tc)
    for item in tok:
        item.done.append(tt)

    t_mod = [[], [], []]

    def ada_load(which, c):
        return which, c, ring.load(wchunk(ada_src[which], 256 * c, 256))

    def ada_use(which, c, item):
        w = item.place[:, :].rearrange("p (k n) -> p k n", k=8)
        bank, before, free = PS.take()

        def mm(e):
            for k in range(KT):
                g = k % 4
                last = e.matmul(bank[32 * g:32 * g + 32, 0:256], SC[:, k, :], w[:, k, :], start=(k < 4), stop=(k >= 4))
            return last
        tp = pe(mm, item.ready, before, t_sc)
        item.done.append(tp)
        AT, bf, fr = AB.take()
        ta = act(lambda e: e.activation(AT[:, 0:256], bank[:, 0:256], ACT.Copy), tp, bf)
        free.append(ta)
        bank2, before, free = PS.take()

        def tr(e):
            for m in range(2):
                last = e.transpose(bank2[:, 128 * m:128 * m + 128], AT[:, 128 * m:128 * m + 128], ident)
            return last
        tp = pe(tr, ta, before)
        fr.append(tp)
        t1 = dve(lambda e: e.tensor_reduce(
            MOD[:, which, 2 * c:2 * c + 2, :],
            bank2[:, 0:256].rearrange("p (m g j) -> p m j g", m=2, g=4)[:, :, 0:3, :], AX.X, ALU.add), tp)
        free.append(t1)
        bcol = (V_BADA + 48 * which if which < 2 else V_BADA2) + 2 * c
        td = dve(lambda e: e.tensor_tensor(
            MOD[:, which, 2 * c:2 * c + 2, :], MOD[:, which, 2 * c:2 * c + 2, :],
            VEC[:, bcol:bcol + 2].unsqueeze(2).to_broadcast([128, 2, 3]), ALU.add), t1, t_vec)
        t_mod[which].append(td)

    def split_weights(parts, n):
        (wh, wl), before, free = WS.take()
        k0 = 0
        th, tl = [], []
        for chunk, col, K in parts:
            item = chunk.get()
            w = chunk.view(item.place)[:, :, col:col + n]
            h, l = wh[:, k0:k0 + K, 0:n], wl[:, k0:k0 + K, 0:n]
            t = act(lambda e, h=h, w=w: e.activation(h, w, ACT.Copy), item.ready, before)
            th.append(t)
            t = dve(lambda e, h=h, l=l, w=w: e.tensor_tensor(l, w, h.bitcast(F32), ALU.subtract),
                    item.ready, before, t)
            tl.append(t)
            item.done.append(t)
            k0 += K
        return wh, wl, k0, th, tl, free

    def linear(tiles, xh, xl, t_in, N, evac, hooks=None):
        hooks = list(hooks or [])
        n_hooks = len(hooks)
        nxt = split_weights(*tiles[0])
        for i, (_, n) in enumerate(tiles):
            h, l, K, th, tl, free_w = nxt
            if i + 1 < len(tiles):
                nxt = split_weights(*tiles[i + 1])
            bank, before, free = PS.take()

            def mms(e, ks, parts, h=h, l=l, K=K, n=n, bank=bank):
                for k in ks:
                    for wi, xi in parts:
                        w_, x_ = (h, l)[wi][:, k, 0:n], (xh, xl)[xi](k)
                        first = k == 0 and (wi, xi) == (0, 0)
                        final = k == K - 1 and wi == 1
                        last = e.matmul(bank[0:n, 0:N], w_, x_, start=first, stop=final)
                return last

            if i == 0:
                for k in range(K):
                    pe(lambda e, k=k, f=mms: f(e, [k], ((0, 0), (0, 1))), before, th, t_in[k])
            else:
                pe(lambda e, f=mms, K=K: f(e, range(K), ((0, 0), (0, 1))), before, th, t_in)
            tp = pe(lambda e, f=mms, K=K: f(e, range(K), ((1, 0),)), tl)
            free_w.append(tp)
            free.extend(evac(i, bank, tp))
            while n_hooks - len(hooks) < n_hooks * (i + 1) // len(tiles):
                hooks.pop(0)()

    def split_out(src, hi, lo, tok_, *waits):
        th = act(lambda e: e.activation(hi, src, ACT.Copy), tok_, *waits)
        tl = dve(lambda e: e.tensor_tensor(lo, src, hi.bitcast(F32), ALU.subtract), th, tok_, *waits)
        return th, tl

    def rstd(sums, mean, out, *waits):
        t = act(lambda e: e.activation(out, sums, ACT.Ln, bias=EB[:, 0:1], scale=mean), t_eb, *waits)
        return act(lambda e: e.activation(out, out, ACT.Exp, scale=-0.5), t)

    def adaln(N, t_src, scales, TB, hi, lo, t_free, keep=None):
        bank, before, free = PS.take()
        for k in range(KT):
            sq, bf, fr = TB.take()
            if k % 2:
                ts = act(lambda e, k=k, sq=sq: e.activation(sq[:, 0:N], XT[:, k, 0:N], ACT.Square), t_src[k], bf)
            else:
                ts = dve(lambda e, k=k, sq=sq: e.tensor_tensor(sq[:, 0:N], XT[:, k, 0:N], XT[:, k, 0:N], ALU.mult),
                         t_src[k], bf)
            tp = pe(lambda e, k=k, sq=sq, bank=bank: e.matmul(bank[:, 0:N], ONES[:, :], sq[:, 0:N],
                                                               start=(k == 0), stop=(k == KT - 1)), ts, before, t_ones)
            fr.append(tp)
        rb = tmp[7]
        tr = rstd(bank[:, 0:N], 1.0 / D, rb[:, 0:N], tp, t_free)
        free.append(tr)
        out = []
        for k in range(KT):
            t, bf, fr = TB.take()
            t1 = dve(lambda e, k=k, t=t: e.tensor_tensor(t[:, 0:N], XT[:, k, 0:N], rb[:, 0:N], ALU.mult), tr, bf)
            dst = t if keep is None else keep(k)
            for cols, s, b, tw in scales:
                t2 = act(lambda e, k=k, t=t, dst=dst, cols=cols, s=s, b=b: e.activation(
                    dst[:, cols[0]:cols[1]], t[:, cols[0]:cols[1]], ACT.Identity, bias=b(k), scale=s(k)),
                    t1, tw, t_free)
            if hi is None:
                fr.append(t2)
                out.append([t2])
                continue
            th, tl = split_out(dst[:, 0:N], hi(k), lo(k), t2, t_free)
            fr.append(tl)
            out.append([th, tl])
        return out

    n_st = [0]
    st_free = [[] for _ in range(16)]

    def stat():
        k = n_st[0] % 16
        n_st[0] += 1
        before, st_free[k] = st_free[k], []
        return ST[:, 3 * k:3 * k + 3], before, st_free[k]

    def attention(jobs, PB, PTB, pair_done):
        steps = [(h, a) for h in range(len(jobs)) for a in range(len(jobs[h]["nk"]))]
        state, head_pt, pair = {}, {}, {}

        def scores(h, a):
            J = jobs[h]
            n = 128 * J["nk"][a]
            bank, before, free = PS.take()
            tp = pe(lambda e: e.matmul(bank[:, 0:n], J["q"](a), J["k"](n), start=True, stop=True),
                    before, J["waits"])
            P, bf, fr = PB.take()
            st, sbf, sfr = stat()
            src = bank
            if J["mask"] is not None:
                tp = dve(lambda e: e.tensor_tensor(P[:, 0:n], bank[:, 0:n], J["mask"](a), ALU.add), tp, bf)
                free.append(tp)
                src = P
            tm = dve(lambda e: e.tensor_reduce(st[:, 0:1], src[:, 0:n], AX.X, ALU.max, negate=True), tp, sbf)
            te = act(lambda e: e.activation(P[:, 0:n], src[:, 0:n], ACT.Exp, bias=st[:, 0:1],
                                            accum_out=st[:, 1:2]), tm, bf, tp)
            if src is bank:
                free.append(te)
            tr = dve(lambda e: e.reciprocal(st[:, 2:3], st[:, 1:2]), te)
            tn = dve(lambda e: e.tensor_scalar(P[:, 0:n], P[:, 0:n], st[:, 2:3], None, ALU.mult), tr)
            sfr.append(tn)
            state[h, a] = (P, fr, tn)

        def turn(h, a):
            J = jobs[h]
            nk = J["nk"][a]
            P, fr, tn = state.pop((h, a))
            if a == 0:
                head_pt[h] = (*PTB.take(), [])
            PT, bf, ptfr, toks = head_pt[h]
            bank, before, free = PS.take()

            def tr(e):
                for j in range(nk):
                    last = e.transpose(bank[:, 128 * j:128 * j + 128], P[:, 128 * j:128 * j + 128], ident)
                return last
            tp = pe(tr, tn, before)
            fr.append(tp)
            tc = act(lambda e: e.activation(PT[:, 0:nk, 128 * a:128 * a + 128],
                                            bank[:, 0:128 * nk].rearrange("p (j n) -> p j n", n=128), ACT.Copy),
                     tp, bf)
            free.append(tc)
            toks.append(tc)

        def values(h):
            J = jobs[h]
            PT, bf, ptfr, toks = head_pt.pop(h)
            if h % 2 == 0:
                pair[0] = PS.take()
            bank, before, free = pair[0]
            nk = J["nk"]
            r = 64 * (h % 2)

            def pv(e):
                groups = [(0, 128 * len(nk), nk[0])] if len(set(nk)) == 1 else \
                    [(128 * a, 128 * a + 128, nk[a]) for a in range(len(nk))]
                for lo, hi, m in groups:
                    for j in range(m):
                        last = e.matmul(bank[r:r + 64, lo:hi], J["v"](j), PT[:, j, lo:hi],
                                        start=(j == 0), stop=(j == m - 1))
                return last
            tp = pe(pv, toks, before, J["waits"])
            ptfr.append(tp)
            if h % 2:
                free.extend(pair_done(h // 2, bank, tp))

        LAG = 2
        for i in range(len(steps) + LAG):
            if i < len(steps):
                scores(*steps[i])
            if i >= LAG:
                h, a = steps[i - LAG]
                turn(h, a)
                if a == len(jobs[h]["nk"]) - 1:
                    values(h)

    MH = lambda m, lo, hi: GH[:, m, lo:hi]
    ML = lambda m, lo, hi: GL[:, m, lo:hi]

    def head_norm(src, rows_n, gain, MT, dst, waits, mean=1.0 / 64, red=None, t_free=None):
        n = rows_n
        sq, bf, fr = MT.take()
        ts = act(lambda e: e.activation(sq[:, 0:n], src, ACT.Square), waits, bf)
        bank, before, free = PS.take()
        tp = pe(lambda e: e.matmul(bank[:, 0:n], bd if red is None else red, sq[:, 0:n], start=True, stop=True),
                ts, before)
        t2 = rstd(bank[:, 0:n], mean, sq[:, 0:n], tp)
        free.append(t2)
        t3 = dve(lambda e: e.scalar_tensor_tensor(dst, src, gain, sq[:, 0:n], ALU.mult, ALU.mult), t2, waits, t_free)
        fr.append(t3)
        return t3

    def rope_into(dst, straight, turned, cos, sin, MT, waits, t_free=None):
        a, bf, fr = MT.take()
        t1 = dve(lambda e: e.tensor_tensor(a[:, 0:256], turned, sin, ALU.mult), waits, bf)
        t2 = dve(lambda e: e.tensor_tensor(dst, straight, cos, ALU.mult), waits, t_free)
        t3 = dve(lambda e: e.tensor_tensor(dst, dst, a[:, 0:256], ALU.add), t1, t2)
        fr.append(t3)
        return t1, t3

    def fm(ap, k=8):
        return ap.rearrange("p (k n) -> p k n", k=k)

    def wide(src, c0, n):
        return Chunk(lambda: ring.load(wchunk(src, c0, n)), lambda place: fm(place[:, 0:8 * n]))

    for c in range(24):
        ada_use(*ada_load(0, c))

    ada_queue = [(w, c) for w in (1, 2) for c in range(24)]

    def layer(i, t_x, rdy_wp):
        both = i == 0
        N = 512 if both else 256
        streams = (0, 1) if both else (0,)
        tmp_free = fence()
        TB = Buffers(tmp[:7], tmp_free)
        t_sg = dve(lambda e: e.scalar_tensor_tensor(
            SG[:, :, :], MOD[:, i, 8:16, 0:2], 1.0,
            VEC[:, V_GMIX + 8 * i:V_GMIX + 8 * i + 8].unsqueeze(2).to_broadcast([128, 8, 2]),
            ALU.add, ALU.mult), t_mod[i], t_vec, tmp_free)
        scales = [((256 * s, 256 * s + 256), lambda k, s=s: SG[:, k, s:s + 1], lambda k, s=s: MOD[:, i, k, s:s + 1], t_sg)
                  for s in (0, 1)]
        t_h = adaln(512, t_x, scales, TB, lambda k: HH[:, k, :], lambda k: HL[:, k, :], tmp_free)
        zfree = fence()
        chunks = [wide(A["w_in"][i], 256 * c, 256) for c in range(5)]

        def tile_of(m):
            return [(chunks[m // 2], 128 * (m % 2), 8)], 128

        t_q, t_k, t_z = [None] * 4, [None], []

        def evac(j, bank, tp):
            if j < 4:
                t_q[j] = act(lambda e: e.activation(QT[:, j, 0:N], bank[:, 0:N], ACT.Copy), tp, zfree)
                return [t_q[j]]
            t_k[0] = act(lambda e: e.activation(KTr[:, :], bank[:, :], ACT.Copy), tp, zfree)
            return [t_k[0]]

        xh, xl = lambda k: HH[:, k, 0:N], lambda k: HL[:, k, 0:N]
        linear([tile_of(m) for m in range(4)], xh, xl, t_h, N, evac)
        xh, xl = lambda k: HH[:, k, :], lambda k: HL[:, k, :]

        ZT = Buffers(zt, zfree)

        def evac_z(j, bank, tp, nt):
            t, bf, fr = ZT.take()
            tc = act(lambda e: e.activation(t[:, 0:128 * nt], bank[:, 0:128 * nt], ACT.Copy), tp, bf)
            bank2, before, free2 = PS.take()

            def tr(e):
                for a in range(nt):
                    last = e.transpose(bank2[:, 128 * a:128 * a + 128], t[:, 128 * a:128 * a + 128], ident)
                return last
            tt = pe(tr, tc, before)
            fr.append(tt)
            td = dve(lambda e: e.tensor_copy(Z[:, 0:nt, 128 * j:128 * j + 128],
                                             bank2[:, 0:128 * nt].rearrange("p (a n) -> p a n", n=128)), tt, zfree)
            free2.append(td)
            t_z.append(td)
            return [tc]
        nt = 4 if both else 2
        linear([tile_of(m) for m in (4, 5)], xh, xl, t_h, 512,
               lambda j, b, tp: evac_z(0, b, tp, 4) if j else evac(4, b, tp))
        xh, xl = lambda k: HH[:, k, 0:N], lambda k: HL[:, k, 0:N]
        linear([tile_of(m) for m in range(6, 10)], xh, xl, t_h, N,
               lambda j, b, tp: evac_z(j + 1, b, tp, nt))
        hfree = fence()
        MT, PB, PTB = Buffers(mt, hfree), Buffers(pbuf, hfree), Buffers(ptbuf, hfree)
        const = [ring.load(lambda e, place, sem, nm=nm, n=n: e.dma_start(place[:, 0:n], A[nm]).then_inc(sem, 16))
                 for nm, n in (("k_pool", 2048), ("k_mix", K_END))]
        kp, kc = const[0].place, const[1].place
        qg = VEC[:, V_QG + i:V_QG + i + 1]
        kg = VEC[:, V_KG + i:V_KG + i + 1]
        mfree = hfree
        t_kn = head_norm(KTr[:, :], 512, kg, MT, KTr[:, :], t_k[0])
        t_kd = []
        for g in range(2):
            bank, before, free = PS.take()
            tp = pe(lambda e, g=g, bank=bank: e.matmul(bank[:, :], kc[:, K_D + 128 * g:K_D + 128 * g + 128],
                                                       KTr[:, :], start=True, stop=True), t_kn, before, const[0].ready, const[1].ready)
            bank2, before, free2 = PS.take()
            tp2 = pe(lambda e, g=g, bank2=bank2: e.matmul(bank2[:, 0:256], kc[:, K_RD + 128 * g:K_RD + 128 * g + 128],
                                                          KTr[:, 0:256], start=True, stop=True), before)
            t0 = act(lambda e, g=g, bank=bank: e.activation(KD[:, g, 256:512], bank[:, 256:512], ACT.Copy), tp, hfree)
            t1, t3 = rope_into(KD[:, g, 0:256], bank[:, 0:256], bank2[:, 0:256], cos1, sin1, MT, [tp2, t0], hfree)
            free.extend([t0, t3])
            free2.append(t1)
            t_kd += [t0, t3]
        t_qr = [[], []]
        for m in range(4):
            tn = head_norm(QT[:, m, 0:N], N, qg, MT, QT[:, m, 0:N], [t_q[m], t_qg])
            bank, before, free = PS.take()
            tp = pe(lambda e, m=m, bank=bank: e.matmul(bank[:, 0:256], kc[:, K_R1:K_R1 + 128], QT[:, m, 0:256],
                                                       start=True, stop=True), tn, before)
            t1, t3 = rope_into(QR[:, m, 0:256], QT[:, m, 0:256], bank[:, 0:256], cos1, sin1, MT, [tp, tn], hfree)
            free.append(t1)
            t_qr[0].append(t3)
            t_qr[1].append(tn)
        t_m = [[] for _ in range(8)]

        def out_split(bank, m, lo, tp, scale=None):
            t, bf, fr = MT.take()
            if scale is None:
                tc = dve(lambda e: e.tensor_copy(t[:, 0:256], bank[:, 0:256]), tp, bf)
            else:
                tc = dve(lambda e: e.tensor_scalar(t[:, 0:256], bank[:, 0:256], scale, None, ALU.mult), tp, bf)
            th, tl = split_out(t[:, 0:256], MH(m, lo, lo + 256), ML(m, lo, lo + 256), tc, mfree)
            fr.append(tl)
            t_m[m] += [th, tl]
            return [tc]

        for s in streams:
            src = QR if s == 0 else QT
            jobs = []
            for h in range(8):
                r, m, g = 64 * (h % 2), h // 2, h // 4
                k0 = 0 if s == 0 else 256
                jobs.append({
                    "q": lambda a, r=r, m=m, s=s, src=src: src[r:r + 64, m, 256 * s + 128 * a:256 * s + 128 * a + 128],
                    "k": lambda n, r=r, g=g, k0=k0: KD[r:r + 64, g, k0:k0 + n],
                    "v": lambda j, g=g, s=s: Z[:, 2 * s + j, 64 * g:64 * g + 64],
                    "nk": [4, 4] if s == 0 else [2, 2], "mask": None,
                    "waits": [t_kd, t_qr[s][m], t_z[0]],
                })
            attention(jobs, PB, PTB, lambda p, bank, tp, s=s: out_split(bank, p, 256 * s, tp))
        for s in streams:
            for j in range(2):
                bank, before, free = PS.take()

                def mm(e, s=s, j=j, bank=bank):
                    for a in range(2):
                        for t in range(2):
                            c = 128 + 128 * j + 64 * a
                            p = K_POOL + 1024 * t + 256 * (2 * j + a)
                            last = e.matmul(bank[64 * a:64 * a + 64, 0:256], Z[:, 2 * s + t, c:c + 64],
                                            kp[:, p:p + 256], start=(t == 0), stop=(t == 1))
                    return last
                tp = pe(mm, t_z, before, const[0].ready, const[1].ready)
                d, bf, fr = MT.take()
                tc = act(lambda e, d=d, bank=bank: e.activation(d[:, 0:256], bank[:, 0:256], ACT.Copy), tp, bf)
                free.append(tc)
                bank, before, free = PS.take()
                tp = pe(lambda e, j=j, d=d, bank=bank: e.matmul(bank[:, 0:256], WPF[:, j, :], d[:, 0:256],
                                                                start=True, stop=True), tc, before, rdy_wp)
                fr.append(tp)
                free.extend(out_split(bank, 4 + j, 256 * s, tp, VEC[:, V_PS + 2 * i + j:V_PS + 2 * i + j + 1]))
            for j in range(2):
                bank, before, free = PS.take()

                def mm(e, s=s, j=j, bank=bank):
                    for t in range(2):
                        last = e.matmul(bank[:, :], Z[:, 2 * s + t, 384 + 128 * j:512 + 128 * j],
                                        kc[:, K_DFT + 512 * t:K_DFT + 512 * t + 512], start=(t == 0), stop=(t == 1))
                    return last
                tp = pe(mm, t_z, before, const[0].ready, const[1].ready)
                d, bf, fr = MT.take()
                tc = act(lambda e, d=d, bank=bank: e.activation(d[:, :], bank[:, :], ACT.Copy), tp, bf)
                free.append(tc)
                bank, before, free = PS.take()

                def mm(e, d=d, bank=bank):
                    e.matmul(bank[:, 0:256], kc[:, K_CD:K_SD], d[:, 0:256], start=True, stop=False)
                    return e.matmul(bank[:, 0:256], kc[:, K_SD:K_END], d[:, 256:512], start=False, stop=True)
                tp = pe(mm, tc, before)
                fr.append(tp)
                d, bf, fr = MT.take()
                tc = act(lambda e, d=d, bank=bank: e.activation(d[:, 0:256], bank[:, 0:256], ACT.Copy), tp, bf)
                free.append(tc)
                bank, before, free = PS.take()
                tp = pe(lambda e, j=j, d=d, bank=bank: e.matmul(bank[:, 0:256], WPF[:, 2 + j, :], d[:, 0:256],
                                                                start=True, stop=True), tc, before, rdy_wp)
                fr.append(tp)
                free.extend(out_split(bank, 6 + j, 256 * s, tp))
        for item in const:
            item.done.append(pe.last())
        t_mixers = fence()
        rdy_wp = load_mixer_weights(1, [pe.last()]) if both else None
        chunks_o = [wide(A["w_out"][i], 256 * c, 256) for c in range(4)]

        def residual(gate):
            def f(j, bank, tp):
                out = []
                for s in streams:
                    sl = slice(256 * s, 256 * s + 256)
                    out.append(dve(lambda e, sl=sl, s=s: e.scalar_tensor_tensor(
                        XT[:, j, sl], bank[:, sl], MOD[:, i, gate + j, s:s + 1], XT[:, j, sl], ALU.mult, ALU.add),
                        tp, t_xw[j]))
                t_xw[j] = out
                return out
            return f

        t_xw = [[t, fence()] for t in t_x]
        tiles = [([(chunks_o[m // 2], 128 * (m % 2), 8)], 128) for m in range(8)]
        linear(tiles, lambda k: GH[:, k, 0:N], lambda k: GL[:, k, 0:N], t_m, N, residual(16))
        TB = Buffers(tmp[:7], t_mixers)
        t_sg2 = dve(lambda e: e.scalar_tensor_tensor(
            SG[:, :, :], MOD[:, i, 32:40, 0:2], 1.0,
            VEC[:, V_GFFN + 8 * i:V_GFFN + 8 * i + 8].unsqueeze(2).to_broadcast([128, 8, 2]),
            ALU.add, ALU.mult), t_mod[i], t_mixers)
        scales = [((256 * s, 256 * s + 256), lambda k, s=s: SG[:, k, s:s + 1],
                   lambda k, s=s: MOD[:, i, 24 + k, s:s + 1], t_sg2) for s in streams]
        t_h = adaln(N, t_xw, scales, TB, lambda k: HH[:, k, 0:N], lambda k: HL[:, k, 0:N], t_mixers)
        xh, xl = lambda k: HH[:, k, 0:N], lambda k: HL[:, k, 0:N]
        g_free = fence()
        for half in range(2):
            items = []
            for c in range(0, 1408, 256):
                n = min(256, 1408 - c)
                gate = wide(A["w_gate_up"][i], 1408 * half + c, n)
                up = wide(A["w_gate_up"][i], 2816 + 1408 * half + c, n)
                for j in range(n // 128):
                    items += [([(gate, 128 * j, 8)], 128), ([(up, 128 * j, 8)], 128)]
            t_g = [[] for _ in range(HALF)]
            held = {}

            def evac(j, bank, tp):
                m = j // 2
                if j % 2 == 0:
                    t, bf, fr = TB.take()
                    ts = act(lambda e: e.activation(t[:, 0:N], bank[:, 0:N], ACT.Silu), tp, bf)
                    held[m] = (t, fr, ts)
                    return [ts]
                t, fr, ts = held.pop(m)
                t2 = dve(lambda e: e.tensor_tensor(t[:, 0:N], bank[:, 0:N], t[:, 0:N], ALU.mult), tp, ts)
                th, tl = split_out(t[:, 0:N], GH[:, m, 0:N], GL[:, m, 0:N], t2, g_free)
                fr.append(tl)
                t_g[m] += [th, tl]
                return [t2]
            hooks = []
            if both and half == 0:
                for fr in AB.free:
                    fr.append(t_mixers)
            if both:
                for _ in range(24):
                    w, c = ada_queue.pop(0)
                    hooks.append(lambda w=w, c=c: ada_use(*ada_load(w, c)))
            linear(items, xh, xl, t_h, N, evac, hooks)
            downs = []
            vd = A["w_down"][i].rearrange("(k p) n -> p k n", p=128)
            for c in range(4):
                pair = []
                for k0, kn in ((0, 6), (6, 5)):
                    def fill(e, place, sem, c=c, k0=k0, kn=kn, half=half):
                        e.dma_start(place[:, 0:kn * 256].rearrange("p (k n) -> p k n", k=kn),
                                    vd[:, HALF * half + k0:HALF * half + k0 + kn, 256 * c:256 * c + 256])\
                            .then_inc(sem, 16)
                    pair.append((Chunk(lambda fill=fill: ring.load(fill),
                                       lambda place, kn=kn: fm(place[:, 0:kn * 256], kn)), kn))
                downs += [([(ck, 128 * j, kn) for ck, kn in pair], 128) for j in range(2)]
            linear(downs, lambda k: GH[:, k, 0:N], lambda k: GL[:, k, 0:N], t_g, N, residual(40))
            g_free = fence()
        return t_xw, rdy_wp

    def second(t_x):
        N = 256
        V2 = 2
        M2H = at("M2H", [128, 8, 256], F32R, oG)
        M2L = at("M2L", [128, 8, 256], F32R, oG + 8 * KB)
        o = oG + 16 * KB
        QKM = at("QKM", [128, 8, 259], F32, o)
        QK2 = at("QK2", [128, 8, 256], F32, o + 8320)
        TWO = at("TWO", [128, B_END], F32, o + 16512)
        CS2 = at("CS2", [128, 2, 256], F32, o + 20128)
        GI = at("GI", [4, 256], F32, o + 22176)
        GF = at("GF", [4, 256], F32, o + 23200)
        BG = at("BG", [4, 2], F32, o + 24224)
        SEL = at("SEL", [4, 4, 128], F32, o + 24256)
        QA = at("QA", [128, 4, 256], F32, oZ)
        KA = at("KA", [128, 4, 256], F32, oZ + 4 * KB)
        VA = at("VA", [128, 2, 512], F32, oZ + 8 * KB)
        VM = at("VM", [128, 2, 512], F32, oZ + 12 * KB)
        OM = at("OM", [128, 4, 256], F32, oZ + 16 * KB)
        start = fence()
        s_two = nc.alloc_semaphore("s_two")
        pool.raw(lambda e: e.dma_start(TWO[:, :], A["k_two"]).then_inc(s_two, 16), start)
        for j in range(2):
            pool.raw(lambda e, j=j: e.dma_start(
                BG[:, j:j + 1], A["b_gate_2"][0][4 * j:4 * j + 4].rearrange("(h o) -> h o", o=1)).then_inc(s_two, 16),
                start)
        POSI = at("POSI", [128, 256], I32, o + 8320 + 7168)
        pool.raw(lambda e: e.dma_start(POSI[:, :], A["positions_2"][0].partition_broadcast(128)).then_inc(s_two, 16),
                 start)
        r_two = (s_two, 64)
        ang, nn, rr, rc, mk = (QK2[:, j, :] for j in range(5))
        t = dve(lambda e: e.tensor_copy(ang, POSI[:, :]), r_two, start)
        t = dve(lambda e: e.tensor_scalar(ang, ang, TWO[:, B_FREQ:B_FREQ + 1], None, ALU.mult), t)
        t = dve(lambda e: e.tensor_scalar(nn, ang, float(1 / (2 * np.pi)), 12582912.0, ALU.mult, ALU.add), t)
        t = dve(lambda e: e.tensor_scalar(nn, nn, 12582912.0, None, ALU.subtract), t)
        c1 = 6.28125
        c2 = float(np.float32(np.round((2 * np.pi - c1) * 2 ** 20) / 2 ** 20))
        c3 = float(2 * np.pi - c1 - c2)
        src = ang
        for c in (c1, c2, c3):
            t = dve(lambda e, c=c, src=src: e.scalar_tensor_tensor(rr, nn, -c, src, ALU.mult, ALU.add), t)
            src = rr
        LIM = 3.1415925
        t = dve(lambda e: e.tensor_scalar(rr, rr, LIM, -LIM, ALU.min, ALU.max), t)
        t_sin = act(lambda e: e.activation(CS2[:, 1, :], rr, ACT.Sin), t, start)
        t = dve(lambda e: e.tensor_scalar(rc, rr, float(np.pi / 2), None, ALU.add), t)
        t = dve(lambda e: e.tensor_scalar(mk, rc, float(np.pi), float(-2 * np.pi), ALU.is_gt, ALU.mult), t)
        t = dve(lambda e: e.tensor_tensor(rc, rc, mk, ALU.add), t)
        t = dve(lambda e: e.tensor_scalar(rc, rc, LIM, -LIM, ALU.min, ALU.max), t)
        t_cs = act(lambda e: e.activation(CS2[:, 0, :], rc, ACT.Sin), t)
        t_pad = dve(lambda e: e.memset(QKM[:, :, 0:3], 0.0), start)
        t_sel = [dve(lambda e, h=h: e.tensor_scalar(SEL[:, h, :], ONES[0:4, :], ident[0:4, h:h + 1], None, ALU.mult),
                     start, t_ones, (s_res, 16)) for h in range(4)]
        TB = Buffers(tmp[:7], start)
        t_sg = dve(lambda e: e.scalar_tensor_tensor(
            SG[:, :, 0], MOD[:, 2, 8:16, V2], 1.0, VEC[:, V_N1:V_N1 + 8], ALU.add, ALU.mult), t_mod[2], t_vec, start)
        scales = [((0, 256), lambda k: SG[:, k, 0:1], lambda k: MOD[:, 2, k, V2:V2 + 1], t_sg)]
        xh, xl = lambda k: HH[:, k, 0:N], lambda k: HL[:, k, 0:N]
        t_h = adaln(N, t_x, scales, TB, xh, xl, start)
        zfree = fence()
        chunks = [wide(A["w_in_2"][0], 256 * c, min(256, 3592 - 256 * c)) for c in range(15)]
        tiles = [([(chunks[m // 2], 128 * (m % 2), 8)], 128) for m in range(28)]
        tiles += [([(chunks[14], 4 * j, 8)], 4) for j in range(2)]
        t_qa, t_ka, t_va, t_qk, t_vm, t_om, t_g = ([] for _ in range(7))
        zt2 = [at(f"ZU{j}", [128, 256], F32, oG + KB * j) for j in range(3)]
        ZT = Buffers(zt2, start)

        def rows_of(bank, tp, dst, m, toks):
            tb, bf, fr = ZT.take()
            tc = act(lambda e: e.activation(tb[:, :], bank[:, 0:256], ACT.Copy), tp, bf)
            bank2, before, free2 = PS.take()

            def tr(e):
                for a in range(2):
                    last = e.transpose(bank2[:, 128 * a:128 * a + 128], tb[:, 128 * a:128 * a + 128], ident)
                return last
            tt = pe(tr, tc, before)
            fr.append(tt)
            td = dve(lambda e: e.tensor_copy(dst[:, :, 128 * m:128 * m + 128],
                                             bank2[:, 0:256].rearrange("p (a n) -> p a n", n=128)), tt, zfree)
            free2.append(td)
            toks.append(td)
            return [tc]

        def conv(j, tq):
            out = QK2[:, j, :]
            w = [VEC[:, V_CW + 8 * t + j:V_CW + 8 * t + j + 1] for t in range(4)]
            t1 = dve(lambda e: e.tensor_scalar(out, QKM[:, j, 0:256], w[0], VEC[:, V_CB + j:V_CB + j + 1],
                                               ALU.mult, ALU.add), tq, t_pad, t_cs, t_sin)
            for i in range(1, 4):
                t1 = dve(lambda e, i=i: e.scalar_tensor_tensor(out, QKM[:, j, i:i + 256], w[i], out,
                                                               ALU.mult, ALU.add), t1)
            t1 = act(lambda e: e.activation(out, out, ACT.Silu), t1)
            if j >= 4:
                t1 = dve(lambda e: e.tensor_scalar(out, out, float(128 ** -0.5), None, ALU.mult), t1)
            t_qk.append(t1)

        def evac(i, bank, tp):
            if i < 4:
                t1 = act(lambda e: e.activation(QA[:, i, :], bank[:, 0:256], ACT.Copy, scale=0.125), tp, zfree)
                t_qa.append(t1)
            elif i < 8:
                t1 = act(lambda e: e.activation(KA[:, i - 4, :], bank[:, 0:256], ACT.Copy), tp, zfree)
                t_ka.append(t1)
            elif i < 12:
                return rows_of(bank, tp, VA, i - 8, t_va)
            elif i < 20:
                t1 = dve(lambda e: e.tensor_copy(QKM[:, i - 12, 3:259], bank[:, 0:256]), tp, start)
                conv(i - 12, t1)
            elif i < 24:
                return rows_of(bank, tp, VM, i - 20, t_vm)
            elif i < 28:
                t1 = act(lambda e: e.activation(OM[:, i - 24, :], bank[:, 0:256], ACT.Sigmoid), tp, zfree)
                t_om.append(t1)
            else:
                dst = (GI, GF)[i - 28]
                t1 = dve(lambda e: e.tensor_scalar(dst[:, :], bank[0:4, 0:256], BG[:, i - 28:i - 27], None, ALU.add),
                         tp, r_two)
                t_g.append(t1)
            return [t1]
        linear(tiles, xh, xl, t_h, N, evac)
        hfree = fence()
        MT, PB, PTB = Buffers(mt, hfree), Buffers(pbuf, hfree), Buffers(ptbuf, hfree)
        QRB = at("QRB", [128, 4, 256], F32, oH)
        KRB = at("KRB", [128, 4, 256], F32, oH + 4 * KB)
        t_r = []
        for m in range(4):
            pair = []
            for src, dst, tq in ((QA, QRB, t_qa[m]), (KA, KRB, t_ka[m])):
                bank, before, free = PS.take()
                tp = pe(lambda e, src=src, m=m, bank=bank: e.matmul(
                    bank[:, 0:256], TWO[:, B_R2:B_R2 + 128], src[:, m, :], start=True, stop=True), tq, before, r_two)
                t1, t3 = rope_into(dst[:, m, :], src[:, m, :], bank[:, 0:256], CS2[:, 0, :], CS2[:, 1, :], MT,
                                   [tp, t_cs, t_sin], hfree)
                free.append(t1)
                pair.append(t3)
            t_r.append(pair)
        t_m = [[] for _ in range(8)]

        def gated_out(t, m, t3, fr, gate=None):
            if gate is not None:
                t3 = dve(lambda e: e.tensor_tensor(t[:, 0:256], t[:, 0:256], gate, ALU.mult), t3, t_om)
            th, tl = split_out(t[:, 0:256], M2H[:, m, :], M2L[:, m, :], t3, hfree)
            fr.append(tl)
            t_m[m] += [th, tl]

        def pair_done(p, bank, tp):
            t, bf, fr = MT.take()
            tc = act(lambda e: e.activation(t[:, 0:256], bank[:, 0:256], ACT.Copy), tp, bf)
            t3 = head_norm(t[:, 0:256], 256, VEC[:, V_AG + p:V_AG + p + 1], MT, t[:, 0:256], tc)
            gated_out(t, p, t3, fr)
            return [tc]

        jobs = [{
            "q": lambda a, r=64 * (h % 2), m=h // 2: QRB[r:r + 64, m, 128 * a:128 * a + 128],
            "k": lambda n, r=64 * (h % 2), m=h // 2: KRB[r:r + 64, m, 0:n],
            "v": lambda j, h=h: VA[:, j, 64 * h:64 * h + 64],
            "nk": [1, 2],
            "mask": lambda a: TWO[:, B_TRI + 128 * (1 - a):B_TRI + 256],
            "waits": [t_r[h // 2], t_va],
        } for h in range(8)]
        attention(jobs, PB, PTB, pair_done)
        lfree = fence()
        G4 = at("G4", [4, 8, 256], F32, oH)
        ab, lf, cum, bb, mm_, em, wi, nm = (G4[:, j, :] for j in range(8))
        BC = at("BC", [128, 2, 4], F32, oH + 8 * KB)
        S1 = at("S1", [4, 1], F32, oH + 8 * KB + 64)
        names = ("WT", "QW", "KW", "SWt", "DN")
        WT, QW, KW, SWt, DN = (at(nm_, [128, 4, 256], F32, oH + 9 * KB + 4 * KB * j) for j, nm_ in enumerate(names))
        CNa = at("CNa", [128, 256], F32, oH + 29 * KB)
        CNb = at("CNb", [128, 256], F32, oH + 30 * KB)
        CN = Buffers([CNa, CNb], lfree)
        ones4 = ONES[0:4, 0:128]
        t1 = act(lambda e: e.activation(ab, GF[:, :], ACT.Abs), t_g, lfree)
        t1 = act(lambda e: e.activation(ab, ab, ACT.Exp, scale=-1.0), t1)
        t1 = act(lambda e: e.activation(ab, ab, ACT.Ln, bias=ONES[0:4, 0:1]), t1)
        t1 = dve(lambda e: e.scalar_tensor_tensor(lf, GF[:, :], 0.0, ab, ALU.min, ALU.subtract), t1, t_g)
        ts = [dve(lambda e, c=c: e.tensor_tensor_scan(cum[:, 128 * c:128 * c + 128], ones4,
                                                      lf[:, 128 * c:128 * c + 128], 0.0, ALU.mult, ALU.add), t1)
              for c in range(2)]
        tb_ = dve(lambda e: e.tensor_tensor(bb, GI[:, :], cum, ALU.subtract), ts, t_g)
        t2 = dve(lambda e: e.tensor_tensor_scan(mm_[:, 0:128], bb[:, 0:128], bb[:, 0:128], 0.0, ALU.max, ALU.max), tb_)
        tm0 = dve(lambda e: e.tensor_tensor(S1[:, :], cum[:, 127:128], mm_[:, 127:128], ALU.add), t2)
        t3 = dve(lambda e: e.tensor_tensor_scan(mm_[:, 128:256], bb[:, 128:256], bb[:, 128:256], S1[:, 0:1],
                                                ALU.max, ALU.max), tm0)
        tn_ = dve(lambda e: e.tensor_scalar(nm, mm_, -1.0, None, ALU.mult), t3)
        te = dve(lambda e: e.tensor_tensor(em, cum, mm_, ALU.add), t3)
        te = act(lambda e: e.activation(em, em, ACT.Exp, scale=-1.0), te)
        tw = act(lambda e: e.activation(wi[:, 0:128], mm_[:, 128:256], ACT.Exp, bias=S1[:, 0:1], scale=-1.0), t3)
        bank, before, free = PS.take()

        def tr(e, bank=bank):
            for c in range(2):
                last = e.transpose(bank[:, 4 * c:4 * c + 4], bb[:, 128 * c:128 * c + 128], ident[0:4, 0:4])
            return last
        tp = pe(tr, tb_, before)
        t_bc = dve(lambda e, bank=bank: e.tensor_copy(BC[:, :, :], bank[:, 0:8].rearrange("p (c h) -> p c h", c=2)),
                   tp, lfree)
        free.append(t_bc)
        t_wt, t_qw, t_kw = [], [], []
        for h in range(4):
            bank, before, free = PS.take()
            tp = pe(lambda e, h=h, bank=bank: e.matmul(bank[:, 0:256], SEL[:, h, :], nm, start=True, stop=True),
                    tn_, t_sel, before)
            t1 = dve(lambda e, h=h, bank=bank: e.tensor_tensor(
                WT[:, h, :].rearrange("p (c n) -> p c n", c=2), bank[:, 0:256].rearrange("p (c n) -> p c n", c=2),
                TWO[:, B_TRIT:B_TRIT + 128].unsqueeze(1).to_broadcast([128, 2, 128]), ALU.add), tp, lfree)
            free.append(t1)
            w2_ = [act(lambda e, h=h, c=c: e.activation(WT[:, h, 128 * c:128 * c + 128], WT[:, h, 128 * c:128 * c + 128],
                                                        ACT.Exp, bias=BC[:, c, h:h + 1]), t1, t_bc) for c in range(2)]
            t_wt.append(w2_)
            bank, before, free = PS.take()
            tp = pe(lambda e, h=h, bank=bank: e.matmul(bank[:, 0:128], SEL[:, h, :], wi[:, 0:128],
                                                       start=True, stop=True), tw, before)
            t1 = dve(lambda e, h=h, bank=bank: e.tensor_tensor(QW[:, h, 0:128], QK2[:, h, 128:256], bank[:, 0:128],
                                                               ALU.mult), tp, t_qk, lfree)
            free.append(t1)
            t_qw.append(t1)
            bank, before, free = PS.take()
            tp = pe(lambda e, h=h, bank=bank: e.transpose(bank[:, 0:128], QK2[:, 4 + h, 0:128], ident), t_qk, before)
            t1 = dve(lambda e, h=h, bank=bank: e.tensor_scalar(KW[:, h, 0:128], bank[:, 0:128], WT[:, h, 127:128], None,
                                                               ALU.mult), tp, w2_, lfree)
            free.append(t1)
            t_kw.append(t1)
        for h in range(4):
            bank, before, free = PS.take()

            def st_mm(e, h=h, bank=bank):
                e.matmul(bank[:, 0:128], KW[:, h, 0:128], VM[:, 0, 128 * h:128 * h + 128], start=True, stop=True)
                return e.matmul(bank[:, 128:256], KW[:, h, 0:128], ONES[:, :], start=True, stop=True)
            tp = pe(st_mm, t_kw[h], t_vm, before)
            cn, bf, fr_cn = CN.take()
            t_cn = act(lambda e, cn=cn, bank=bank: e.activation(cn[:, :], bank[:, 0:256], ACT.Copy), tp, bf)
            free.append(t_cn)
            bank, before, free = PS.take()

            def s_mm(e, h=h, bank=bank):
                for c in range(2):
                    sl = slice(128 * c, 128 * c + 128)
                    last = e.matmul(bank[:, sl], QK2[:, 4 + h, sl], QK2[:, h, sl], start=True, stop=True)
                return last
            tp = pe(s_mm, t_qk, before)
            t_s = dve(lambda e, h=h, bank=bank: e.tensor_tensor(SWt[:, h, :], bank[:, 0:256], WT[:, h, :], ALU.mult),
                      tp, t_wt[h], lfree)
            free.append(t_s)
            bn, before, free_n = PS.take()
            bd_, before2, free_d = PS.take()

            def n_mm(e, h=h, bn=bn, bd_=bd_, cn=cn):
                for bk, lhs, st_ in ((bn, lambda c: VM[:, c, 128 * h:128 * h + 128], cn[:, 0:128]),
                                     (bd_, lambda c: ONES[:, :], cn[:, 128:256])):
                    e.matmul(bk[:, 0:128], lhs(0), SWt[:, h, 0:128], start=True, stop=True)
                    e.matmul(bk[:, 128:256], lhs(1), SWt[:, h, 128:256], start=True, stop=False)
                    last = e.matmul(bk[:, 128:256], st_, QW[:, h, 0:128], start=False, stop=True)
                return last
            tp = pe(n_mm, t_s, t_cn, t_qw[h], t_vm, before, before2)
            fr_cn.append(tp)
            be, before, free_e = PS.take()
            tpe = pe(lambda e, h=h, be=be: e.matmul(be[:, 0:256], SEL[:, h, :], em, start=True, stop=True), te, before)
            d = DN[:, h, :]
            t1 = act(lambda e, d=d, bd_=bd_: e.activation(d, bd_[:, 0:256], ACT.Abs), tp, lfree)
            free_d.append(t1)
            t1 = dve(lambda e, d=d, be=be: e.tensor_tensor(d, be[:, 0:256], d, ALU.max), t1, tpe)
            free_e.append(t1)
            t1 = dve(lambda e, d=d: e.reciprocal(d, d), t1)
            t1 = dve(lambda e, d=d, bn=bn: e.tensor_tensor(d, bn[:, 0:256], d, ALU.mult), t1, tp)
            free_n.append(t1)
            sq = Buffers([SWt[:, h, :]], [tp])
            t3 = head_norm(d, 256, VEC[:, V_MG + h:V_MG + h + 1], sq, d, t1, mean=1.0 / 128, red=ONES[:, :])
            gated_out(DN[:, h, :], 4 + h, t3, [], gate=OM[:, h, :])
        t_xw = [[t, fence()] for t in t_x]

        def residual2(i, bank, tp):
            t1 = dve(lambda e: e.scalar_tensor_tensor(XT[:, i, 0:256], bank[:, 0:256], MOD[:, 2, 16 + i, V2:V2 + 1],
                                                      XT[:, i, 0:256], ALU.mult, ALU.add), tp, t_xw[i])
            t_xw[i] = [t1]
            return [t1]
        chunks_o = [wide(A["w_out_2"][0], 256 * c, 256) for c in range(4)]
        linear([([(chunks_o[m // 2], 128 * (m % 2), 8)], 128) for m in range(8)],
               lambda k: M2H[:, k, :], lambda k: M2L[:, k, :], t_m, N, residual2)
        t_dense = fence()
        H2 = at("H2", [128, 8, 256], F32, o)
        WR = at("WR", [128, 8, 36], F32, oZ + 16 * KB)
        RB = at("RB", [128, 36], F32, oZ + 16 * KB + 1152)
        s_wr = nc.alloc_semaphore("s_wr")
        for c0, n, wn, bn_ in ((0, 4, "w_rg_2", "b_rg_2"), (4, 32, "w_re_2", "b_re_2")):
            pool.raw(lambda e, c0=c0, n=n, wn=wn: e.dma_start(
                WR[:, :, c0:c0 + n], A[wn][0].rearrange("(k p) n -> p k n", p=128)).then_inc(s_wr, 16), lfree, t_m[7])
            pool.raw(lambda e, c0=c0, n=n, bn_=bn_: e.dma_start(
                RB[:, c0:c0 + n], A[bn_][0].partition_broadcast(128)).then_inc(s_wr, 16))
        TB = Buffers(tmp[:7], t_dense)
        t_sg = dve(lambda e: e.scalar_tensor_tensor(
            SG[:, :, 0], MOD[:, 2, 32:40, V2], 1.0, VEC[:, V_N2:V_N2 + 8], ALU.add, ALU.mult), t_dense)
        scales = [((0, 256), lambda k: SG[:, k, 0:1], lambda k: MOD[:, 2, 24 + k, V2:V2 + 1], t_sg)]
        t_h2 = adaln(N, t_xw, scales, TB, None, None, t_dense, keep=lambda k: H2[:, k, :])
        rfree = fence()
        rt = at("RT", [128, 1800], F32, oZ)
        off = [0]

        def small(*shape):
            n = int(np.prod(shape))
            ap = rt[:, off[0]:off[0] + n]
            off[0] += n
            if len(shape) == 2:
                ap = ap.rearrange("p (a b) -> p a b", a=shape[0])
            elif len(shape) == 3:
                ap = ap.rearrange("p (a b c) -> p a b c", a=shape[0], b=shape[1])
            return ap
        LG, G8, MX, MXE = small(2, 36), small(2, 8), small(2, 8), small(2, 8)
        IX, IXE = small(2, 8), small(2, 8)
        EG, GW, GIF, OG, EP, E8 = small(2, 4), small(2), small(2), small(2, 4), small(2, 32), small(2, 8)
        R1, RD, WGT, IDF = small(2), small(2), small(2, 2), small(2, 2)
        AA, A01, PR, PC = small(4, 32), small(2, 32), small(4, 32), small(96)
        PP, S0, S1b, BIG, GS, BLK, POS = (small(4) for _ in range(7))
        IND, XI, TX, BS, TJ, EIA = small(32), small(32), small(32), small(2, 32), small(32), small(16)
        GB, PM, iota2 = small(4, N_BLOCKS), small(N_BLOCKS), small(128)
        WS_ = small(N_BLOCKS)
        INTS = at("INTS", [128, 16], I32, oZ + 8128)
        bank, before, free = PS.take()

        def lg(e, bank=bank):
            for a in range(2):
                for k in range(KT):
                    last = e.matmul(bank[:, 36 * a:36 * a + 36], H2[:, k, 128 * a:128 * a + 128], WR[:, k, :],
                                    start=(k == 0), stop=(k == KT - 1))
            return last
        tp = pe(lg, t_h2, (s_wr, 64), before)
        dq = [None]

        def d(fn, *w):
            dq[0] = dve(fn, dq[0], *w)
            return dq[0]
        bank_lg = bank
        t = d(lambda e: e.tensor_tensor(LG, bank_lg[:, 0:72].rearrange("p (a n) -> p a n", a=2),
                                        RB[:, :].unsqueeze(1).to_broadcast([128, 2, 36]), ALU.add), tp, rfree)
        free.append(t)
        d(lambda e: e.memset(G8, -3.0e38))
        d(lambda e: e.tensor_copy(G8[:, :, 0:4], LG[:, :, 0:4]))

        def top(src, mx, ix):
            for a in range(2):
                d(lambda e, a=a: e.max(mx[:, a, :], src[:, a, :]))
                d(lambda e, a=a: e.max_index(ix[:, a, :].bitcast(U32), mx[:, a, :], src[:, a, :]))
        top(G8, MX, IX)
        d(lambda e: e.tensor_copy(GIF, IX[:, :, 0].bitcast(U32)))
        t = d(lambda e: e.tensor_tensor(EG, LG[:, :, 0:4], MX[:, :, 0:1].to_broadcast([128, 2, 4]), ALU.subtract))
        t = act(lambda e: e.activation(EG, EG, ACT.Exp), t)
        iota = TWO[:, B_IOTA:B_IOTA + 128]
        d(lambda e: e.tensor_tensor(OG, iota[:, 0:4].unsqueeze(1).to_broadcast([128, 2, 4]),
                                    GIF.unsqueeze(2).to_broadcast([128, 2, 4]), ALU.is_equal))
        for a in range(2):
            d(lambda e, a=a: e.tensor_tensor(
                EP[:, a, :].rearrange("p (j g) -> p j g", g=4),
                LG[:, a, 4:36].rearrange("p (g j) -> p j g", g=4),
                OG[:, a, :].unsqueeze(1).to_broadcast([128, 8, 4]), ALU.mult))
        d(lambda e: e.tensor_reduce(E8, EP.rearrange("p a (j g) -> p a j g", g=4), AX.X, ALU.add))
        top(E8, MXE, IXE)
        d(lambda e: e.tensor_reduce(GW, EG, AX.X, ALU.add), t)
        d(lambda e: e.reciprocal(GW, GW))
        t = d(lambda e: e.tensor_tensor(R1, MXE[:, :, 1], MXE[:, :, 0], ALU.subtract))
        t = act(lambda e: e.activation(R1, R1, ACT.Exp), t)
        d(lambda e: e.tensor_copy(IDF, IXE[:, :, 0:2].bitcast(U32)))
        d(lambda e: e.scalar_tensor_tensor(IDF, GIF.unsqueeze(2).to_broadcast([128, 2, 2]), 8.0, IDF,
                                           ALU.mult, ALU.add))
        d(lambda e: e.tensor_tensor(AA, iota[:, 0:32].unsqueeze(1).to_broadcast([128, 4, 32]),
                                    IDF.rearrange("p a k -> p (a k)").unsqueeze(2).to_broadcast([128, 4, 32]),
                                    ALU.is_equal))
        A4 = AA.rearrange("p (a k) n -> p a k n", a=2)
        t_a = d(lambda e: e.tensor_tensor(A01, A4[:, :, 0, :], A4[:, :, 1, :], ALU.add))
        bank2, before, free2 = PS.take()

        def cnt(e):
            slt = TWO[:, B_SLT:B_SLT + 128]
            e.matmul(bank2[:, 0:32], slt, A01[:, 0, :], start=True, stop=True)
            e.matmul(bank2[:, 32:64], slt, A01[:, 1, :], start=True, stop=False)
            e.matmul(bank2[:, 32:64], ONES[:, :], A01[:, 0, :], start=False, stop=True)
            e.matmul(bank2[:, 64:96], ONES[:, :], A01[:, 0, :], start=True, stop=False)
            return e.matmul(bank2[:, 64:96], ONES[:, :], A01[:, 1, :], start=False, stop=True)
        tp = pe(cnt, t_a, before)
        d(lambda e: e.tensor_scalar(RD, R1, 1.0, None, ALU.add), t)
        d(lambda e: e.reciprocal(RD, RD))
        d(lambda e: e.tensor_tensor(WGT[:, :, 0], GW, RD, ALU.mult))
        t_wgt = d(lambda e: e.tensor_tensor(WGT[:, :, 1], WGT[:, :, 0], R1, ALU.mult))
        free2.append(d(lambda e: e.tensor_copy(PC, bank2[:, 0:96]), tp))
        d(lambda e: e.tensor_scalar(IND, PC[:, 64:96], float(CAP), None, ALU.is_gt))
        for j in (2, 3):
            d(lambda e, j=j: e.scalar_tensor_tensor(IND, PC[:, 64:96], float(j * CAP), IND, ALU.is_gt, ALU.add))
        d(lambda e: e.tensor_tensor_scan(TX, ONES[:, 0:32], IND, 0.0, ALU.mult, ALU.add))
        d(lambda e: e.tensor_copy(EIA[:, 14:15], TX[:, 31:32]))
        d(lambda e: e.tensor_tensor(XI, TX, IND, ALU.subtract))
        d(lambda e: e.tensor_copy(BS[:, 0, :], iota[:, 0:32]))
        d(lambda e: e.tensor_scalar(BS[:, 1, :], XI, float(N_EXP - 1), None, ALU.add))
        for j in range(N_EXTRA):
            d(lambda e, j=j: e.tensor_scalar(TJ, XI, float(j), None, ALU.is_le))
            d(lambda e, j=j: e.scalar_tensor_tensor(TJ, TX, float(j), TJ, ALU.is_gt, ALU.mult))
            d(lambda e, j=j: e.tensor_tensor(TJ, TJ, iota[:, 0:32], ALU.mult))
            d(lambda e, j=j: e.tensor_reduce(EIA[:, j:j + 1], TJ, AX.X, ALU.add))
            d(lambda e, j=j: e.tensor_scalar(EIA[:, 7 + j:8 + j], EIA[:, 14:15], float(j), None, ALU.is_gt))
        t_ints = d(lambda e: e.tensor_copy(INTS[:, 0:15], EIA[:, 0:15]))
        for src, dst in ((PC[:, 0:64].rearrange("p (a n) -> p a n", a=2).unsqueeze(2).to_broadcast([128, 2, 2, 32]), PP),
                         (BS[:, 0, :].unsqueeze(1).to_broadcast([128, 4, 32]), S0),
                         (BS[:, 1, :].unsqueeze(1).to_broadcast([128, 4, 32]), S1b)):
            a_ = AA if src.ndim == 3 else A4
            p_ = PR if src.ndim == 3 else PR.rearrange("p (a k) n -> p a k n", a=2)
            d(lambda e, src=src, a_=a_, p_=p_: e.tensor_tensor(p_, a_, src, ALU.mult))
            d(lambda e, dst=dst: e.tensor_reduce(dst, PR, AX.X, ALU.add))
        d(lambda e: e.tensor_scalar(BIG, PP, float(CAP), None, ALU.is_ge))
        d(lambda e: e.tensor_tensor(S1b, S1b, S0, ALU.subtract))
        d(lambda e: e.tensor_tensor(S1b, S1b, BIG, ALU.mult))
        for j in (2, 3):
            d(lambda e, j=j: e.scalar_tensor_tensor(BIG, PP, float(j * CAP), BIG, ALU.is_ge, ALU.add))
        d(lambda e: e.scalar_tensor_tensor(POS, BIG, float(-CAP), PP, ALU.mult, ALU.add))
        d(lambda e: e.tensor_tensor(BLK, S0, S1b, ALU.add))
        d(lambda e: e.tensor_tensor(BLK, BLK, BIG, ALU.add))
        d(lambda e: e.scalar_tensor_tensor(GS, BLK, float(CAP), POS, ALU.mult, ALU.add))
        for q in range(4):
            d(lambda e, q=q: e.tensor_scalar(GB[:, q, :], iota[:, 0:N_BLOCKS], float(-CAP), GS[:, q:q + 1],
                                             ALU.mult, ALU.add))
        bmod = TWO[:, B_MOD:B_MOD + 128]
        bank3, before3, free3 = PS.take()
        tp = pe(lambda e: e.transpose(bank3[:, 0:128], bmod, ident), before3, r_two)
        free3.append(d(lambda e: e.tensor_scalar(PM, iota[:, 0:N_BLOCKS], float(CAP), bank3[:, 0:1], ALU.mult, ALU.add),
                       tp))
        d(lambda e: e.tensor_copy(iota2, iota))
        PW = at("PW", [128, 4, 128], F32, oZ + 8 * KB + 512)
        QW2 = at("QW2", [128, 4, N_BLOCKS], F32, oZ + 10 * KB + 512)
        DG = at("DG", [128, 4, 128], F32, oZ + 11 * KB + 512)
        GSR = at("GSR", [128, 2, 256], F32, oZ + 14 * KB)
        for q in range(4):
            d(lambda e, q=q: e.tensor_scalar(PW[:, q, :], bmod, POS[:, q:q + 1], None, ALU.is_equal))
            d(lambda e, q=q: e.tensor_scalar(QW2[:, q, :], iota[:, 0:N_BLOCKS], BLK[:, q:q + 1], WGT[:, q // 2, q % 2:q % 2 + 1],
                                             ALU.is_equal, ALU.mult))
            t_dg = d(lambda e, q=q: e.tensor_scalar(DG[:, q, :], ident, GS[:, q:q + 1], None, ALU.mult))
        bank4, before4, free4 = PS.take()
        bank5, before5, free5 = PS.take()

        def slots(e):
            for q in range(4):
                e.matmul(bank4[:, 0:N_BLOCKS], PW[:, q, :], QW2[:, q, :], start=(q == 0), stop=(q == 3))
            for q in range(4):
                c = 256 * (q % 2) + 128 * (q // 2)
                last = e.matmul(bank5[:, c:c + 128], ONES[:, :], DG[:, q, :], start=True, stop=True)
            return last
        tp = pe(slots, t_dg, before4, before5)
        free4.append(d(lambda e: e.tensor_copy(WS_, bank4[:, 0:N_BLOCKS]), tp))
        t_gb = d(lambda e: e.tensor_copy(GSR[:, :, :], bank5[:, :].rearrange("p (k n) -> p k n", k=2)), tp)
        free5.append(t_gb)
        H2P = at("H2P", [128, 3, 2, 1024], BF16, oG + 24 * KB)
        HR = Buffers([at(f"HR{i}", [128, 512], F32, oZ + 16 * KB + 2 * KB * i) for i in range(2)], [rfree, t_gb])
        t_h2p = []
        for a in range(2):
            for hf in range(2):
                bank, before, free = PS.take()

                def tr(e, a=a, hf=hf, bank=bank):
                    for k in range(4):
                        last = e.transpose(bank[:, 128 * k:128 * k + 128], H2[:, 4 * hf + k, 128 * a:128 * a + 128], ident)
                    return last
                tp = pe(tr, t_h2, before)
                sl = slice(512 * hf, 512 * hf + 512)
                r, bf, fr = HR.take()
                t1 = act(lambda e, a=a, sl=sl, bank=bank: e.activation(H2P[:, 0, a, sl], bank[:, :], ACT.Copy), tp, rfree, t_gb)
                t2 = dve(lambda e, a=a, sl=sl, bank=bank, r=r: e.tensor_tensor(r[:, :], bank[:, :], H2P[:, 0, a, sl],
                                                                               ALU.subtract), t1, tp, bf)
                free.append(t2)
                t3 = act(lambda e, a=a, sl=sl, r=r: e.activation(H2P[:, 1, a, sl], r[:, :], ACT.Copy), t2, t_gb)
                t4 = dve(lambda e, a=a, sl=sl, r=r: e.tensor_tensor(H2P[:, 2, a, sl], r[:, :], H2P[:, 1, a, sl],
                                                                    ALU.subtract), t3)
                fr.append(t4)
                t_h2p += [t1, t3, t4]
        xg_at = [at(f"XG{i}", [128, 8, 128], F32R, oG + 4 * KB * i) for i in range(2)]
        st_at = [at(f"ST{i}", [128, 256], F32R, oG + 8 * KB + KB * i) for i in range(4)]
        STT = at("STT", [128, 2, 256], F32, oG + 12 * KB)
        ZERO = at("ZERO", [128, 128], BF16, oG + 14 * KB)
        SBT = at("SBT", [128, 4, 64], BF16, oG + 14 * KB + 256)
        sb_at = [at(f"SB{i}", [128, 2, 64], BF16, oG + 14 * KB + 768 + 256 * i) for i in range(2)]
        sm_at = [at(f"SM{i}", [128, 4, 64], F32, oZ + 9 * KB + KB * i) for i in range(2)]
        u_at = [at(f"U{i}", [128, 512], F32, oG + 16 * KB + 2 * KB * i) for i in range(4)]
        gg_at = [at(f"GG{i}", [128, 4, 128], F32R, oG + 36 * KB + 2 * KB * i) for i in range(2)]
        y_at = [(at(f"YH{i}", [128, 512], F32R, oG + 40 * KB + 2 * KB * i),
                       at(f"YL{i}", [128, 512], F32R, oZ + 16 * KB + 2 * KB * i)) for i in range(2)]
        wm_at = [(at(f"MH{i}", [128, 1024], F32R, o_), at(f"ML{i}", [128, 1024], F32R, o_ + 4 * KB))
                      for i, o_ in enumerate([oH + 8 * KB * j for j in range(4)] + [oW, oW + 8 * KB])]
        w_src = (A["w1_2"][0], A["w3_2"][0], A["w2_2"][0])
        acc, acc_before = banks[0:4], [list(f) for f in PS.free[0:4]]
        t_zero = pool(lambda e: e.memset(ZERO[:, :], 0.0), t_dense)

        def clear(e):
            for bk in acc:
                last = e.matmul(bk[:, :], ZERO[:, :], H2P[:, 0, 0, 0:512], start=True, stop=False)
            return last
        t_clear = pe(clear, t_zero, t_h2p, acc_before)

        def blocks(base, n_blocks, pe, act, dve, pool, ring, bank_free):
            XGB, STB, SB_, SMB, GGB, WM = (Buffers(p, t_dense) for p in (xg_at, st_at, sb_at, sm_at, gg_at, wm_at))
            for f in SMB.free:
                f.append(t_gb)
            UB, YB = Buffers(u_at, [t_dense, t_h2p]), Buffers(y_at, [t_dense, t_h2p])
            PE4 = Buffers(banks[4:8])
            PE4.free = [list(f) for f in bank_free]

            def expert_loads(which, extra):
                regs = {}

                def fill(j):
                    src, k = w_src[j // 2], j % 2
                    n = 512 if j < 4 else 1024
                    kn = 2048 // n

                    def f(e, place, sem):
                        dst = place[:, :].rearrange("p (k n) -> p k n", k=kn)
                        if not extra:
                            e.dma_start(dst, src[which].rearrange("(k p) n -> p k n", p=128)[:, kn * k:kn * k + kn, :])\
                                .then_inc(sem, 16)
                            return
                        if j == 0:
                            e.wait_ge(*t_ints)
                            regs["e"] = e.value_load(INTS[0:1, which:which + 1], min_val=0, max_val=N_EXP - 1)
                            regs["on"] = e.value_load(INTS[0:1, 7 + which:8 + which], min_val=0, max_val=1)
                        v = src[bass.ds(regs["e"], 1)].rearrange("a (k p) n -> p (a k) n", p=128)
                        e.dma_start(dst, v[:, kn * k:kn * k + kn, :], cond=regs["on"]).then_inc(sem, 16)
                    return f
                return [fill(j) for j in range(6)]

            def places(b):
                S, bf, fr_s = SB_.take()
                t1 = dve(lambda e: e.tensor_tensor(SBT[:, :, :], iota2[:, 0:64].unsqueeze(1).to_broadcast([128, 4, 64]),
                                                    GB[:, :, b:b + 1].to_broadcast([128, 4, 64]), ALU.is_equal),
                          t_gb, pool.last())
                v = SBT[:, :, :].rearrange("p (a k) n -> p a k n", k=2)
                t_s = pool(lambda e: e.tensor_tensor(S[:, :, :], v[:, :, 0, :], v[:, :, 1, :], ALU.add), t1, bf)
                ST, bf, fr_st = STB.take()
                t1 = pool(lambda e: e.tensor_scalar(STT[:, :, :], GSR[:, :, :], PM[:, b:b + 1], None, ALU.is_equal),
                          t_s)
                t_st = pool(lambda e: e.tensor_tensor(ST[:, :], STT[:, 0, :], STT[:, 1, :], ALU.add), t1, bf)
                return S, t_s, fr_s, ST, t_st, fr_st

            def gather(S, t_s, fr_s):
                xg, bf, fr = XGB.take()
                bank, before, free = PE4.take()

                def mm(e):
                    for k in range(8):
                        for a in range(2):
                            for q in range(3):
                                last = e.matmul(bank[:, 64 * k:64 * k + 64], H2P[:, q, a, 128 * k:128 * k + 128],
                                                S[:, a, :], start=(a == 0 and q == 0), stop=(a == 1 and q == 2))
                    return last
                tp = pe(mm, t_s, t_h2p, before)
                fr_s.append(tp)
                v = bank[:, :].rearrange("p (k n) -> p k n", k=8)
                t1 = act(lambda e: e.activation(xg[:, :, 0:64], v, ACT.Copy), tp, bf)
                t2 = dve(lambda e: e.tensor_tensor(xg[:, :, 64:128], v, xg[:, :, 0:64].bitcast(F32), ALU.subtract),
                         t1, tp, bf)
                free.append(t2)
                return xg, [t1, t2], fr

            n_part = [0]

            def part_of(item, u):
                (wh, wl), bf, fr = WM.take()
                src = item.place[:, 1024 * u:1024 * u + 1024]
                th = act(lambda e: e.activation(wh[:, :], src, ACT.Copy), item.ready, bf)
                n_part[0] += 1
                eng = pool if n_part[0] % 4 == 0 else dve
                tl = eng(lambda e: e.tensor_tensor(wl[:, :], src, wh[:, :].bitcast(F32), ALU.subtract),
                         item.ready, bf, th)
                item.done.append(tl)
                return wh, wl, th, tl, fr

            AHEAD = 5
            fills, ready = [], []

            def part():
                while fills and len(ready) <= AHEAD:
                    item = ring.load(fills.pop(0))
                    ready.extend([part_of(item, 0), part_of(item, 1)])
                return ready.pop(0)

            def up_half(xg, toks, mid=None):
                bank, before, free = PE4.take()
                for q in range(4):
                    wh, wl, th, tl, fr = part()

                    def mm(e, q=q, w=wh, lo=0):
                        for j in range(2):
                            k = 2 * q + j
                            last = e.matmul(bank[:, :], xg[:, k, :], w[:, 512 * j:512 * j + 512], start=(k == 0 and not lo),
                                            stop=(k == 7 and lo == 1))
                        return last
                    pe(mm, toks, th, before)
                    tp = pe(lambda e, q=q, w=wl, f=mm: f(e, q, w, 1), tl)
                    fr.append(tp)
                    if q == 1 and mid is not None:
                        mid()
                U, bf, fr_u = UB.take()
                tu = act(lambda e: e.activation(U[:, :], bank[:, :], ACT.Copy), tp, bf)
                free.append(tu)
                return U, tu, fr_u

            def turned(U, tu, fr_u):
                bank, before, free = PE4.take()

                def tr(e):
                    for k in range(4):
                        last = e.transpose(bank[:, 128 * k:128 * k + 128], U[:, 128 * k:128 * k + 128], ident)
                    return last
                tp = pe(tr, tu, before)
                fr_u.append(tp)
                v = bank[:, :].rearrange("p (k n) -> p k n", k=4)
                s_, bf, fr = SMB.take()
                t1 = act(lambda e: e.activation(s_[:, :, :], v[:, :, 0:64], ACT.Copy), tp, bf)
                t2 = dve(lambda e: e.tensor_tensor(s_[:, :, :], v[:, :, 64:128], s_[:, :, :], ALU.add), t1)
                free.append(t2)
                return s_, t2, fr

            def hidden(g, u):
                s1, t1, f1 = g
                s3, t3, f3 = u
                ta = act(lambda e: e.activation(s1[:, :, :], s1[:, :, :], ACT.Silu), t1)
                tm = dve(lambda e: e.tensor_tensor(s1[:, :, :], s1[:, :, :], s3[:, :, :], ALU.mult), ta, t3)
                f3.append(tm)
                gg, bf, fr = GGB.take()
                th = act(lambda e: e.activation(gg[:, :, 0:64], s1[:, :, :], ACT.Copy), tm, bf)
                tl = dve(lambda e: e.tensor_tensor(gg[:, :, 64:128], s1[:, :, :], gg[:, :, 0:64].bitcast(F32), ALU.subtract),
                         th, bf)
                f1.append(tl)
                return gg, [th, tl], fr

            def down_half(b, gg, toks, fr_g, mid=None):
                two_banks = [PE4.take() for _ in range(2)]
                for k in range(4):
                    wh, wl, th, tl, fr = part()

                    def mm(e, k=k, w=wh, lo=0):
                        for j in range(2):
                            last = e.matmul(two_banks[j][0][:, :], gg[:, k, :], w[:, 512 * j:512 * j + 512],
                                            start=(k == 0 and not lo), stop=(k == 3 and lo == 1))
                        return last
                    pe(mm, toks, th, [t[1] for t in two_banks])
                    tp = pe(lambda e, k=k, w=wl, f=mm: f(e, k, w, 1), tl)
                    fr.append(tp)
                    if k == 1 and mid is not None:
                        mid()
                fr_g.append(tp)
                out = []
                for bk, _, free in two_banks:
                    (yh, yl), bf, fr = YB.take()
                    t1 = act(lambda e, yh=yh, bk=bk: e.activation(yh[:, :], bk[:, :], ACT.Copy, scale=WS_[:, b:b + 1]), tp, bf)
                    t2 = dve(lambda e, yh=yh, yl=yl, bk=bk: e.scalar_tensor_tensor(
                        yl[:, :], bk[:, :], WS_[:, b:b + 1], yh[:, :].bitcast(F32), ALU.mult, ALU.subtract), t1, bf)
                    free.append(t2)
                    out.append((yh, yl, t2, fr))
                return out

            def give_back(ys, ST, t_st, fr_st):
                for j, (yh, yl, ty, fr) in enumerate(ys):
                    def mm(e, j=j, yh=yh, yl=yl):
                        for k in range(4):
                            bk = acc[2 * j + k // 2][:, 256 * (k % 2):256 * (k % 2) + 256]
                            for y in (yh, yl):
                                last = e.matmul(bk, y[:, 128 * k:128 * k + 128], ST[:, :], start=False, stop=False)
                        return last
                    tp = pe(mm, ty, t_st, t_clear)
                    fr.append(tp)
                fr_st.append(tp)

            n_b = n_blocks
            all_fills = [expert_loads(j, base > 0) for j in range(n_b)]
            for i in range(n_b + 1):
                if i < n_b:
                    fills += all_fills[i][0:4]
                if i:
                    fills += all_fills[i - 1][4:6]
            pls, xgs, hid, ys = {0: places(base)}, {}, {}, {}
            xgs[0] = gather(*pls[0][0:3])

            def back(j):
                if j >= 0:
                    give_back(ys.pop(j), *pls.pop(j)[3:])

            for i in range(n_b + 1):
                if i < n_b:
                    xg, toks, fr_x = xgs.pop(i)
                    if i + 1 < n_b:
                        pls[i + 1] = places(base + i + 1)
                    g1 = up_half(xg, toks)
                    u1 = up_half(xg, toks, lambda: back(i - 2))
                    fr_x.append(pe.last())
                    if i + 1 < n_b:
                        xgs[i + 1] = gather(*pls[i + 1][0:3])
                    t1 = turned(*g1)
                else:
                    back(i - 2)

                def mid():
                    if i < n_b:
                        hid[i] = hidden(t1, turned(*u1))
                if i:
                    ys[i - 1] = down_half(base + i - 1, *hid.pop(i - 1), mid)
                else:
                    mid()
            back(n_b - 1)

        blocks(0, N_EXP, pe, act, dve, pool, ring, PS.free[4:8])
        done = fence()
        subs = [Engine(nc.alloc_semaphore(f"s_x{n}")) for n in ("pe", "act", "dve", "pool", "sp")]
        xsems = [nc.alloc_semaphore(f"s_xr{i}") for i in range(8)]
        xcounts = [0] * 8
        s_join = nc.alloc_semaphore("s_join")
        blocks(N_EXP, N_EXTRA, *subs[:4], Ring(subs[4], ring_slots, xsems, xcounts, [[] for _ in range(8)]), [[]] * 4)

        def maybe(sub, ends):
            def f(e):
                more = e.value_load(INTS[0:1, 14:15], min_val=0, max_val=N_EXTRA)
                with e.If(more > 0):
                    sub.emit(e)
                    for s_, n_ in ends:
                        e.wait_ge(s_, n_)
                    e.sem_inc(s_join, 1)
                with e.Else():
                    e.sem_inc(s_join, 1)
            return f
        for eng, sub in zip((pe, act, dve, pool, sp), subs):
            eng.raw(maybe(sub, [sub.last()] if sub.n else list(zip(xsems, xcounts))), t_ints, done)
        joined = (s_join, 5)

        def close(e):
            for bk in acc:
                last = e.matmul(bk[:, :], ZERO[:, :], H2P[:, 0, 0, 0:512], start=False, stop=True)
            return last
        pe(close, joined)
        done = fence() + [joined]
        PS.free = [list(done) for _ in range(8)]
        t_xf = []
        for k in range(KT):
            t1 = dve(lambda e, k=k: e.scalar_tensor_tensor(
                XT[:, k, 0:256], acc[k // 2][:, 256 * (k % 2):256 * (k % 2) + 256], MOD[:, 2, 40 + k, V2:V2 + 1],
                XT[:, k, 0:256], ALU.mult, ALU.add), done)
            t_xf.append(t1)
        for f in PS.free:
            f.append(t1)
        TB = Buffers(tmp[:7], done)
        OUT = at("OUT", [128, 2, 1024], F32, oR + 24 * KB)
        bank_s, before, free_s = PS.take()
        for k in range(KT):
            sq, bf, fr = TB.take()
            ts = act(lambda e, k=k, sq=sq: e.activation(sq[:, 0:N], XT[:, k, 0:N], ACT.Square), t_xf[k], bf)
            tp = pe(lambda e, k=k, sq=sq: e.matmul(bank_s[:, 0:N], ONES[:, :], sq[:, 0:N],
                                                   start=(k == 0), stop=(k == KT - 1)), ts, before)
            fr.append(tp)
        rb = tmp[7]
        tr_ = rstd(bank_s[:, 0:N], 1.0 / D, rb[:, 0:N], tp, done)
        free_s.append(tr_)
        banks_o = [PS.take() for _ in range(4)]
        t_o = []
        for k in range(KT):
            t_, bf, fr = TB.take()
            t1 = dve(lambda e, k=k, t_=t_: e.scalar_tensor_tensor(t_[:, 0:N], XT[:, k, 0:N], VEC[:, V_NF + k:V_NF + k + 1],
                                                                  rb[:, 0:N], ALU.mult, ALU.mult), tr_, bf)

            def tr(e, k=k, t_=t_):
                for a in range(2):
                    last = e.transpose(banks_o[2 * a + k // 4][0][:, 128 * (k % 4):128 * (k % 4) + 128],
                                       t_[:, 128 * a:128 * a + 128], ident)
                return last
            tp = pe(tr, t1, [banks_o[j][1] for j in range(4)])
            fr.append(tp)
            if k % 4 == 3:
                hf = k // 4
                for a in range(2):
                    bk = banks_o[2 * a + hf][0]
                    t_o.append((dve if a else act)(
                        (lambda e, a=a, bk=bk, hf=hf: e.tensor_copy(OUT[:, a, 512 * hf:512 * hf + 512], bk[:, :])) if a else
                        (lambda e, a=a, bk=bk, hf=hf: e.activation(OUT[:, a, 512 * hf:512 * hf + 512], bk[:, :], ACT.Copy)),
                        tp, done))
        s_out = nc.alloc_semaphore("s_out")
        sp.raw(lambda e: e.dma_start(A["out"][0].rearrange("(a p) d -> p a d", p=128), OUT[:, :, :]).then_inc(s_out, 16),
               t_o)
        sp.raw(lambda e: None, (s_out, 16), (s_wr, 64), r_two, (s_res, 16))

    r = layer(0, t_x, rdy_wp)
    r = layer(1, [[t] for t in r[0]], r[1])
    second([[t] for t in r[0]])
    sp.raw(lambda e: None, [(sems[k], counts[k]) for k in range(N_SLOTS) if counts[k]], (s_wp, 256), (s_vec, n_vec[0]))
    finish(nc, pe, act, dve, pool, sp)


def finish(nc, pe, act, dve, pool, sp):
    with nc.Block() as block:
        @block.tensor
        def _(e):
            pe.emit(e)

        @block.scalar
        def _(e):
            act.emit(e)

        @block.vector
        def _(e):
            dve.emit(e)

        @block.gpsimd
        def _(e):
            pool.emit(e)

        @block.sync
        def _(e):
            sp.emit(e)


_INS = ("x", "c", "ctx", "c_ctx", "w_ada", "b_ada", "g_mix", "g_ffn", "w_in", "q_gain", "k_gain", "w_pool",
        "pool_scale", "w_four", "w_out", "w_gate_up", "w_down", "c_2", "positions_2", "w_ada_2", "b_ada_2",
        "norm1_g_2", "w_in_2", "b_gate_2", "conv_w_2", "conv_b_2", "attn_out_g_2", "mlstm_out_g_2", "w_out_2",
        "norm2_g_2", "w_rg_2", "b_rg_2", "w_re_2", "b_re_2", "w1_2", "w3_2", "w2_2", "norm_f_g_2")
_OUTS = [((1, 256, 1024), "float32")]


def kernel(**inputs):
    import numpy as _np
    import concourse.bacc as _bacc
    from concourse import mybir as _mybir
    from concourse.bass_utils import run_bass_kernel_spmd as _run

    nc = _bacc.Bacc("TRN2", target_bir_lowering=False, num_devices=1)
    arrays, args = {}, {}
    for name, a in [(n, inputs[n]) for n in _INS] + sorted(constants().items()):
        a = _np.ascontiguousarray(a)
        arrays[f"in_{name}_dram"] = a
        args[name] = nc.dram_tensor(f"in_{name}_dram", a.shape, _mybir.dt.from_np(a.dtype), kind="ExternalInput").ap()
    shape, dtype = _OUTS[0]
    args["out"] = nc.dram_tensor("out_0_dram", shape, _mybir.dt.from_np(_np.dtype(dtype)), kind="ExternalOutput").ap()
    block_program(nc, args)
    r = _run(nc, [arrays], core_ids=[0])
    return r.results[0]["out_0_dram"]
```

```python
import numpy as np
import concourse.bass as bass
from concourse import mybir

F32 = mybir.dt.float32
F32R = mybir.dt.float32r
BF16 = mybir.dt.bfloat16
I32 = mybir.dt.int32
U32 = mybir.dt.uint32
ALU = mybir.AluOpType
ACT = mybir.ActivationFunctionType
AX = mybir.AxisListType

D = 1024
KT = 8
NEG = -1.0e30
EPS = 1e-6
HALF = 11
N_EXP = 32
CAP = 64
N_EXTRA = 7
N_BLOCKS = N_EXP + N_EXTRA
N_SLOTS = 16

V_C, V_CCTX, V_C2, V_GMIX, V_GFFN = 0, 8, 16, 24, 40
V_N1, V_N2, V_NF, V_CW, V_CB, V_AG, V_MG = 56, 64, 72, 80, 112, 120, 124
V_BADA, V_PS, V_QG, V_KG, V_BADA2 = 128, 224, 228, 230, 256

K_POOL, K_DFT, K_R1, K_D, K_RD, K_CD, K_SD = 0, 0, 1024, 1152, 1408, 1664, 1792
K_END = 1920
S_ID, S_BD, S_COS, S_SIN = 0, 128, 256, 512
S_END = 768
B_R2, B_TRI, B_TRIT, B_SLT, B_IOTA, B_FREQ, B_MOD = 0, 128, 384, 512, 640, 768, 769
B_END = 897


def constants():
    eye = np.eye(128)
    blocks = np.kron(np.eye(2), np.ones((64, 64)))
    r1 = np.zeros((128, 128))
    r2 = np.zeros((128, 128))
    for m in range(128):
        if (m // 16) % 2 == 0:
            r1[m, m + 16] = -1
        else:
            r1[m, m - 16] = 1
        if (m // 32) % 2 == 0:
            r2[m, m + 32] = -1
        else:
            r2[m, m - 32] = 1
    dup = [np.zeros((128, 128)) for _ in range(2)]
    for g in range(2):
        for m in range(128):
            dup[g][m, 64 * g + m % 64] = 1
    t = np.arange(256)
    freqs = np.float32(10000.0) ** (-np.arange(16, dtype=np.float32) / np.float32(16))
    ang = np.zeros((128, 256), np.float32)
    for m in range(128):
        a, f = (m % 64) // 32, m % 16
        ids = (t // 64 if a == 0 else t % 64).astype(np.float32)
        ang[m] = ids * freqs[f]
    lt = 2 * np.pi * ((t[:, None] * t[None, :]) % 256) / 256
    c = np.arange(64)
    ld = 2 * np.pi * ((c[:, None] * c[None, :]) % 64) / 64
    dft = np.concatenate([np.cos(lt), np.sin(lt)], axis=1) / 16.0
    pool = np.zeros((256, 4, 256))
    for w, win in enumerate((2, 4, 8, 16)):
        for i in range(256):
            lo, hi = max(i - win // 2, 0), min(i + win - win // 2, 256)
            pool[lo:hi, w, i] += 1.0 / (hi - lo)
            pool[i, w, i] -= 1.0
    mix = np.zeros((128, K_END))
    kpool = pool.reshape(2, 128, 1024).transpose(1, 0, 2).reshape(128, 2048)
    mix[:, K_DFT:K_R1] = dft.reshape(2, 128, 512).transpose(1, 0, 2).reshape(128, 1024)
    mix[:, K_R1:K_D] = r1.T
    for g in range(2):
        mix[:, K_D + 128 * g:K_D + 128 * g + 128] = dup[g].T
        mix[:, K_RD + 128 * g:K_RD + 128 * g + 128] = (r1 @ dup[g]).T
    mix[:, K_CD:K_SD] = np.kron(np.eye(2), np.cos(ld) / 8.0)
    mix[:, K_SD:K_END] = np.kron(np.eye(2), -np.sin(ld) / 8.0)
    res = np.zeros((128, S_END))
    res[:, S_ID:S_BD] = eye
    res[:, S_BD:S_COS] = blocks
    res[:, S_COS:S_SIN] = np.cos(ang)
    res[:, S_SIN:S_END] = np.sin(ang)
    two = np.zeros((128, B_END))
    i = np.arange(128)
    two[:, B_R2:B_TRI] = r2.T
    two[:, B_TRI + 128:B_TRIT] = np.where(i[None, :] <= i[:, None], 0, NEG)
    two[:, B_TRIT:B_SLT] = np.where(i[:, None] <= i[None, :], 0, NEG)
    two[:, B_SLT:B_IOTA] = i[:, None] < i[None, :]
    two[:, B_IOTA:B_FREQ] = np.arange(128)
    half = np.arange(32, dtype=np.float32)
    inv = np.float32(10000.0) ** (-half / np.float32(32))
    two[:, B_FREQ] = inv[i % 32]
    two[:, B_MOD:B_END] = i % CAP
    return {"k_pool": np.ascontiguousarray(kpool, np.float32), "k_mix": mix.astype(np.float32), "k_res": res.astype(np.float32), "k_two": two.astype(np.float32)}


class Engine:

    def __init__(self, sem):
        self.sem, self.n, self.entries = sem, 0, []

    def __call__(self, fn, *waits):
        self.n += 1
        self.entries.append((fn, waits, True))
        return (self.sem, self.n)

    def raw(self, fn, *waits):
        self.entries.append((fn, waits, False))

    def last(self):
        return (self.sem, self.n)

    def emit(self, eng):
        reached = {}

        def wait(tokens):
            for t in tokens:
                if isinstance(t, list):
                    wait(t)
                elif t is not None and t[1] > reached.get(t[0].name, 0):
                    eng.wait_ge(t[0], t[1])
                    reached[t[0].name] = t[1]

        for fn, waits, counted in self.entries:
            wait(list(waits))
            ins = fn(eng)
            if counted:
                ins.then_inc(self.sem, 1)


class Buffers:

    def __init__(self, places, free=()):
        self.places, self.i = places, 0
        self.free = [list(free) for _ in places]
        self.kept = set()

    def take(self, keep=False):
        while self.i % len(self.places) in self.kept:
            self.i += 1
        k = self.i % len(self.places)
        self.i += 1
        if keep:
            self.kept.add(k)
        before, self.free[k] = self.free[k], []
        return self.places[k], before, self.free[k]

    def give(self, place):
        self.kept -= {k for k in self.kept if self.places[k] is place}


class Loaded:
    def __init__(self, place, ready):
        self.place, self.ready, self.done = place, ready, []


class Chunk:

    def __init__(self, load, view):
        self.load, self.view, self.item = load, view, None

    def get(self):
        if self.item is None:
            self.item = self.load()
        return self.item


class Ring:

    def __init__(self, sp, slots, sems, counts, before):
        self.sp, self.slots, self.sems, self.counts = sp, slots, sems, counts
        self.before, self.i = before, 0
        self.kept = set()

    def load(self, fill, dmas=1, keep=False):
        while self.i % len(self.slots) in self.kept:
            self.i += 1
        k = self.i % len(self.slots)
        self.i += 1
        if keep:
            self.kept.add(k)
        place, sem = self.slots[k], self.sems[k]
        self.counts[k] += 16 * dmas
        item = Loaded(place, (sem, self.counts[k]))
        self.sp.raw(lambda e: fill(e, place, sem), self.before[k])
        self.before[k] = item.done
        return item


def block_program(nc, A):
    pe, act, dve, pool, sp = (Engine(nc.alloc_semaphore(n)) for n in
                              ("s_pe", "s_act", "s_dve", "s_pool", "s_sp"))
    KB = 1024
    BASE = 16512

    def at(name, shape, dt, off):
        return nc.alloc_sbuf_tensor_at(name, shape, dt, offset=BASE + off)

    oX, oH, oG, oR, oZ, oS, oW = 0, 16 * KB, 48 * KB, 92 * KB, 156 * KB, 176 * KB, 176 * KB + 9888
    XT = at("XT", [128, KT, 512], F32, oX)
    HH = at("HH", [128, KT, 512], F32R, oH)
    HL = at("HL", [128, KT, 512], F32R, oH + 16 * KB)
    GH = at("GH", [128, HALF, 512], F32R, oG)
    GL = at("GL", [128, HALF, 512], F32R, oG + 22 * KB)
    ring_slots = [at(f"R{i}", [128, 2048], F32, oR + 8 * KB * i) for i in range(8)]
    ws = [(at(f"WH{i}", [128, HALF, 128], F32R, oW + i * 11264),
           at(f"WL{i}", [128, HALF, 128], F32R, oW + i * 11264 + 5632)) for i in range(2)]
    QT = at("QT", [128, 4, 512], F32, oZ)
    KTr = at("KTr", [128, 512], F32, oZ + 8 * KB)
    Z = at("Z", [128, 4, 640], F32, oZ + 10 * KB)
    tmp = [at(f"TMP{i}", [128, 512], F32, oZ + 2 * KB * i) for i in range(8)]
    RES = at("RES", [128, S_END], F32, oS)
    ONES = at("ONES", [128, 128], F32, oS + 3072)
    VEC = at("VEC", [128, 304], F32, oS + 3584)
    MOD = at("MOD", [128, 3, 48, 3], F32, oS + 4800)
    SG = at("SG", [128, 8, 2], F32, oS + 6528)
    WPF = at("WPF", [128, 4, 128], F32, oS + 6592)
    ST = at("ST", [128, 48], F32, oS + 8640)
    EB = at("EB", [128, 1], F32, oS + 8832)
    SC = at("SC", [128, KT, 32], F32, oS + 8864)
    ab_g = [at(f"AT{i}", [128, 256], F32, oG + 20 * KB + KB * i) for i in range(2)]
    AB = Buffers(ab_g)
    QR = at("QR", [128, 4, 512], F32, oH)
    KD = at("KD", [128, 2, 512], F32, oH + 8 * KB)
    mt = [at(f"MT{i}", [128, 512], F32, oH + 12 * KB + 2 * KB * i) for i in range(3)]
    mt_more = [at(f"MU{i}", [128, 512], F32, oG + 38 * KB + 2 * KB * i) for i in range(3)]
    pbuf = [at(f"P{i}", [128, 512], F32, o_) for i, o_ in enumerate(
        (oH + 18 * KB, oH + 20 * KB, oH + 22 * KB, oG + 16 * KB, oG + 18 * KB))]
    ptbuf = [at(f"PT{i}", [128, 4, 256], F32, oH + 24 * KB + 4 * KB * i) for i in range(2)]
    zt = [at(f"ZT{i}", [128, 512], F32, oG + 2 * KB * i) for i in range(3)]
    VR = at("VR", [128, 3, 128], F32, oG)

    banks = [nc.alloc_psum_tensor(f"ps{i}", [128, 512], F32) for i in range(8)]
    PS = Buffers(banks)
    WS = Buffers(ws)
    ident = RES[:, S_ID:S_BD]
    bd = RES[:, S_BD:S_COS]
    cos1, sin1 = RES[:, S_COS:S_SIN], RES[:, S_SIN:S_END]

    def fence():
        return [pe.last(), act.last(), dve.last(), pool.last()]

    s_res, s_vec, s_wp = (nc.alloc_semaphore(n) for n in ("s_res", "s_vec", "s_wp"))
    sems = [nc.alloc_semaphore(f"s_r{i}") for i in range(N_SLOTS)]
    counts = [0] * N_SLOTS
    ring = Ring(sp, ring_slots, sems, counts, [[] for _ in range(8)])

    pool.raw(lambda e: e.dma_start(RES[:, :], A["k_res"]).then_inc(s_res, 16))
    t_ones = dve(lambda e: e.memset(ONES[:, :], 1.0))
    t_wpf = dve(lambda e: e.memset(WPF[:, :, :], 0.0))
    t_eb = dve(lambda e: e.memset(EB[:, :], EPS))
    t_vr = dve(lambda e: e.memset(VR[:, :, :], 0.0))
    n_vec = [0]

    def vec_rows(col, ap):
        t, r = divmod(col, 128)
        n = ap.shape[0]
        n_vec[0] += 16
        eng = (act, sp)[n_vec[0] // 16 % 2]
        eng.raw(lambda e: e.dma_start(VR[r:r + n, t, 0:ap.shape[1]], ap).then_inc(s_vec, 16), t_vr)

    def rows(ap, pattern, **kw):
        return ap.rearrange(pattern, **kw)

    one = "(a p) -> a p"
    vec_rows(V_C, rows(A["c"], "o (a p) -> (o a) p", p=128))
    vec_rows(V_CCTX, rows(A["c_ctx"], one, p=128))
    vec_rows(V_BADA, rows(A["b_ada"], "l (a p) -> (l a) p", p=128))
    vec_rows(V_GMIX, rows(A["g_mix"], "l (a p) -> (l a) p", p=128))
    vec_rows(V_GFFN, rows(A["g_ffn"], "l (a p) -> (l a) p", p=128))
    vec_rows(V_C2, rows(A["c_2"], "o (a p) -> (o a) p", p=128))
    vec_rows(V_N1, rows(A["norm1_g_2"], "o (a p) -> (o a) p", p=128))
    vec_rows(V_N2, rows(A["norm2_g_2"], "o (a p) -> (o a) p", p=128))
    vec_rows(V_NF, rows(A["norm_f_g_2"], one, p=128))
    vec_rows(V_CW, rows(A["conv_w_2"], "o i (a p) -> (o i a) p", p=128))
    vec_rows(V_CB, rows(A["conv_b_2"], "o (a p) -> (o a) p", p=128))
    vec_rows(V_AG, rows(A["attn_out_g_2"], "o (a p) -> (o a) p", p=128))
    vec_rows(V_MG, rows(A["mlstm_out_g_2"], "o (a p) -> (o a) p", p=128))
    vec_rows(V_PS, rows(A["pool_scale"], "l (a p) -> (l a) p", p=128))
    vec_rows(V_BADA2, rows(A["b_ada_2"], "o (a p) -> (o a) p", p=128))
    for base, name in ((V_QG, "q_gain"), (V_KG, "k_gain")):
        for c in range(2):
            n_vec[0] += 16
            (act, sp)[n_vec[0] // 16 % 2].raw(lambda e, base=base, name=name, c=c: e.dma_start(
                VR[base - 128:base - 126, 1, 64 * c:64 * c + 64], A[name]).then_inc(s_vec, 16), t_vr)

    def load_mixer_weights(layer, free):
        for k, name in enumerate(("w_pool", "w_four")):
            for g in range(4):
                h = 64 * (g % 2)
                pool.raw(lambda e, k=k, g=g, h=h, name=name: e.dma_start(
                    WPF[h:h + 64, 2 * k + g // 2, h:h + 64], A[name][layer, g]).then_inc(s_wp, 16),
                    t_wpf, free)
        return (s_wp, 128 * (layer + 1))

    rdy_wp = load_mixer_weights(0, [])

    def transpose(out, in_, n=128):
        return lambda e: e.transpose(out, in_, ident[0:n, 0:n])

    def fill_tokens(name):
        def fill(e, place, sem):
            e.dma_start(place[:, :].rearrange("p (a d) -> p a d", a=2),
                        A[name][0].rearrange("(a p) d -> p a d", p=128)).then_inc(sem, 16)
        return fill

    tok = [ring.load(fill_tokens("x")), ring.load(fill_tokens("ctx"))]

    ada_src = [A["w_ada"][0], A["w_ada"][1], A["w_ada_2"][0]]

    def wchunk(src, c0, n):
        v = src.rearrange("(k p) n -> p k n", p=128)

        def fill(e, place, sem):
            e.dma_start(place[:, 0:8 * n].rearrange("p (k n) -> p k n", k=8), v[:, :, c0:c0 + n])\
                .then_inc(sem, 16)
        return fill

    t_vec = []
    bank, before, free = PS.take()
    for t in range(3):
        tt = pe(lambda e, t=t, bank=bank: e.transpose(bank[:, 128 * t:128 * t + 128], VR[:, t, :], ident),
                (s_res, 16), (s_vec, n_vec[0]), before)
    t_vec = dve(lambda e, bank=bank: e.tensor_copy(VEC[:, :], bank[:, 0:304]), tt)
    free.append(t_vec)
    t_qg = dve(lambda e: e.tensor_scalar(VEC[:, V_QG:V_QG + 2], VEC[:, V_QG:V_QG + 2], 0.125, None, ALU.mult), t_vec)
    t_sc = dve(lambda e: e.memset(SC[:, :, :], 0.0))
    t_sc = act(lambda e: e.activation(SC[:, :, 0:3], VEC[:, 0:24].rearrange("p (j k) -> p k j", j=3), ACT.Silu),
               t_vec, t_sc)

    t_x = []
    for k in range(KT):
        bank, before, free = PS.take()
        for a in range(4):
            tt = pe(lambda e, k=k, a=a, bank=bank: e.transpose(
                bank[:, 128 * a:128 * a + 128],
                tok[a // 2].place[:, 1024 * (a % 2) + 128 * k:1024 * (a % 2) + 128 * k + 128], ident),
                tok[a // 2].ready, before, (s_res, 16))
        tc = dve(lambda e, k=k, bank=bank: e.tensor_copy(XT[:, k, :], bank[:, :]), tt)
        free.append(tc)
        t_x.append(tc)
    for item in tok:
        item.done.append(tt)

    t_mod = [[], [], []]

    def ada_load(which, c):
        return which, c, ring.load(wchunk(ada_src[which], 256 * c, 256))

    def ada_use(which, c, item):
        w = item.place[:, :].rearrange("p (k n) -> p k n", k=8)
        bank, before, free = PS.take()

        def mm(e):
            for k in range(KT):
                g = k % 4
                last = e.matmul(bank[32 * g:32 * g + 32, 0:256], SC[:, k, :], w[:, k, :], start=(k < 4), stop=(k >= 4))
            return last
        tp = pe(mm, item.ready, before, t_sc)
        item.done.append(tp)
        AT, bf, fr = AB.take()
        ta = act(lambda e: e.activation(AT[:, 0:256], bank[:, 0:256], ACT.Copy), tp, bf)
        free.append(ta)

        def rest():
            bank2, before, free = PS.take()

            def tr(e):
                for m in range(2):
                    last = e.transpose(bank2[:, 128 * m:128 * m + 128], AT[:, 128 * m:128 * m + 128], ident)
                return last
            tp = pe(tr, ta, before)
            fr.append(tp)
            t1 = dve(lambda e: e.tensor_reduce(
                MOD[:, which, 2 * c:2 * c + 2, :],
                bank2[:, 0:256].rearrange("p (m g j) -> p m j g", m=2, g=4)[:, :, 0:3, :], AX.X, ALU.add), tp)
            free.append(t1)
            bcol = (V_BADA + 48 * which if which < 2 else V_BADA2) + 2 * c
            td = dve(lambda e: e.tensor_tensor(
                MOD[:, which, 2 * c:2 * c + 2, :], MOD[:, which, 2 * c:2 * c + 2, :],
                VEC[:, bcol:bcol + 2].unsqueeze(2).to_broadcast([128, 2, 3]), ALU.add), t1, t_vec)
            t_mod[which].append(td)
        return rest

    def split_weights(parts, n):
        (wh, wl), before, free = WS.take()
        k0 = 0
        th, tl = [], []
        for chunk, col, K in parts:
            item = chunk.get()
            w = chunk.view(item.place)[:, :, col:col + n]
            h, l = wh[:, k0:k0 + K, 0:n], wl[:, k0:k0 + K, 0:n]
            t = act(lambda e, h=h, w=w: e.activation(h, w, ACT.Copy), item.ready, before)
            th.append(t)
            t = dve(lambda e, h=h, l=l, w=w: e.tensor_tensor(l, w, h.bitcast(F32), ALU.subtract),
                    item.ready, before, t)
            tl.append(t)
            item.done.append(t)
            k0 += K
        return wh, wl, k0, th, tl, free

    def linear(tiles, xh, xl, t_in, N, evac, hooks=None, first=None):
        hooks = list(hooks or [])
        n_hooks = len(hooks)
        nxt = first or split_weights(*tiles[0])
        for i, (_, n) in enumerate(tiles):
            h, l, K, th, tl, free_w = nxt
            if i + 1 < len(tiles):
                nxt = split_weights(*tiles[i + 1])
            bank, before, free = PS.take()

            def mms(e, ks, parts, h=h, l=l, K=K, n=n, bank=bank):
                for k in ks:
                    for wi, xi in parts:
                        w_, x_ = (h, l)[wi][:, k, 0:n], (xh, xl)[xi](k)
                        first = k == 0 and (wi, xi) == (0, 0)
                        final = k == K - 1 and wi == 1
                        last = e.matmul(bank[0:n, 0:N], w_, x_, start=first, stop=final)
                return last

            if i == 0:
                for k in range(K):
                    pe(lambda e, k=k, f=mms: f(e, [k], ((0, 0), (0, 1))), before, th, t_in[k])
            else:
                pe(lambda e, f=mms, K=K: f(e, range(K), ((0, 0), (0, 1))), before, th, t_in)
            tp = pe(lambda e, f=mms, K=K: f(e, range(K), ((1, 0),)), tl)
            free_w.append(tp)
            free.extend(evac(i, bank, tp))
            while n_hooks - len(hooks) < n_hooks * (i + 1) // len(tiles):
                hooks.pop(0)()

    def split_out(src, hi, lo, tok_, *waits):
        th = act(lambda e: e.activation(hi, src, ACT.Copy), tok_, *waits)
        tl = dve(lambda e: e.tensor_tensor(lo, src, hi.bitcast(F32), ALU.subtract), th, tok_, *waits)
        return th, tl

    def rstd(sums, mean, out, *waits):
        t = act(lambda e: e.activation(out, sums, ACT.Ln, bias=EB[:, 0:1], scale=mean), t_eb, *waits)
        return act(lambda e: e.activation(out, out, ACT.Exp, scale=-0.5), t)

    class Sums:

        def __init__(self, N, TB):
            self.N, self.TB, self.n = N, TB, 0
            self.bank, self.before, self.free = PS.take(keep=True)

        def add(self, k, tok_):
            N, bank, n = self.N, self.bank, self.n
            self.n += 1
            sq, bf, fr = self.TB.take()
            if k % 2 == 0:
                ts = act(lambda e: e.activation(sq[:, 0:N], XT[:, k, 0:N], ACT.Square), tok_, bf)
            else:
                ts = dve(lambda e: e.tensor_tensor(sq[:, 0:N], XT[:, k, 0:N], XT[:, k, 0:N], ALU.mult), tok_, bf)
            self.tp = pe(lambda e: e.matmul(bank[:, 0:N], ONES[:, :], sq[:, 0:N], start=(n == 0), stop=(n == KT - 1)),
                         ts, self.before, t_ones)
            fr.append(self.tp)

        def late(self, i, toks):
            if i:
                self.add(i - 1, list(toks[i - 1]))
            if i == KT - 1:
                self.add(i, list(toks[i]))

    def adaln(sums, scales, hi, lo, t_free, keep=None):
        N, TB = sums.N, sums.TB
        rb = tmp[7]
        tr = rstd(sums.bank[:, 0:N], 1.0 / D, rb[:, 0:N], sums.tp, t_free)
        sums.free.append(tr)
        PS.give(sums.bank)
        out, begun = [], []

        def begin(k):
            t, bf, fr = TB.take()
            t1 = dve(lambda e: e.tensor_tensor(t[:, 0:N], XT[:, k, 0:N], rb[:, 0:N], ALU.mult), tr, bf)
            begun.append((t, fr, t1))

        for k in range(3):
            begin(k)
        for k in range(KT):
            t, fr, t1 = begun[k]
            dst = t if keep is None else keep(k)
            t2 = []
            for n, (cols, s, b, tw) in enumerate(scales):
                if n:
                    t2.append(pool(lambda e, k=k, t=t, dst=dst, cols=cols, s=s, b=b: e.tensor_scalar(
                        dst[:, cols[0]:cols[1]], t[:, cols[0]:cols[1]], s(k), b(k), ALU.mult, ALU.add),
                        t1, tw, t_free))
                else:
                    t2.append(act(lambda e, k=k, t=t, dst=dst, cols=cols, s=s, b=b: e.activation(
                        dst[:, cols[0]:cols[1]], t[:, cols[0]:cols[1]], ACT.Identity, bias=b(k), scale=s(k)),
                        t1, tw, t_free))
            if k + 3 < KT:
                begin(k + 3)
            if hi is None:
                fr.extend(t2)
                out.append(t2)
                continue
            th, tl = split_out(dst[:, 0:N], hi(k), lo(k), t2, t_free)
            fr.append(tl)
            out.append([th, tl])
        return out

    n_st = [0]
    st_free = [[] for _ in range(16)]

    def stat():
        k = n_st[0] % 16
        n_st[0] += 1
        before, st_free[k] = st_free[k], []
        return ST[:, 3 * k:3 * k + 3], before, st_free[k]

    def attention(jobs, PB, PTB, pair_done, fill=None):
        steps = [(h, a) for h in range(len(jobs)) for a in range(len(jobs[h]["nk"]))]
        state, head_pt, pair = {}, {}, {}

        def scores(h, a):
            J = jobs[h]
            n = 128 * J["nk"][a]
            bank, before, free = PS.take()
            tp = pe(lambda e: e.matmul(bank[:, 0:n], J["q"](a), J["k"](n), start=True, stop=True),
                    before, J["waits"])
            P, bf, fr = PB.take()
            st, sbf, sfr = stat()
            src = bank
            if J["mask"] is not None:
                tp = dve(lambda e: e.tensor_tensor(P[:, 0:n], bank[:, 0:n], J["mask"](a), ALU.add), tp, bf)
                free.append(tp)
                src = P
            tm = dve(lambda e: e.tensor_reduce(st[:, 0:1], src[:, 0:n], AX.X, ALU.max, negate=True), tp, sbf)
            te = act(lambda e: e.activation(P[:, 0:n], src[:, 0:n], ACT.Exp, bias=st[:, 0:1],
                                            accum_out=st[:, 1:2]), tm, bf, tp)
            if src is bank:
                free.append(te)
            state[h, a] = (P, fr, te, st, sfr, n)

        def divide(h, a):
            P, fr, te, st, sfr, n = state[h, a]
            tr = dve(lambda e: e.reciprocal(st[:, 2:3], st[:, 1:2]), te)
            tn = dve(lambda e: e.tensor_scalar(P[:, 0:n], P[:, 0:n], st[:, 2:3], None, ALU.mult), tr)
            sfr.append(tn)
            state[h, a] = (P, fr, tn)

        def turn(h, a):
            J = jobs[h]
            nk = J["nk"][a]
            P, fr, tn = state.pop((h, a))
            if a == 0:
                head_pt[h] = (*PTB.take(), [])
            PT, bf, ptfr, toks = head_pt[h]
            bank, before, free = PS.take()

            def tr(e):
                for j in range(nk):
                    last = e.transpose(bank[:, 128 * j:128 * j + 128], P[:, 128 * j:128 * j + 128], ident)
                return last
            tp = pe(tr, tn, before)
            fr.append(tp)
            tc = act(lambda e: e.activation(PT[:, 0:nk, 128 * a:128 * a + 128],
                                            bank[:, 0:128 * nk].rearrange("p (j n) -> p j n", n=128), ACT.Copy),
                     tp, bf)
            free.append(tc)
            toks.append(tc)

        def values(h):
            J = jobs[h]
            PT, bf, ptfr, toks = head_pt.pop(h)
            if h % 2 == 0:
                pair[0] = PS.take(keep=True)
            bank, before, free = pair[0]
            nk = J["nk"]
            r = 64 * (h % 2)

            def pv(e):
                groups = [(0, 128 * len(nk), nk[0])] if len(set(nk)) == 1 else \
                    [(128 * a, 128 * a + 128, nk[a]) for a in range(len(nk))]
                for lo, hi, m in groups:
                    for j in range(m):
                        last = e.matmul(bank[r:r + 64, lo:hi], J["v"](j), PT[:, j, lo:hi],
                                        start=(j == 0), stop=(j == m - 1))
                return last
            tp = pe(pv, toks, before, J["waits"])
            ptfr.append(tp)
            if h % 2:
                free.extend(pair_done(h // 2, bank, tp))
                PS.give(bank)

        LAG = 3
        for i in range(len(steps) + LAG):
            if i < len(steps):
                scores(*steps[i])
                if fill is not None:
                    fill()
            if 1 <= i <= len(steps):
                divide(*steps[i - 1])
            if i >= LAG:
                h, a = steps[i - LAG]
                turn(h, a)
                if a == len(jobs[h]["nk"]) - 1:
                    values(h)

    MH = lambda m, lo, hi: GH[:, m, lo:hi]
    ML = lambda m, lo, hi: GL[:, m, lo:hi]

    def head_norm(src, rows_n, gain, MT, dst, waits, mean=1.0 / 64, red=None, t_free=None):
        n = rows_n
        sq, bf, fr = MT.take()
        ts = act(lambda e: e.activation(sq[:, 0:n], src, ACT.Square), waits, bf)
        bank, before, free = PS.take()
        tp = pe(lambda e: e.matmul(bank[:, 0:n], bd if red is None else red, sq[:, 0:n], start=True, stop=True),
                ts, before)
        t2 = rstd(bank[:, 0:n], mean, sq[:, 0:n], tp)
        free.append(t2)
        t3 = dve(lambda e: e.scalar_tensor_tensor(dst, src, gain, sq[:, 0:n], ALU.mult, ALU.mult), t2, waits, t_free)
        fr.append(t3)
        return t3

    def head_norms(jobs, MT, mean=1.0 / 64, red=None):
        held, out = [], []
        for src, n, gain, dst, waits in jobs:
            sq, bf, fr = MT.take()
            ts = act(lambda e, src=src, n=n, sq=sq: e.activation(sq[:, 0:n], src, ACT.Square), waits, bf)
            bank, before, free = PS.take()
            tp = pe(lambda e, n=n, sq=sq, bank=bank: e.matmul(bank[:, 0:n], bd if red is None else red, sq[:, 0:n],
                                                          start=True, stop=True), ts, before)
            held.append((sq, fr, bank, free, tp))
        toks = []
        for (src, n, gain, dst, waits), (sq, fr, bank, free, tp) in zip(jobs, held):
            t = act(lambda e, n=n, sq=sq, bank=bank: e.activation(sq[:, 0:n], bank[:, 0:n], ACT.Ln, bias=EB[:, 0:1],
                                                                  scale=mean), tp, t_eb)
            free.append(t)
            toks.append(t)
        for (src, n, gain, dst, waits), (sq, fr, bank, free, tp), t in zip(jobs, held, toks):
            t = act(lambda e, n=n, sq=sq: e.activation(sq[:, 0:n], sq[:, 0:n], ACT.Exp, scale=-0.5), t)
            t = dve(lambda e, src=src, n=n, gain=gain, dst=dst, sq=sq: e.scalar_tensor_tensor(
                dst, src, gain, sq[:, 0:n], ALU.mult, ALU.mult), t, waits)
            fr.append(t)
            out.append(t)
        return out

    def rope_into(dst, straight, turned, cos, sin, MT, waits, t_free=None):
        a, bf, fr = MT.take()
        t1 = dve(lambda e: e.tensor_tensor(a[:, 0:256], turned, sin, ALU.mult), waits, bf)
        t2 = dve(lambda e: e.tensor_tensor(dst, straight, cos, ALU.mult), waits, t_free)
        t3 = dve(lambda e: e.tensor_tensor(dst, dst, a[:, 0:256], ALU.add), t1, t2)
        fr.append(t3)
        return t1, t3

    def fm(ap, k=8):
        return ap.rearrange("p (k n) -> p k n", k=k)

    def wide(src, c0, n):
        return Chunk(lambda: ring.load(wchunk(src, c0, n)), lambda place: fm(place[:, 0:8 * n]))

    AB.places = ab_g
    rest = None
    for c in range(8):
        rest_before, rest = rest, ada_use(*ada_load(0, c))
        if rest_before:
            rest_before()
    rest()
    ada_queue = [(0, c) for c in range(8, 24)] + [(w, c) for w in (1, 2) for c in range(24)]

    ada_rest = []

    def filler():
        begun = ada_use(*ada_load(*ada_queue.pop(0))) if ada_queue else None
        if ada_rest:
            ada_rest.pop()()
        if begun:
            ada_rest.append(begun)

    TB0 = Buffers(tmp[:7])
    sums0 = Sums(512, TB0)
    for k in range(KT):
        sums0.add(k, t_x[k])

    def layer(i, t_x, rdy_wp, sums, t_h_free, t_ab):
        both = i == 0
        N = 512 if both else 256
        streams = (0, 1) if both else (0,)
        for f in AB.free:
            f.extend(t_ab)
        tmp_free = t_h_free
        t_sg = dve(lambda e: e.scalar_tensor_tensor(
            SG[:, :, :], MOD[:, i, 8:16, 0:2], 1.0,
            VEC[:, V_GMIX + 8 * i:V_GMIX + 8 * i + 8].unsqueeze(2).to_broadcast([128, 8, 2]),
            ALU.add, ALU.mult), list(t_mod[i]), t_vec, tmp_free)
        scales = [((256 * s, 256 * s + 256), lambda k, s=s: SG[:, k, s:s + 1], lambda k, s=s: MOD[:, i, k, s:s + 1], t_sg)
                  for s in (0, 1)]
        chunks = [wide(A["w_in"][i], 256 * c, 256) for c in range(5)]

        def tile_of(m):
            return [(chunks[m // 2], 128 * (m % 2), 8)], 128

        first = split_weights(*tile_of(0))
        t_h = adaln(sums, scales, lambda k: HH[:, k, :], lambda k: HL[:, k, :], tmp_free)
        zfree = fence()
        t_q, t_k, t_z = [None] * 4, [None], []

        def evac(j, bank, tp):
            if j < 4:
                t_q[j] = act(lambda e: e.activation(QT[:, j, 0:N], bank[:, 0:N], ACT.Copy), tp, zfree)
                return [t_q[j]]
            t_k[0] = act(lambda e: e.activation(KTr[:, :], bank[:, :], ACT.Copy), tp, zfree)
            return [t_k[0]]

        xh, xl = lambda k: HH[:, k, 0:N], lambda k: HL[:, k, 0:N]
        n_fill = 16 if both else 0
        linear([tile_of(m) for m in range(4)], xh, xl, t_h, N, evac, [filler] * (n_fill // 2), first)
        xh, xl = lambda k: HH[:, k, :], lambda k: HL[:, k, :]

        ZT = Buffers(zt, zfree)

        def evac_z(j, bank, tp, nt):
            t, bf, fr = ZT.take()
            tc = act(lambda e: e.activation(t[:, 0:128 * nt], bank[:, 0:128 * nt], ACT.Copy), tp, bf)
            bank2, before, free2 = PS.take()

            def tr(e):
                for a in range(nt):
                    last = e.transpose(bank2[:, 128 * a:128 * a + 128], t[:, 128 * a:128 * a + 128], ident)
                return last
            tt = pe(tr, tc, before)
            fr.append(tt)
            td = dve(lambda e: e.tensor_copy(Z[:, 0:nt, 128 * j:128 * j + 128],
                                             bank2[:, 0:128 * nt].rearrange("p (a n) -> p a n", n=128)), tt, zfree)
            free2.append(td)
            t_z.append(td)
            return [tc]
        nt = 4 if both else 2
        linear([tile_of(m) for m in (4, 5)], xh, xl, t_h, 512,
               lambda j, b, tp: evac_z(0, b, tp, 4) if j else evac(4, b, tp))
        xh, xl = lambda k: HH[:, k, 0:N], lambda k: HL[:, k, 0:N]
        linear([tile_of(m) for m in range(6, 10)], xh, xl, t_h, N,
               lambda j, b, tp: evac_z(j + 1, b, tp, nt), [filler] * (n_fill // 2))
        hfree = fence()
        MT, PB, PTB = Buffers(mt + mt_more, hfree), Buffers(pbuf, hfree), Buffers(ptbuf, hfree)
        const = [ring.load(lambda e, place, sem, nm=nm, n=n: e.dma_start(place[:, 0:n], A[nm]).then_inc(sem, 16), keep=True)
                 for nm, n in (("k_pool", 2048), ("k_mix", K_END))]
        kp, kc = const[0].place, const[1].place
        qg = VEC[:, V_QG + i:V_QG + i + 1]
        kg = VEC[:, V_KG + i:V_KG + i + 1]
        mfree = hfree
        t_kn, *t_qn = head_norms([(KTr[:, :], 512, kg, KTr[:, :], t_k[0])] +
                                 [(QT[:, m, 0:N], N, qg, QT[:, m, 0:N], [t_q[m], t_qg]) for m in range(4)], MT)
        t_kd = []
        for g in range(2):
            bank, before, free = PS.take()
            tp = pe(lambda e, g=g, bank=bank: e.matmul(bank[:, :], kc[:, K_D + 128 * g:K_D + 128 * g + 128],
                                                       KTr[:, :], start=True, stop=True), t_kn, before, const[0].ready, const[1].ready)
            bank2, before, free2 = PS.take()
            tp2 = pe(lambda e, g=g, bank2=bank2: e.matmul(bank2[:, 0:256], kc[:, K_RD + 128 * g:K_RD + 128 * g + 128],
                                                          KTr[:, 0:256], start=True, stop=True), before)
            t0 = act(lambda e, g=g, bank=bank: e.activation(KD[:, g, 256:512], bank[:, 256:512], ACT.Copy), tp, hfree)
            t1, t3 = rope_into(KD[:, g, 0:256], bank[:, 0:256], bank2[:, 0:256], cos1, sin1, MT, [tp2, t0], hfree)
            free.extend([t0, t3])
            free2.append(t1)
            t_kd += [t0, t3]
        t_qr = [[], []]
        for m in range(4):
            tn = t_qn[m]
            bank, before, free = PS.take()
            tp = pe(lambda e, m=m, bank=bank: e.matmul(bank[:, 0:256], kc[:, K_R1:K_R1 + 128], QT[:, m, 0:256],
                                                       start=True, stop=True), tn, before)
            t1, t3 = rope_into(QR[:, m, 0:256], QT[:, m, 0:256], bank[:, 0:256], cos1, sin1, MT, [tp, tn], hfree)
            free.append(t1)
            t_qr[0].append(t3)
            t_qr[1].append(tn)
        t_m = [[] for _ in range(8)]

        def out_split(bank, m, lo, tp, scale=None):
            t, bf, fr = MT.take()
            if scale is None:
                tc = dve(lambda e: e.tensor_copy(t[:, 0:256], bank[:, 0:256]), tp, bf)
            else:
                tc = dve(lambda e: e.tensor_scalar(t[:, 0:256], bank[:, 0:256], scale, None, ALU.mult), tp, bf)
            th, tl = split_out(t[:, 0:256], MH(m, lo, lo + 256), ML(m, lo, lo + 256), tc, mfree)
            fr.append(tl)
            t_m[m] += [th, tl]
            return [tc]

        for s in streams:
            src = QR if s == 0 else QT
            jobs = []
            for h in range(8):
                r, m, g = 64 * (h % 2), h // 2, h // 4
                k0 = 0 if s == 0 else 256
                jobs.append({
                    "q": lambda a, r=r, m=m, s=s, src=src: src[r:r + 64, m, 256 * s + 128 * a:256 * s + 128 * a + 128],
                    "k": lambda n, r=r, g=g, k0=k0: KD[r:r + 64, g, k0:k0 + n],
                    "v": lambda j, g=g, s=s: Z[:, 2 * s + j, 64 * g:64 * g + 64],
                    "nk": [4, 4] if s == 0 else [2, 2], "mask": None,
                    "waits": [t_kd, t_qr[s][m], t_z[0]],
                })
            attention(jobs, PB, PTB, lambda p, bank, tp, s=s: out_split(bank, p, 256 * s, tp), filler)
        for s in streams:
            for j in range(2):
                bank, before, free = PS.take()

                def mm(e, s=s, j=j, bank=bank):
                    for a in range(2):
                        for t in range(2):
                            c = 128 + 128 * j + 64 * a
                            p = K_POOL + 1024 * t + 256 * (2 * j + a)
                            last = e.matmul(bank[64 * a:64 * a + 64, 0:256], Z[:, 2 * s + t, c:c + 64],
                                            kp[:, p:p + 256], start=(t == 0), stop=(t == 1))
                    return last
                tp = pe(mm, t_z, before, const[0].ready, const[1].ready)
                d, bf, fr = MT.take()
                tc = act(lambda e, d=d, bank=bank: e.activation(d[:, 0:256], bank[:, 0:256], ACT.Copy), tp, bf)
                free.append(tc)
                bank, before, free = PS.take()
                tp = pe(lambda e, j=j, d=d, bank=bank: e.matmul(bank[:, 0:256], WPF[:, j, :], d[:, 0:256],
                                                                start=True, stop=True), tc, before, rdy_wp)
                fr.append(tp)
                free.extend(out_split(bank, 4 + j, 256 * s, tp, VEC[:, V_PS + 2 * i + j:V_PS + 2 * i + j + 1]))
            for j in range(2):
                bank, before, free = PS.take()

                def mm(e, s=s, j=j, bank=bank):
                    for t in range(2):
                        last = e.matmul(bank[:, :], Z[:, 2 * s + t, 384 + 128 * j:512 + 128 * j],
                                        kc[:, K_DFT + 512 * t:K_DFT + 512 * t + 512], start=(t == 0), stop=(t == 1))
                    return last
                tp = pe(mm, t_z, before, const[0].ready, const[1].ready)
                d, bf, fr = MT.take()
                tc = act(lambda e, d=d, bank=bank: e.activation(d[:, :], bank[:, :], ACT.Copy), tp, bf)
                free.append(tc)
                bank, before, free = PS.take()

                def mm(e, d=d, bank=bank):
                    e.matmul(bank[:, 0:256], kc[:, K_CD:K_SD], d[:, 0:256], start=True, stop=False)
                    return e.matmul(bank[:, 0:256], kc[:, K_SD:K_END], d[:, 256:512], start=False, stop=True)
                tp = pe(mm, tc, before)
                fr.append(tp)
                d, bf, fr = MT.take()
                tc = act(lambda e, d=d, bank=bank: e.activation(d[:, 0:256], bank[:, 0:256], ACT.Copy), tp, bf)
                free.append(tc)
                bank, before, free = PS.take()
                tp = pe(lambda e, j=j, d=d, bank=bank: e.matmul(bank[:, 0:256], WPF[:, 2 + j, :], d[:, 0:256],
                                                                start=True, stop=True), tc, before, rdy_wp)
                fr.append(tp)
                free.extend(out_split(bank, 6 + j, 256 * s, tp))
        if ada_rest:
            ada_rest.pop()()
        for item in const:
            item.done.append(pe.last())
        ring.kept = set()
        t_mixers = fence()
        rdy_wp = load_mixer_weights(1, [pe.last()]) if both else None
        chunks_o = [wide(A["w_out"][i], 256 * c, 256) for c in range(4)]

        def residual(gate, sums=None):
            def f(j, bank, tp):
                out = []
                for s in streams:
                    sl = slice(256 * s, 256 * s + 256)
                    out.append(dve(lambda e, sl=sl, s=s: e.scalar_tensor_tensor(
                        XT[:, j, sl], bank[:, sl], MOD[:, i, gate + j, s:s + 1], XT[:, j, sl], ALU.mult, ALU.add),
                        tp, t_xw[j], t_mod[i]))
                t_xw[j] = out
                if sums is not None:
                    sums.late(j, t_xw)
                return out
            return f

        t_xw = [[t, fence()] for t in t_x]
        tiles = [([(chunks_o[m // 2], 128 * (m % 2), 8)], 128) for m in range(8)]
        TB = Buffers(tmp[:7], t_mixers)
        sums = Sums(N, TB)
        linear(tiles, lambda k: GH[:, k, 0:N], lambda k: GL[:, k, 0:N], t_m, N, residual(16, sums))
        t_sg2 = dve(lambda e: e.scalar_tensor_tensor(
            SG[:, :, :], MOD[:, i, 32:40, 0:2], 1.0,
            VEC[:, V_GFFN + 8 * i:V_GFFN + 8 * i + 8].unsqueeze(2).to_broadcast([128, 8, 2]),
            ALU.add, ALU.mult), t_mod[i], t_mixers)
        scales = [((256 * s, 256 * s + 256), lambda k, s=s: SG[:, k, s:s + 1],
                   lambda k, s=s: MOD[:, i, 24 + k, s:s + 1], t_sg2) for s in streams]
        def items_of(half):
            items = []
            for c in range(0, 1408, 256):
                n = min(256, 1408 - c)
                gate = wide(A["w_gate_up"][i], 1408 * half + c, n)
                up = wide(A["w_gate_up"][i], 2816 + 1408 * half + c, n)
                for j in range(n // 128):
                    items += [([(gate, 128 * j, 8)], 128), ([(up, 128 * j, 8)], 128)]
            return items
        items = items_of(0)
        first = split_weights(*items[0])
        t_h = adaln(sums, scales, lambda k: HH[:, k, 0:N], lambda k: HL[:, k, 0:N], t_mixers)
        xh, xl = lambda k: HH[:, k, 0:N], lambda k: HL[:, k, 0:N]
        g_free = fence()
        for half in range(2):
            if half:
                items, first = items_of(1), None
            t_g = [[] for _ in range(HALF)]
            held = {}

            def evac(j, bank, tp):
                m = j // 2
                if j % 2 == 0:
                    t, bf, fr = TB.take()
                    ts = act(lambda e: e.activation(t[:, 0:N], bank[:, 0:N], ACT.Silu), tp, bf)
                    held[m] = (t, fr, ts)
                    return [ts]
                t, fr, ts = held.pop(m)
                t2 = dve(lambda e: e.tensor_tensor(t[:, 0:N], bank[:, 0:N], t[:, 0:N], ALU.mult), tp, ts)
                th, tl = split_out(t[:, 0:N], GH[:, m, 0:N], GL[:, m, 0:N], t2, g_free)
                fr.append(tl)
                t_g[m] += [th, tl]
                return [t2]
            linear(items, xh, xl, t_h, N, evac, None, first)
            t_read = fence()
            downs = []
            vd = A["w_down"][i].rearrange("(k p) n -> p k n", p=128)
            for c in range(4):
                pair = []
                for k0, kn in ((0, 6), (6, 5)):
                    def fill(e, place, sem, c=c, k0=k0, kn=kn, half=half):
                        e.dma_start(place[:, 0:kn * 256].rearrange("p (k n) -> p k n", k=kn),
                                    vd[:, HALF * half + k0:HALF * half + k0 + kn, 256 * c:256 * c + 256])\
                            .then_inc(sem, 16)
                    pair.append((Chunk(lambda fill=fill: ring.load(fill),
                                       lambda place, kn=kn: fm(place[:, 0:kn * 256], kn)), kn))
                downs += [([(ck, 128 * j, kn) for ck, kn in pair], 128) for j in range(2)]
            nxt_sums = Sums(N, TB) if half else None
            linear(downs, lambda k: GH[:, k, 0:N], lambda k: GL[:, k, 0:N], t_g, N, residual(40, nxt_sums))
            g_free = fence()
        return t_xw, rdy_wp, nxt_sums, t_read, g_free

    def second(t_x, sums, t_read):
        N = 256
        V2 = 2
        M2H = at("M2H", [128, 8, 256], F32R, oG)
        M2L = at("M2L", [128, 8, 256], F32R, oG + 8 * KB)
        o = oG + 16 * KB
        QKM = at("QKM", [128, 8, 259], F32, o)
        QK2 = at("QK2", [128, 8, 256], F32, o + 8320)
        TWO = at("TWO", [128, B_END], F32, o + 16512)
        CS2 = at("CS2", [128, 2, 256], F32, o + 20128)
        GI = at("GI", [4, 256], F32, o + 22176)
        GF = at("GF", [4, 256], F32, o + 23200)
        BG = at("BG", [4, 2], F32, o + 24224)
        SEL = at("SEL", [4, 4, 128], F32, o + 24256)
        QA = at("QA", [128, 4, 256], F32, oZ)
        KA = at("KA", [128, 4, 256], F32, oZ + 4 * KB)
        VA = at("VA", [128, 2, 512], F32, oZ + 8 * KB)
        VM = at("VM", [128, 2, 512], F32, oZ + 12 * KB)
        OM = at("OM", [128, 4, 256], F32, oZ + 16 * KB)
        start = fence()
        s_two = nc.alloc_semaphore("s_two")
        pool.raw(lambda e: e.dma_start(TWO[:, :], A["k_two"]).then_inc(s_two, 16), start)
        for j in range(2):
            pool.raw(lambda e, j=j: e.dma_start(
                BG[:, j:j + 1], A["b_gate_2"][0][4 * j:4 * j + 4].rearrange("(h o) -> h o", o=1)).then_inc(s_two, 16),
                start)
        POSI = at("POSI", [128, 256], I32, o + 8320 + 7168)
        pool.raw(lambda e: e.dma_start(POSI[:, :], A["positions_2"][0].partition_broadcast(128)).then_inc(s_two, 16),
                 start)
        r_two = (s_two, 64)
        late = {}

        def tables():
            ang, nn, rr, rc, mk = (QK2[:, j, :] for j in range(5))
            t = dve(lambda e: e.tensor_copy(ang, POSI[:, :]), r_two, start)
            t = dve(lambda e: e.tensor_scalar(ang, ang, TWO[:, B_FREQ:B_FREQ + 1], None, ALU.mult), t)
            t = dve(lambda e: e.tensor_scalar(nn, ang, float(1 / (2 * np.pi)), 12582912.0, ALU.mult, ALU.add), t)
            t = dve(lambda e: e.tensor_scalar(nn, nn, 12582912.0, None, ALU.subtract), t)
            c1 = 6.28125
            c2 = float(np.float32(np.round((2 * np.pi - c1) * 2 ** 20) / 2 ** 20))
            c3 = float(2 * np.pi - c1 - c2)
            src = ang
            for c in (c1, c2, c3):
                t = dve(lambda e, c=c, src=src: e.scalar_tensor_tensor(rr, nn, -c, src, ALU.mult, ALU.add), t)
                src = rr
            LIM = 3.1415925
            t = dve(lambda e: e.tensor_scalar(rr, rr, LIM, -LIM, ALU.min, ALU.max), t)
            t_sin = act(lambda e: e.activation(CS2[:, 1, :], rr, ACT.Sin), t, start)
            t = dve(lambda e: e.tensor_scalar(rc, rr, float(np.pi / 2), None, ALU.add), t)
            t = dve(lambda e: e.tensor_scalar(mk, rc, float(np.pi), float(-2 * np.pi), ALU.is_gt, ALU.mult), t)
            t = dve(lambda e: e.tensor_tensor(rc, rc, mk, ALU.add), t)
            t = dve(lambda e: e.tensor_scalar(rc, rc, LIM, -LIM, ALU.min, ALU.max), t)
            t_cs = act(lambda e: e.activation(CS2[:, 0, :], rc, ACT.Sin), t)
            t_pad = dve(lambda e: e.memset(QKM[:, :, 0:3], 0.0), start)
            t_sel = [dve(lambda e, h=h: e.tensor_scalar(SEL[:, h, :], ONES[0:4, :], ident[0:4, h:h + 1], None, ALU.mult),
                         start, t_ones, (s_res, 16)) for h in range(4)]
            late.update(t_sin=t_sin, t_cs=t_cs, t_pad=t_pad, t_sel=t_sel)

        t_sg = dve(lambda e: e.scalar_tensor_tensor(
            SG[:, :, 0], MOD[:, 2, 8:16, V2], 1.0, VEC[:, V_N1:V_N1 + 8], ALU.add, ALU.mult), t_mod[2], t_vec, start)
        scales = [((0, 256), lambda k: SG[:, k, 0:1], lambda k: MOD[:, 2, k, V2:V2 + 1], t_sg)]
        xh, xl = lambda k: HH[:, k, 0:N], lambda k: HL[:, k, 0:N]
        chunks = [wide(A["w_in_2"][0], 256 * c, min(256, 3592 - 256 * c)) for c in range(15)]
        tiles = [([(chunks[m // 2], 128 * (m % 2), 8)], 128) for m in range(28)]
        tiles += [([(chunks[14], 4 * j, 8)], 4) for j in range(2)]
        first = split_weights(*tiles[0])
        t_h = adaln(sums, scales, xh, xl, t_read)
        zfree = fence()
        t_qa, t_ka, t_va, t_qk, t_vm, t_om, t_g = ([] for _ in range(7))
        zt2 = [at(f"ZU{j}", [128, 256], F32, oG + KB * j) for j in range(3)]
        ZT = Buffers(zt2, start)

        def rows_of(bank, tp, dst, m, toks):
            tb, bf, fr = ZT.take()
            tc = act(lambda e: e.activation(tb[:, :], bank[:, 0:256], ACT.Copy), tp, bf)
            bank2, before, free2 = PS.take()

            def tr(e):
                for a in range(2):
                    last = e.transpose(bank2[:, 128 * a:128 * a + 128], tb[:, 128 * a:128 * a + 128], ident)
                return last
            tt = pe(tr, tc, before)
            fr.append(tt)
            td = dve(lambda e: e.tensor_copy(dst[:, :, 128 * m:128 * m + 128],
                                             bank2[:, 0:256].rearrange("p (a n) -> p a n", n=128)), tt, zfree)
            free2.append(td)
            toks.append(td)
            return [tc]

        def conv(j, tq):
            out = QK2[:, j, :]
            w = [VEC[:, V_CW + 8 * t + j:V_CW + 8 * t + j + 1] for t in range(4)]
            t1 = dve(lambda e: e.tensor_scalar(out, QKM[:, j, 0:256], w[0], VEC[:, V_CB + j:V_CB + j + 1],
                                               ALU.mult, ALU.add), tq, late["t_pad"], late["t_cs"], late["t_sin"])
            for i in range(1, 4):
                t1 = dve(lambda e, i=i: e.scalar_tensor_tensor(out, QKM[:, j, i:i + 256], w[i], out,
                                                               ALU.mult, ALU.add), t1)
            t1 = act(lambda e: e.activation(out, out, ACT.Silu), t1)
            if j >= 4:
                t1 = dve(lambda e: e.tensor_scalar(out, out, float(128 ** -0.5), None, ALU.mult), t1)
            t_qk.append(t1)

        def evac(i, bank, tp):
            if i == 1:
                tables()
            if i < 4:
                t1 = act(lambda e: e.activation(QA[:, i, :], bank[:, 0:256], ACT.Copy, scale=0.125), tp, zfree)
                t_qa.append(t1)
            elif i < 8:
                t1 = act(lambda e: e.activation(KA[:, i - 4, :], bank[:, 0:256], ACT.Copy), tp, zfree)
                t_ka.append(t1)
            elif i < 12:
                return rows_of(bank, tp, VA, i - 8, t_va)
            elif i < 20:
                t1 = dve(lambda e: e.tensor_copy(QKM[:, i - 12, 3:259], bank[:, 0:256]), tp, start)
                conv(i - 12, t1)
            elif i < 24:
                return rows_of(bank, tp, VM, i - 20, t_vm)
            elif i < 28:
                t1 = act(lambda e: e.activation(OM[:, i - 24, :], bank[:, 0:256], ACT.Sigmoid), tp, zfree)
                t_om.append(t1)
            else:
                dst = (GI, GF)[i - 28]
                t1 = dve(lambda e: e.tensor_scalar(dst[:, :], bank[0:4, 0:256], BG[:, i - 28:i - 27], None, ALU.add),
                         tp, r_two)
                t_g.append(t1)
            return [t1]
        linear(tiles, xh, xl, t_h, N, evac, None, first)
        pb2 = [at(f"PB{i}", [128, 256], F32, oH + 18 * KB + KB * i) for i in range(6)]
        t_cs, t_sin, t_sel = late["t_cs"], late["t_sin"], late["t_sel"]
        hfree = fence()
        MT, PB, PTB = Buffers(mt, hfree), Buffers(pb2, hfree), Buffers(ptbuf, hfree)
        QRB = at("QRB", [128, 4, 256], F32, oH)
        KRB = at("KRB", [128, 4, 256], F32, oH + 4 * KB)
        t_r = []
        for m in range(4):
            pair = []
            for src, dst, tq in ((QA, QRB, t_qa[m]), (KA, KRB, t_ka[m])):
                bank, before, free = PS.take()
                tp = pe(lambda e, src=src, m=m, bank=bank: e.matmul(
                    bank[:, 0:256], TWO[:, B_R2:B_R2 + 128], src[:, m, :], start=True, stop=True), tq, before, r_two)
                t1, t3 = rope_into(dst[:, m, :], src[:, m, :], bank[:, 0:256], CS2[:, 0, :], CS2[:, 1, :], MT,
                                   [tp, t_cs, t_sin], hfree)
                free.append(t1)
                pair.append(t3)
            t_r.append(pair)
        t_m = [[] for _ in range(8)]

        t_att = []
        AO = [XT[:, 1 + p, 256:512] for p in range(4)]

        def split_mixed(m, src, t3):
            th, tl = split_out(src, M2H[:, m, :], M2L[:, m, :], t3, hfree)
            t_m[m] += [th, tl]

        def pair_done(p, bank, tp):
            tc = act(lambda e: e.activation(AO[p], bank[:, 0:256], ACT.Copy), tp, hfree)
            t_att.append(tc)
            return [tc]

        jobs = [{
            "q": lambda a, r=64 * (h % 2), m=h // 2: QRB[r:r + 64, m, 128 * a:128 * a + 128],
            "k": lambda n, r=64 * (h % 2), m=h // 2: KRB[r:r + 64, m, 0:n],
            "v": lambda j, h=h: VA[:, j, 64 * h:64 * h + 64],
            "nk": [1, 2],
            "mask": lambda a: TWO[:, B_TRI + 128 * (1 - a):B_TRI + 256],
            "waits": [t_r[h // 2], t_va],
        } for h in range(8)]
        attention(jobs, PB, PTB, pair_done)
        SQ4 = Buffers([at(f"SQ{j}", [128, 256], F32, oH + 8 * KB + KB * j) for j in range(4)], hfree)
        t3s = head_norms([(AO[p], 256, VEC[:, V_AG + p:V_AG + p + 1], AO[p], t_att[p]) for p in range(4)], SQ4)
        for p in range(4):
            split_mixed(p, AO[p], t3s[p])
        lfree = fence()
        G4 = at("G4", [4, 8, 256], F32, oH)
        ab, lf, cum, bb, mm_, em, wi, nm = (G4[:, j, :] for j in range(8))
        BC = at("BC", [128, 2, 4], F32, oH + 8 * KB)
        S1 = at("S1", [4, 1], F32, oH + 8 * KB + 64)
        names = ("WT", "QW", "KW", "SWt", "DN")
        WT, QW, KW, SWt, DN = (at(nm_, [128, 4, 256], F32, oH + 9 * KB + 4 * KB * j) for j, nm_ in enumerate(names))
        CNa = at("CNa", [128, 256], F32, oH + 29 * KB)
        CNb = at("CNb", [128, 256], F32, oH + 30 * KB)
        CNc = at("CNc", [128, 256], F32, oH + 31 * KB)
        cns = [CNa[:, :], CNb[:, :], CNc[:, :], XT[:, 0, 256:512]]
        ones4 = ONES[0:4, 0:128]
        t1 = act(lambda e: e.activation(ab, GF[:, :], ACT.Abs), t_g, lfree)
        t1 = act(lambda e: e.activation(ab, ab, ACT.Exp, scale=-1.0), t1)
        t1 = act(lambda e: e.activation(ab, ab, ACT.Ln, bias=ONES[0:4, 0:1]), t1)
        t1 = dve(lambda e: e.scalar_tensor_tensor(lf, GF[:, :], 0.0, ab, ALU.min, ALU.subtract), t1, t_g)
        ts = [dve(lambda e, c=c: e.tensor_tensor_scan(cum[:, 128 * c:128 * c + 128], ones4,
                                                      lf[:, 128 * c:128 * c + 128], 0.0, ALU.mult, ALU.add), t1)
              for c in range(2)]
        tb_ = dve(lambda e: e.tensor_tensor(bb, GI[:, :], cum, ALU.subtract), ts, t_g)
        t2 = dve(lambda e: e.tensor_tensor_scan(mm_[:, 0:128], bb[:, 0:128], bb[:, 0:128], 0.0, ALU.max, ALU.max), tb_)
        tm0 = dve(lambda e: e.tensor_tensor(S1[:, :], cum[:, 127:128], mm_[:, 127:128], ALU.add), t2)
        t3 = dve(lambda e: e.tensor_tensor_scan(mm_[:, 128:256], bb[:, 128:256], bb[:, 128:256], S1[:, 0:1],
                                                ALU.max, ALU.max), tm0)
        tn_ = dve(lambda e: e.tensor_scalar(nm, mm_, -1.0, None, ALU.mult), t3)
        te = dve(lambda e: e.tensor_tensor(em, cum, mm_, ALU.add), t3)
        te = act(lambda e: e.activation(em, em, ACT.Exp, scale=-1.0), te)
        tw = act(lambda e: e.activation(wi[:, 0:128], mm_[:, 128:256], ACT.Exp, bias=S1[:, 0:1], scale=-1.0), t3)
        bank, before, free = PS.take()

        def tr(e, bank=bank):
            for c in range(2):
                last = e.transpose(bank[:, 4 * c:4 * c + 4], bb[:, 128 * c:128 * c + 128], ident[0:4, 0:4])
            return last
        tp = pe(tr, tb_, before)
        t_bc = dve(lambda e, bank=bank: e.tensor_copy(BC[:, :, :], bank[:, 0:8].rearrange("p (c h) -> p c h", c=2)),
                   tp, lfree)
        free.append(t_bc)
        t_wt, t_qw, t_kw = [], [], []
        for h in range(4):
            bank, before, free = PS.take()
            tp = pe(lambda e, h=h, bank=bank: e.matmul(bank[:, 0:256], SEL[:, h, :], nm, start=True, stop=True),
                    tn_, t_sel, before)
            t1 = dve(lambda e, h=h, bank=bank: e.tensor_tensor(
                WT[:, h, :].rearrange("p (c n) -> p c n", c=2), bank[:, 0:256].rearrange("p (c n) -> p c n", c=2),
                TWO[:, B_TRIT:B_TRIT + 128].unsqueeze(1).to_broadcast([128, 2, 128]), ALU.add), tp, lfree)
            free.append(t1)
            w2_ = [act(lambda e, h=h, c=c: e.activation(WT[:, h, 128 * c:128 * c + 128], WT[:, h, 128 * c:128 * c + 128],
                                                        ACT.Exp, bias=BC[:, c, h:h + 1]), t1, t_bc) for c in range(2)]
            t_wt.append(w2_)
            bank, before, free = PS.take()
            tp = pe(lambda e, h=h, bank=bank: e.matmul(bank[:, 0:128], SEL[:, h, :], wi[:, 0:128],
                                                       start=True, stop=True), tw, before)
            t1 = dve(lambda e, h=h, bank=bank: e.tensor_tensor(QW[:, h, 0:128], QK2[:, h, 128:256], bank[:, 0:128],
                                                               ALU.mult), tp, t_qk, lfree)
            free.append(t1)
            t_qw.append(t1)
            bank, before, free = PS.take()
            tp = pe(lambda e, h=h, bank=bank: e.transpose(bank[:, 0:128], QK2[:, 4 + h, 0:128], ident), t_qk, before)
            t1 = dve(lambda e, h=h, bank=bank: e.tensor_scalar(KW[:, h, 0:128], bank[:, 0:128], WT[:, h, 127:128], None,
                                                               ALU.mult), tp, w2_, lfree)
            free.append(t1)
            t_kw.append(t1)
        t_den, chunk_tokens = [], []
        for h in range(4):
            bank, before, free = PS.take()

            def st_mm(e, h=h, bank=bank):
                e.matmul(bank[:, 0:128], KW[:, h, 0:128], VM[:, 0, 128 * h:128 * h + 128], start=True, stop=True)
                return e.matmul(bank[:, 128:256], KW[:, h, 0:128], ONES[:, :], start=True, stop=True)
            tp = pe(st_mm, t_kw[h], t_vm, before)
            cn = cns[h]
            t_cn = act(lambda e, cn=cn, bank=bank: e.activation(cn, bank[:, 0:256], ACT.Copy), tp, lfree)
            free.append(t_cn)
            bank, before, free = PS.take()

            def s_mm(e, h=h, bank=bank):
                for c in range(2):
                    sl = slice(128 * c, 128 * c + 128)
                    last = e.matmul(bank[:, sl], QK2[:, 4 + h, sl], QK2[:, h, sl], start=True, stop=True)
                return last
            tp = pe(s_mm, t_qk, before)
            t_s = dve(lambda e, h=h, bank=bank: e.tensor_tensor(SWt[:, h, :], bank[:, 0:256], WT[:, h, :], ALU.mult),
                      tp, t_wt[h], lfree)
            free.append(t_s)
            chunk_tokens.append((cn, t_cn, t_s))
        for h in range(4):
            cn, t_cn, t_s = chunk_tokens[h]
            bn, before, free_n = PS.take()
            bd_, before2, free_d = PS.take()

            def n_mm(e, h=h, bn=bn, bd_=bd_, cn=cn):
                for bk, lhs, st_ in ((bn, lambda c: VM[:, c, 128 * h:128 * h + 128], cn[:, 0:128]),
                                     (bd_, lambda c: ONES[:, :], cn[:, 128:256])):
                    e.matmul(bk[:, 0:128], lhs(0), SWt[:, h, 0:128], start=True, stop=True)
                    e.matmul(bk[:, 128:256], lhs(1), SWt[:, h, 128:256], start=True, stop=False)
                    last = e.matmul(bk[:, 128:256], st_, QW[:, h, 0:128], start=False, stop=True)
                return last
            tp = pe(n_mm, t_s, t_cn, t_qw[h], t_vm, before, before2)
            be, before, free_e = PS.take()
            tpe = pe(lambda e, h=h, be=be: e.matmul(be[:, 0:256], SEL[:, h, :], em, start=True, stop=True), te, before)
            d = DN[:, h, :]
            t1 = act(lambda e, d=d, bd_=bd_: e.activation(d, bd_[:, 0:256], ACT.Abs), tp, lfree)
            free_d.append(t1)
            t1 = dve(lambda e, d=d, be=be: e.tensor_tensor(d, be[:, 0:256], d, ALU.max), t1, tpe)
            free_e.append(t1)
            t1 = dve(lambda e, d=d: e.reciprocal(d, d), t1)
            t1 = dve(lambda e, d=d, bn=bn: e.tensor_tensor(d, bn[:, 0:256], d, ALU.mult), t1, tp)
            free_n.append(t1)
            t_den.append(t1)
        t3s = head_norms([(DN[:, h, :], 256, VEC[:, V_MG + h:V_MG + h + 1], DN[:, h, :], t_den[h]) for h in range(4)],
                         Buffers([SWt[:, h, :] for h in range(4)], [tp]), 1.0 / 128, ONES[:, :])
        for h in range(4):
            t4 = dve(lambda e, h=h: e.tensor_tensor(DN[:, h, :], DN[:, h, :], OM[:, h, :], ALU.mult), t3s[h], t_om)
            split_mixed(4 + h, DN[:, h, :], t4)
        t_xw = [[t, fence()] for t in t_x]

        def residual2(i, bank, tp):
            t1 = dve(lambda e: e.scalar_tensor_tensor(XT[:, i, 0:256], bank[:, 0:256], MOD[:, 2, 16 + i, V2:V2 + 1],
                                                      XT[:, i, 0:256], ALU.mult, ALU.add), tp, t_xw[i])
            t_xw[i] = [t1]
            sums.late(i, t_xw)
            return [t1]
        TB = Buffers(tmp[:7], [pe.last()])
        for f in TB.free:
            f.extend(t_xw[0])
        sums = Sums(N, TB)
        chunks_o = [wide(A["w_out_2"][0], 256 * c, 256) for c in range(4)]
        linear([([(chunks_o[m // 2], 128 * (m % 2), 8)], 128) for m in range(8)],
               lambda k: M2H[:, k, :], lambda k: M2L[:, k, :], t_m, N, residual2)
        t_dense = fence()
        H2 = at("H2", [128, 8, 256], F32, o)
        WR = at("WR", [128, 8, 36], F32, oZ + 16 * KB)
        RB = at("RB", [128, 36], F32, oZ + 16 * KB + 1152)
        s_wr = nc.alloc_semaphore("s_wr")
        for c0, n, wn, bn_ in ((0, 4, "w_rg_2", "b_rg_2"), (4, 32, "w_re_2", "b_re_2")):
            pool.raw(lambda e, c0=c0, n=n, wn=wn: e.dma_start(
                WR[:, :, c0:c0 + n], A[wn][0].rearrange("(k p) n -> p k n", p=128)).then_inc(s_wr, 16), lfree, t_m[7])
            pool.raw(lambda e, c0=c0, n=n, bn_=bn_: e.dma_start(
                RB[:, c0:c0 + n], A[bn_][0].partition_broadcast(128)).then_inc(s_wr, 16))
        t_sg = dve(lambda e: e.scalar_tensor_tensor(
            SG[:, :, 0], MOD[:, 2, 32:40, V2], 1.0, VEC[:, V_N2:V_N2 + 8], ALU.add, ALU.mult), t_dense)
        scales = [((0, 256), lambda k: SG[:, k, 0:1], lambda k: MOD[:, 2, 24 + k, V2:V2 + 1], t_sg)]
        t_h2 = adaln(sums, scales, None, None, t_dense, keep=lambda k: H2[:, k, :])
        rfree = fence()
        rt = at("RT", [128, 1800], F32, oZ)
        off = [0]

        def small(*shape):
            n = int(np.prod(shape))
            ap = rt[:, off[0]:off[0] + n]
            off[0] += n
            if len(shape) == 2:
                ap = ap.rearrange("p (a b) -> p a b", a=shape[0])
            elif len(shape) == 3:
                ap = ap.rearrange("p (a b c) -> p a b c", a=shape[0], b=shape[1])
            return ap
        LG, G8, MX, MXE = small(2, 36), small(2, 8), small(2, 8), small(2, 8)
        IX, IXE = small(2, 8), small(2, 8)
        EG, GW, GIF, OG, EP, E8 = small(2, 4), small(2), small(2), small(2, 4), small(2, 32), small(2, 8)
        R1, RD, WGT, IDF = small(2), small(2), small(2, 2), small(2, 2)
        AA, A01, PR, PC = small(4, 32), small(2, 32), small(4, 32), small(96)
        PP, S0, S1b, BIG, GS, BLK, POS = (small(4) for _ in range(7))
        IND, XI, TX, BS, TJ, EIA = small(32), small(32), small(32), small(2, 32), small(32), small(16)
        GB, PM, iota2 = small(4, N_BLOCKS), small(N_BLOCKS), small(128)
        WS_ = small(N_BLOCKS)
        INTS = at("INTS", [128, 16], I32, oZ + 8128)
        ints = []
        wm_at = [(at(f"MH{i}", [128, 1024], F32R, o_), at(f"ML{i}", [128, 1024], F32R, o_ + 4 * KB))
                      for i, o_ in enumerate([oH + 8 * KB * j for j in range(4)] + [oW, oW + 8 * KB])]
        w_src = (A["w1_2"][0], A["w3_2"][0], A["w2_2"][0])
        def expert_loads(which, extra):
            regs = {}

            def fill(j):
                src, k = w_src[j // 2], j % 2
                n = 512 if j < 4 else 1024
                kn = 2048 // n

                def f(e, place, sem):
                    dst = place[:, :].rearrange("p (k n) -> p k n", k=kn)
                    if not extra:
                        e.dma_start(dst, src[which].rearrange("(k p) n -> p k n", p=128)[:, kn * k:kn * k + kn, :])\
                            .then_inc(sem, 16)
                        return
                    if j == 0:
                        e.wait_ge(*ints[0])
                        regs["e"] = e.value_load(INTS[0:1, which:which + 1], min_val=0, max_val=N_EXP - 1)
                        regs["on"] = e.value_load(INTS[0:1, 7 + which:8 + which], min_val=0, max_val=1)
                    v = src[bass.ds(regs["e"], 1)].rearrange("a (k p) n -> p (a k) n", p=128)
                    e.dma_start(dst, v[:, kn * k:kn * k + kn, :], cond=regs["on"]).then_inc(sem, 16)
                return f
            return [fill(j) for j in range(6)]

        n_part = [0]

        def part_of(item, u, act, dve, pool, WM, eng=None):
            (wh, wl), bf, fr = WM.take()
            src = item.place[:, 1024 * u:1024 * u + 1024]
            th = act(lambda e: e.activation(wh[:, :], src, ACT.Copy), item.ready, bf)
            n_part[0] += 1
            eng = eng or (pool if n_part[0] % 4 == 0 else dve)
            tl = eng(lambda e: e.tensor_tensor(wl[:, :], src, wh[:, :].bitcast(F32), ALU.subtract),
                     item.ready, bf, th)
            item.done.append(tl)
            return wh, wl, th, tl, fr

        AHEAD = 5
        WM = Buffers(wm_at, t_dense)
        primed = []
        for f in expert_loads(0, False)[0:3]:
            item = ring.load(f)
            primed += [part_of(item, u, act, dve, pool, WM, pool) for u in (0, 1)]
        bank, before, free = PS.take()

        def lg(e, bank=bank):
            for a in range(2):
                for k in range(KT):
                    last = e.matmul(bank[:, 36 * a:36 * a + 36], H2[:, k, 128 * a:128 * a + 128], WR[:, k, :],
                                    start=(k == 0), stop=(k == KT - 1))
            return last
        tp_lg = pe(lg, t_h2, (s_wr, 64), before)
        H2P = at("H2P", [128, 3, 2, 1024], BF16, oG)
        HR = Buffers([at(f"HR{i}", [128, 512], F32, oG + 12 * KB + 2 * KB * i) for i in range(2)], [rfree])
        t_h2p = []
        for a in range(2):
            for hf in range(2):
                bank_, before, free = PS.take()

                def tr(e, a=a, hf=hf, bank_=bank_):
                    for k in range(4):
                        last = e.transpose(bank_[:, 128 * k:128 * k + 128], H2[:, 4 * hf + k, 128 * a:128 * a + 128], ident)
                    return last
                tp = pe(tr, t_h2, before)
                sl = slice(512 * hf, 512 * hf + 512)
                r, bf, fr = HR.take()
                t1 = act(lambda e, a=a, sl=sl, bank_=bank_: e.activation(H2P[:, 0, a, sl], bank_[:, :], ACT.Copy), tp, rfree)
                t2 = dve(lambda e, a=a, sl=sl, bank_=bank_, r=r: e.tensor_tensor(r[:, :], bank_[:, :], H2P[:, 0, a, sl],
                                                                               ALU.subtract), t1, tp, bf)
                free.append(t2)
                t3 = act(lambda e, a=a, sl=sl, r=r: e.activation(H2P[:, 1, a, sl], r[:, :], ACT.Copy), t2)
                t4 = dve(lambda e, a=a, sl=sl, r=r: e.tensor_tensor(H2P[:, 2, a, sl], r[:, :], H2P[:, 1, a, sl],
                                                                    ALU.subtract), t3)
                fr.append(t4)
                t_h2p += [t1, t3, t4]
        dq = [None]

        def d(fn, *w):
            dq[0] = dve(fn, dq[0], *w)
            return dq[0]
        tp, bank_lg = tp_lg, bank
        t = d(lambda e: e.tensor_tensor(LG, bank_lg[:, 0:72].rearrange("p (a n) -> p a n", a=2),
                                        RB[:, :].unsqueeze(1).to_broadcast([128, 2, 36]), ALU.add), tp, rfree)
        free.append(t)
        d(lambda e: e.memset(G8, -3.0e38))
        d(lambda e: e.tensor_copy(G8[:, :, 0:4], LG[:, :, 0:4]))

        def top(src, mx, ix):
            for a in range(2):
                d(lambda e, a=a: e.max(mx[:, a, :], src[:, a, :]))
                d(lambda e, a=a: e.max_index(ix[:, a, :].bitcast(U32), mx[:, a, :], src[:, a, :]))
        top(G8, MX, IX)
        d(lambda e: e.tensor_copy(GIF, IX[:, :, 0].bitcast(U32)))
        t = d(lambda e: e.tensor_tensor(EG, LG[:, :, 0:4], MX[:, :, 0:1].to_broadcast([128, 2, 4]), ALU.subtract))
        t = act(lambda e: e.activation(EG, EG, ACT.Exp), t)
        iota = TWO[:, B_IOTA:B_IOTA + 128]
        d(lambda e: e.tensor_tensor(OG, iota[:, 0:4].unsqueeze(1).to_broadcast([128, 2, 4]),
                                    GIF.unsqueeze(2).to_broadcast([128, 2, 4]), ALU.is_equal))
        for a in range(2):
            d(lambda e, a=a: e.tensor_tensor(
                EP[:, a, :].rearrange("p (j g) -> p j g", g=4),
                LG[:, a, 4:36].rearrange("p (g j) -> p j g", g=4),
                OG[:, a, :].unsqueeze(1).to_broadcast([128, 8, 4]), ALU.mult))
        d(lambda e: e.tensor_reduce(E8, EP.rearrange("p a (j g) -> p a j g", g=4), AX.X, ALU.add))
        top(E8, MXE, IXE)
        d(lambda e: e.tensor_reduce(GW, EG, AX.X, ALU.add), t)
        d(lambda e: e.reciprocal(GW, GW))
        t = d(lambda e: e.tensor_tensor(R1, MXE[:, :, 1], MXE[:, :, 0], ALU.subtract))
        t = act(lambda e: e.activation(R1, R1, ACT.Exp), t)
        d(lambda e: e.tensor_copy(IDF, IXE[:, :, 0:2].bitcast(U32)))
        d(lambda e: e.scalar_tensor_tensor(IDF, GIF.unsqueeze(2).to_broadcast([128, 2, 2]), 8.0, IDF,
                                           ALU.mult, ALU.add))
        d(lambda e: e.tensor_tensor(AA, iota[:, 0:32].unsqueeze(1).to_broadcast([128, 4, 32]),
                                    IDF.rearrange("p a k -> p (a k)").unsqueeze(2).to_broadcast([128, 4, 32]),
                                    ALU.is_equal))
        A4 = AA.rearrange("p (a k) n -> p a k n", a=2)
        t_a = d(lambda e: e.tensor_tensor(A01, A4[:, :, 0, :], A4[:, :, 1, :], ALU.add))
        bank2, before, free2 = PS.take()

        def cnt(e):
            slt = TWO[:, B_SLT:B_SLT + 128]
            e.matmul(bank2[:, 0:32], slt, A01[:, 0, :], start=True, stop=True)
            e.matmul(bank2[:, 32:64], slt, A01[:, 1, :], start=True, stop=False)
            e.matmul(bank2[:, 32:64], ONES[:, :], A01[:, 0, :], start=False, stop=True)
            e.matmul(bank2[:, 64:96], ONES[:, :], A01[:, 0, :], start=True, stop=False)
            return e.matmul(bank2[:, 64:96], ONES[:, :], A01[:, 1, :], start=False, stop=True)
        tp = pe(cnt, t_a, before)
        d(lambda e: e.tensor_scalar(RD, R1, 1.0, None, ALU.add), t)
        d(lambda e: e.reciprocal(RD, RD))
        d(lambda e: e.tensor_tensor(WGT[:, :, 0], GW, RD, ALU.mult))
        t_wgt = d(lambda e: e.tensor_tensor(WGT[:, :, 1], WGT[:, :, 0], R1, ALU.mult))
        free2.append(d(lambda e: e.tensor_copy(PC, bank2[:, 0:96]), tp))
        d(lambda e: e.tensor_scalar(IND, PC[:, 64:96], float(CAP), None, ALU.is_gt))
        for j in (2, 3):
            d(lambda e, j=j: e.scalar_tensor_tensor(IND, PC[:, 64:96], float(j * CAP), IND, ALU.is_gt, ALU.add))
        d(lambda e: e.tensor_tensor_scan(TX, ONES[:, 0:32], IND, 0.0, ALU.mult, ALU.add))
        d(lambda e: e.tensor_copy(EIA[:, 14:15], TX[:, 31:32]))
        d(lambda e: e.tensor_tensor(XI, TX, IND, ALU.subtract))
        d(lambda e: e.tensor_copy(BS[:, 0, :], iota[:, 0:32]))
        d(lambda e: e.tensor_scalar(BS[:, 1, :], XI, float(N_EXP - 1), None, ALU.add))
        for src, dst in ((PC[:, 0:64].rearrange("p (a n) -> p a n", a=2).unsqueeze(2).to_broadcast([128, 2, 2, 32]), PP),
                         (BS[:, 0, :].unsqueeze(1).to_broadcast([128, 4, 32]), S0),
                         (BS[:, 1, :].unsqueeze(1).to_broadcast([128, 4, 32]), S1b)):
            a_ = AA if src.ndim == 3 else A4
            p_ = PR if src.ndim == 3 else PR.rearrange("p (a k) n -> p a k n", a=2)
            d(lambda e, src=src, a_=a_, p_=p_: e.tensor_tensor(p_, a_, src, ALU.mult))
            d(lambda e, dst=dst: e.tensor_reduce(dst, PR, AX.X, ALU.add))
        d(lambda e: e.tensor_scalar(BIG, PP, float(CAP), None, ALU.is_ge))
        d(lambda e: e.tensor_tensor(S1b, S1b, S0, ALU.subtract))
        d(lambda e: e.tensor_tensor(S1b, S1b, BIG, ALU.mult))
        for j in (2, 3):
            d(lambda e, j=j: e.scalar_tensor_tensor(BIG, PP, float(j * CAP), BIG, ALU.is_ge, ALU.add))
        d(lambda e: e.scalar_tensor_tensor(POS, BIG, float(-CAP), PP, ALU.mult, ALU.add))
        d(lambda e: e.tensor_tensor(BLK, S0, S1b, ALU.add))
        d(lambda e: e.tensor_tensor(BLK, BLK, BIG, ALU.add))
        d(lambda e: e.scalar_tensor_tensor(GS, BLK, float(CAP), POS, ALU.mult, ALU.add))
        for q in range(4):
            d(lambda e, q=q: e.tensor_scalar(GB[:, q, :], iota[:, 0:N_BLOCKS], float(-CAP), GS[:, q:q + 1],
                                             ALU.mult, ALU.add))
        bmod = TWO[:, B_MOD:B_MOD + 128]
        bank3, before3, free3 = PS.take()
        tp = pe(lambda e: e.transpose(bank3[:, 0:128], bmod, ident), before3, r_two)
        free3.append(d(lambda e: e.tensor_scalar(PM, iota[:, 0:N_BLOCKS], float(CAP), bank3[:, 0:1], ALU.mult, ALU.add),
                       tp))
        d(lambda e: e.tensor_copy(iota2, iota))
        PW = at("PW", [128, 4, 128], F32, oZ + 8 * KB + 512)
        QW2 = at("QW2", [128, 4, N_BLOCKS], F32, oZ + 10 * KB + 512)
        DG = at("DG", [128, 4, 128], F32, oZ + 11 * KB + 512)
        GSR = at("GSR", [128, 2, 256], F32, oZ + 14 * KB)
        for q in range(4):
            d(lambda e, q=q: e.tensor_scalar(PW[:, q, :], bmod, POS[:, q:q + 1], None, ALU.is_equal))
            d(lambda e, q=q: e.tensor_scalar(QW2[:, q, :], iota[:, 0:N_BLOCKS], BLK[:, q:q + 1], WGT[:, q // 2, q % 2:q % 2 + 1],
                                             ALU.is_equal, ALU.mult))
            t_dg = d(lambda e, q=q: e.tensor_scalar(DG[:, q, :], ident, GS[:, q:q + 1], None, ALU.mult))
        bank4, before4, free4 = PS.take()
        bank5, before5, free5 = PS.take()

        def slots(e):
            for q in range(4):
                e.matmul(bank4[:, 0:N_BLOCKS], PW[:, q, :], QW2[:, q, :], start=(q == 0), stop=(q == 3))
            for q in range(4):
                c = 256 * (q % 2) + 128 * (q // 2)
                last = e.matmul(bank5[:, c:c + 128], ONES[:, :], DG[:, q, :], start=True, stop=True)
            return last
        tp = pe(slots, t_dg, before4, before5)
        free4.append(d(lambda e: e.tensor_copy(WS_, bank4[:, 0:N_BLOCKS]), tp))
        t_gb = d(lambda e: e.tensor_copy(GSR[:, :, :], bank5[:, :].rearrange("p (k n) -> p k n", k=2)), tp)
        free5.append(t_gb)
        t_gb = [t_gb]
        def extra_experts():
            for j in range(N_EXTRA):
                d(lambda e, j=j: e.tensor_scalar(TJ, XI, float(j), None, ALU.is_le))
                d(lambda e, j=j: e.scalar_tensor_tensor(TJ, TX, float(j), TJ, ALU.is_gt, ALU.mult))
                d(lambda e, j=j: e.tensor_tensor(TJ, TJ, iota2[:, 0:32], ALU.mult))
                d(lambda e, j=j: e.tensor_reduce(EIA[:, j:j + 1], TJ, AX.X, ALU.add))
                d(lambda e, j=j: e.tensor_scalar(EIA[:, 7 + j:8 + j], EIA[:, 14:15], float(j), None, ALU.is_gt))
            ints.append(d(lambda e: e.tensor_copy(INTS[:, 0:15], EIA[:, 0:15])))

        xg_at = [at(f"XG{i}", [128, 8, 128], F32R, oG + 24 * KB + 4 * KB * i) for i in range(2)]
        st_at = [at(f"ST{i}", [128, 256], F32R, oG + 32 * KB + KB * i) for i in range(4)]
        STT = at("STT", [128, 2, 256], F32, oG + 12 * KB)
        ZERO = at("ZERO", [128, 128], BF16, oG + 14 * KB)
        SBT = at("SBT", [128, 4, 64], BF16, oG + 14 * KB + 256)
        sb_at = [at(f"SB{i}", [128, 2, 64], BF16, oG + 14 * KB + 768 + 256 * i) for i in range(2)]
        sm_at = [at(f"SM{i}", [128, 4, 64], F32, oZ + 9 * KB + KB * i) for i in range(2)]
        u_at = [at(f"U{i}", [128, 512], F32, oG + 16 * KB + 2 * KB * i) for i in range(4)]
        gg_at = [at(f"GG{i}", [128, 4, 128], F32R, oG + 36 * KB + 2 * KB * i) for i in range(2)]
        y_at = [(at(f"YH{i}", [128, 512], F32R, oG + 40 * KB + 2 * KB * i),
                       at(f"YL{i}", [128, 512], F32R, oZ + 16 * KB + 2 * KB * i)) for i in range(2)]
        acc, acc_before = banks[0:4], [list(f) for f in PS.free[0:4]]
        t_zero = pool(lambda e: e.memset(ZERO[:, :], 0.0), t_dense, t_h2p)

        def clear(e):
            for bk in acc:
                last = e.matmul(bk[:, :], ZERO[:, :], H2P[:, 0, 0, 0:512], start=True, stop=False)
            return last
        t_clear = pe(clear, t_zero, t_h2p, acc_before)

        def blocks(base, n_blocks, pe, act, dve, pool, ring, bank_free, WM, primed):
            XGB, STB, SB_, SMB, GGB = (Buffers(p, t_dense) for p in (xg_at, st_at, sb_at, sm_at, gg_at))
            for f in SMB.free:
                f.append(t_gb)
            UB, YB = Buffers(u_at, [t_dense, t_h2p]), Buffers(y_at, [t_dense, t_h2p])
            PE4 = Buffers(banks[4:8])
            PE4.free = [list(f) for f in bank_free]

            def places(b):
                S, bf, fr_s = SB_.take()
                t1 = dve(lambda e: e.tensor_tensor(SBT[:, :, :], iota2[:, 0:64].unsqueeze(1).to_broadcast([128, 4, 64]),
                                                    GB[:, :, b:b + 1].to_broadcast([128, 4, 64]), ALU.is_equal),
                          t_gb, pool.last())
                v = SBT[:, :, :].rearrange("p (a k) n -> p a k n", k=2)
                t_s = pool(lambda e: e.tensor_tensor(S[:, :, :], v[:, :, 0, :], v[:, :, 1, :], ALU.add), t1, bf)
                ST, bf, fr_st = STB.take()
                t1 = pool(lambda e: e.tensor_scalar(STT[:, :, :], GSR[:, :, :], PM[:, b:b + 1], None, ALU.is_equal),
                          t_s)
                t_st = pool(lambda e: e.tensor_tensor(ST[:, :], STT[:, 0, :], STT[:, 1, :], ALU.add), t1, bf)
                return S, t_s, fr_s, ST, t_st, fr_st

            def gather(S, t_s, fr_s):
                xg, bf, fr = XGB.take()
                bank, before, free = PE4.take()

                def mm(e):
                    for k in range(8):
                        for a in range(2):
                            for q in range(3):
                                last = e.matmul(bank[:, 64 * k:64 * k + 64], H2P[:, q, a, 128 * k:128 * k + 128],
                                                S[:, a, :], start=(a == 0 and q == 0), stop=(a == 1 and q == 2))
                    return last
                tp = pe(mm, t_s, t_h2p, before)
                fr_s.append(tp)
                v = bank[:, :].rearrange("p (k n) -> p k n", k=8)
                t1 = act(lambda e: e.activation(xg[:, :, 0:64], v, ACT.Copy), tp, bf)
                t2 = dve(lambda e: e.tensor_tensor(xg[:, :, 64:128], v, xg[:, :, 0:64].bitcast(F32), ALU.subtract),
                         t1, tp, bf)
                free.append(t2)
                return xg, [t1, t2], fr

            fills, ready = [], list(primed)

            def look():
                item = ring.load(fills.pop(0))
                ready.extend(part_of(item, u, act, dve, pool, WM) for u in (0, 1))

            def part():
                while fills and len(ready) <= AHEAD:
                    look()
                return ready.pop(0)

            def up_half(xg, toks, mid=None):
                bank, before, free = PE4.take()
                for q in range(4):
                    wh, wl, th, tl, fr = part()

                    def mm(e, q=q, w=wh, lo=0):
                        for j in range(2):
                            k = 2 * q + j
                            last = e.matmul(bank[:, :], xg[:, k, :], w[:, 512 * j:512 * j + 512], start=(k == 0 and not lo),
                                            stop=(k == 7 and lo == 1))
                        return last
                    pe(mm, toks, th, before)
                    tp = pe(lambda e, q=q, w=wl, f=mm: f(e, q, w, 1), tl)
                    fr.append(tp)
                    if q == 1 and mid is not None:
                        mid()
                U, bf, fr_u = UB.take()
                tu = act(lambda e: e.activation(U[:, :], bank[:, :], ACT.Copy), tp, bf)
                free.append(tu)
                return U, tu, fr_u

            def turned(U, tu, fr_u):
                bank, before, free = PE4.take()

                def tr(e):
                    for k in range(4):
                        last = e.transpose(bank[:, 128 * k:128 * k + 128], U[:, 128 * k:128 * k + 128], ident)
                    return last
                tp = pe(tr, tu, before)
                fr_u.append(tp)
                v = bank[:, :].rearrange("p (k n) -> p k n", k=4)
                s_, bf, fr = SMB.take()
                t1 = act(lambda e: e.activation(s_[:, :, :], v[:, :, 0:64], ACT.Copy), tp, bf)
                t2 = dve(lambda e: e.tensor_tensor(s_[:, :, :], v[:, :, 64:128], s_[:, :, :], ALU.add), t1)
                free.append(t2)
                return s_, t2, fr

            def hidden(g, u):
                s1, t1, f1 = g
                s3, t3, f3 = u
                ta = act(lambda e: e.activation(s1[:, :, :], s1[:, :, :], ACT.Silu), t1)
                tm = dve(lambda e: e.tensor_tensor(s1[:, :, :], s1[:, :, :], s3[:, :, :], ALU.mult), ta, t3)
                f3.append(tm)
                gg, bf, fr = GGB.take()
                th = act(lambda e: e.activation(gg[:, :, 0:64], s1[:, :, :], ACT.Copy), tm, bf)
                tl = dve(lambda e: e.tensor_tensor(gg[:, :, 64:128], s1[:, :, :], gg[:, :, 0:64].bitcast(F32), ALU.subtract),
                         th, bf)
                f1.append(tl)
                return gg, [th, tl], fr

            def down_half(b, gg, toks, fr_g, mid=None):
                two_banks = [PE4.take() for _ in range(2)]
                for k in range(4):
                    wh, wl, th, tl, fr = part()

                    def mm(e, k=k, w=wh, lo=0):
                        for j in range(2):
                            last = e.matmul(two_banks[j][0][:, :], gg[:, k, :], w[:, 512 * j:512 * j + 512],
                                            start=(k == 0 and not lo), stop=(k == 3 and lo == 1))
                        return last
                    pe(mm, toks, th, [t[1] for t in two_banks])
                    tp = pe(lambda e, k=k, w=wl, f=mm: f(e, k, w, 1), tl)
                    fr.append(tp)
                    if k == 1 and mid is not None:
                        mid()
                fr_g.append(tp)
                out = []
                for bk, _, free in two_banks:
                    (yh, yl), bf, fr = YB.take()
                    t1 = act(lambda e, yh=yh, bk=bk: e.activation(yh[:, :], bk[:, :], ACT.Copy, scale=WS_[:, b:b + 1]), tp, bf)
                    t2 = dve(lambda e, yh=yh, yl=yl, bk=bk: e.scalar_tensor_tensor(
                        yl[:, :], bk[:, :], WS_[:, b:b + 1], yh[:, :].bitcast(F32), ALU.mult, ALU.subtract), t1, bf)
                    free.append(t2)
                    out.append((yh, yl, t2, fr))
                return out

            def give_back(ys, ST, t_st, fr_st):
                for j, (yh, yl, ty, fr) in enumerate(ys):
                    def mm(e, j=j, yh=yh, yl=yl):
                        for k in range(4):
                            bk = acc[2 * j + k // 2][:, 256 * (k % 2):256 * (k % 2) + 256]
                            for y in (yh, yl):
                                last = e.matmul(bk, y[:, 128 * k:128 * k + 128], ST[:, :], start=False, stop=False)
                        return last
                    tp = pe(mm, ty, t_st, t_clear)
                    fr.append(tp)
                fr_st.append(tp)

            n_b = n_blocks
            all_fills = [expert_loads(j, base > 0) for j in range(n_b)]
            for i in range(n_b + 1):
                if i < n_b:
                    fills += all_fills[i][0:4]
                if i:
                    fills += all_fills[i - 1][4:6]
            del fills[0:len(ready) // 2]
            while len(ready) <= AHEAD:
                look()
            pls, xgs, hid, ys = {0: places(base)}, {}, {}, {}
            xgs[0] = gather(*pls[0][0:3])

            def back(j):
                if j >= 0:
                    give_back(ys.pop(j), *pls.pop(j)[3:])

            for i in range(n_b + 1):
                if i < n_b:
                    xg, toks, fr_x = xgs.pop(i)
                    if i == 1 and base == 0:
                        extra_experts()
                    if i + 1 < n_b:
                        pls[i + 1] = places(base + i + 1)
                    g1 = up_half(xg, toks)
                    u1 = up_half(xg, toks, lambda: back(i - 2))
                    fr_x.append(pe.last())
                    if i + 1 < n_b:
                        xgs[i + 1] = gather(*pls[i + 1][0:3])
                    t1 = turned(*g1)
                else:
                    back(i - 2)

                def mid():
                    if i < n_b:
                        hid[i] = hidden(t1, turned(*u1))
                if i:
                    ys[i - 1] = down_half(base + i - 1, *hid.pop(i - 1), mid)
                else:
                    mid()
            back(n_b - 1)

        blocks(0, N_EXP, pe, act, dve, pool, ring, PS.free[4:8], WM, primed)
        done = fence()
        subs = [Engine(nc.alloc_semaphore(f"s_x{n}")) for n in ("pe", "act", "dve", "pool", "sp")]
        xsems = [nc.alloc_semaphore(f"s_xr{i}") for i in range(8)]
        xcounts = [0] * 8
        s_join = nc.alloc_semaphore("s_join")
        blocks(N_EXP, N_EXTRA, *subs[:4], Ring(subs[4], ring_slots, xsems, xcounts, [[] for _ in range(8)]), [[]] * 4,
               Buffers(wm_at), [])

        def maybe(sub, ends):
            def f(e):
                more = e.value_load(INTS[0:1, 14:15], min_val=0, max_val=N_EXTRA)
                with e.If(more > 0):
                    sub.emit(e)
                    for s_, n_ in ends:
                        e.wait_ge(s_, n_)
                    e.sem_inc(s_join, 1)
                with e.Else():
                    e.sem_inc(s_join, 1)
            return f
        for eng, sub in zip((pe, act, dve, pool, sp), subs):
            eng.raw(maybe(sub, [sub.last()] if sub.n else list(zip(xsems, xcounts))), ints, done)
        joined = (s_join, 5)

        def close(e):
            for bk in acc:
                last = e.matmul(bk[:, :], ZERO[:, :], H2P[:, 0, 0, 0:512], start=False, stop=True)
            return last
        pe(close, joined)
        done = fence() + [joined]
        PS.free = [list(done) for _ in range(8)]
        t_xf = []
        for k in range(KT):
            t1 = dve(lambda e, k=k: e.scalar_tensor_tensor(
                XT[:, k, 0:256], acc[k // 2][:, 256 * (k % 2):256 * (k % 2) + 256], MOD[:, 2, 40 + k, V2:V2 + 1],
                XT[:, k, 0:256], ALU.mult, ALU.add), done)
            t_xf.append(t1)
        for f in PS.free:
            f.append(t1)
        TB = Buffers(tmp[:7], done)
        OUT = at("OUT", [128, 2, 1024], F32, oR + 24 * KB)
        bank_s, before, free_s = PS.take()
        for k in range(KT):
            sq, bf, fr = TB.take()
            ts = act(lambda e, k=k, sq=sq: e.activation(sq[:, 0:N], XT[:, k, 0:N], ACT.Square), t_xf[k], bf)
            tp = pe(lambda e, k=k, sq=sq: e.matmul(bank_s[:, 0:N], ONES[:, :], sq[:, 0:N],
                                                   start=(k == 0), stop=(k == KT - 1)), ts, before)
            fr.append(tp)
        rb = tmp[7]
        tr_ = rstd(bank_s[:, 0:N], 1.0 / D, rb[:, 0:N], tp, done)
        free_s.append(tr_)
        banks_o = [PS.take() for _ in range(4)]
        t_o = []
        for k in range(KT):
            t_, bf, fr = TB.take()
            t1 = dve(lambda e, k=k, t_=t_: e.scalar_tensor_tensor(t_[:, 0:N], XT[:, k, 0:N], VEC[:, V_NF + k:V_NF + k + 1],
                                                                  rb[:, 0:N], ALU.mult, ALU.mult), tr_, bf)

            def tr(e, k=k, t_=t_):
                for a in range(2):
                    last = e.transpose(banks_o[2 * a + k // 4][0][:, 128 * (k % 4):128 * (k % 4) + 128],
                                       t_[:, 128 * a:128 * a + 128], ident)
                return last
            tp = pe(tr, t1, [banks_o[j][1] for j in range(4)])
            fr.append(tp)
            if k % 4 == 3:
                hf = k // 4
                for a in range(2):
                    bk = banks_o[2 * a + hf][0]
                    t_o.append((dve if a else act)(
                        (lambda e, a=a, bk=bk, hf=hf: e.tensor_copy(OUT[:, a, 512 * hf:512 * hf + 512], bk[:, :])) if a else
                        (lambda e, a=a, bk=bk, hf=hf: e.activation(OUT[:, a, 512 * hf:512 * hf + 512], bk[:, :], ACT.Copy)),
                        tp, done))
        s_out = nc.alloc_semaphore("s_out")
        sp.raw(lambda e: e.dma_start(A["out"][0].rearrange("(a p) d -> p a d", p=128), OUT[:, :, :]).then_inc(s_out, 16),
               t_o)
        sp.raw(lambda e: None, (s_out, 16), (s_wr, 64), r_two, (s_res, 16))

    r = layer(0, t_x, rdy_wp, sums0, [], [])
    r = layer(1, [[t] for t in r[0]], *r[1:])
    second([[t] for t in r[0]], r[2], r[3])
    sp.raw(lambda e: None, [(sems[k], counts[k]) for k in range(N_SLOTS) if counts[k]], (s_wp, 256), (s_vec, n_vec[0]))
    finish(nc, pe, act, dve, pool, sp)


def finish(nc, pe, act, dve, pool, sp):
    with nc.Block() as block:
        @block.tensor
        def _(e):
            pe.emit(e)

        @block.scalar
        def _(e):
            act.emit(e)

        @block.vector
        def _(e):
            dve.emit(e)

        @block.gpsimd
        def _(e):
            pool.emit(e)

        @block.sync
        def _(e):
            sp.emit(e)


_INS = ("x", "c", "ctx", "c_ctx", "w_ada", "b_ada", "g_mix", "g_ffn", "w_in", "q_gain", "k_gain", "w_pool",
        "pool_scale", "w_four", "w_out", "w_gate_up", "w_down", "c_2", "positions_2", "w_ada_2", "b_ada_2",
        "norm1_g_2", "w_in_2", "b_gate_2", "conv_w_2", "conv_b_2", "attn_out_g_2", "mlstm_out_g_2", "w_out_2",
        "norm2_g_2", "w_rg_2", "b_rg_2", "w_re_2", "b_re_2", "w1_2", "w3_2", "w2_2", "norm_f_g_2")
_OUTS = [((1, 256, 1024), "float32")]


def kernel(**inputs):
    import numpy as _np
    import concourse.bacc as _bacc
    from concourse import mybir as _mybir
    from concourse.bass_utils import run_bass_kernel_spmd as _run

    nc = _bacc.Bacc("TRN2", target_bir_lowering=False, num_devices=1)
    arrays, args = {}, {}
    for name, a in [(n, inputs[n]) for n in _INS] + sorted(constants().items()):
        a = _np.ascontiguousarray(a)
        arrays[f"in_{name}_dram"] = a
        args[name] = nc.dram_tensor(f"in_{name}_dram", a.shape, _mybir.dt.from_np(a.dtype), kind="ExternalInput").ap()
    shape, dtype = _OUTS[0]
    args["out"] = nc.dram_tensor("out_0_dram", shape, _mybir.dt.from_np(_np.dtype(dtype)), kind="ExternalOutput").ap()
    block_program(nc, args)
    r = _run(nc, [arrays], core_ids=[0])
    return r.results[0]["out_0_dram"]
```
